# Optimizing a Trainium2 kernel written in Bass

```python
import math
import jax
import jax.numpy as jnp
from jax import lax
import numpy as np

D_MODEL = 1024
BATCH = 1
SEQ = 2048
DEPTH = 1
DEC_BATCH = 8
DEC_SEQ = 1
PAST_LEN = 8192
PAGE_SIZE = 128

HEAD_DIM = 128
MIX_WIDTH = D_MODEL
GDN_HEADS = (MIX_WIDTH // 2) // HEAD_DIM
GDN_DK = HEAD_DIM
GDN_DV = HEAD_DIM
GDN_CONV = 4
GDN_CHUNK = 64
GDN_QK = GDN_HEADS * GDN_DK
GDN_V = GDN_HEADS * GDN_DV
GDN_CONV_CH = 2 * GDN_QK + GDN_V
DSA_HEADS = (MIX_WIDTH - GDN_V) // HEAD_DIM
DSA_KV_HEADS = 2
DSA_GROUP = DSA_HEADS // DSA_KV_HEADS
DSA_Q = DSA_HEADS * HEAD_DIM
DSA_KV = DSA_KV_HEADS * HEAD_DIM
IDX_HEADS = 8
IDX_DIM = 64
INDEX_W_SCALE = (IDX_HEADS * IDX_DIM) ** -0.5
TOPK_MAX = 256
Q_BLOCK = 128
NUM_BUCKETS = 32
MAX_DISTANCE = 128
D_FF = 2816
FFN_CONV = 3
EPS = 1e-6

_SPLIT_SIZES = (GDN_CONV_CH, GDN_V, GDN_HEADS, GDN_HEADS, DSA_Q, DSA_KV, DSA_KV, IDX_HEADS * IDX_DIM, IDX_DIM, IDX_HEADS)
D_IN = sum(_SPLIT_SIZES)
SPLIT_POINTS = tuple(int(p) for p in np.cumsum(_SPLIT_SIZES)[:-1])

kernel_name = 'hybrid_gdn_dsa_convffn_step'

def rms_norm(x, gain):
    xf = x.astype(jnp.float32)
    y = xf * lax.rsqrt(jnp.mean(xf * xf, axis=-1, keepdims=True) + EPS)
    return (y * gain.astype(jnp.float32)).astype(x.dtype)

def l2_normalize(x):
    xf = x.astype(jnp.float32)
    return xf * lax.rsqrt(jnp.sum(xf * xf, axis=-1, keepdims=True) + EPS)

def causal_dwconv(x, buf, w):
    width = w.shape[0]
    t = x.shape[1]
    xx = jnp.concatenate([buf.astype(x.dtype), x], axis=1)
    y = xx[:, 0:t, :] * w[0]
    for j in range(1, width):
        y = y + xx[:, j:j + t, :] * w[j]
    return y, xx[:, xx.shape[1] - (width - 1):, :]

def t5_bucket(rel):
    n = jnp.maximum(rel, 0)
    max_exact = NUM_BUCKETS // 2
    nf = jnp.maximum(n, 1).astype(jnp.float32)
    large = max_exact + (jnp.log(nf / max_exact) / math.log(MAX_DISTANCE / max_exact)
                         * (NUM_BUCKETS - max_exact)).astype(jnp.int32)
    large = jnp.minimum(large, NUM_BUCKETS - 1)
    return jnp.where(n < max_exact, n, large)

def gated_delta_chunked(q, k, v, g, beta, s0):
    bsz, t, nh, dk = q.shape
    dv = v.shape[-1]
    c = GDN_CHUNK
    pad = (-t) % c
    tp = t + pad
    n = tp // c

    def chunks(a):
        a = jnp.pad(a, [(0, 0), (0, pad)] + [(0, 0)] * (a.ndim - 2))
        a = a.reshape((bsz, n, c) + a.shape[2:])
        return jnp.moveaxis(a, 3, 1)

    q, k, v, g, beta = (chunks(a) for a in (q, k, v, g, beta))
    gc = jnp.cumsum(g, axis=-1)
    lower = jnp.tril(jnp.ones((c, c), dtype=bool))
    strict = jnp.tril(jnp.ones((c, c), dtype=bool), -1)
    diff = gc[..., :, None] - gc[..., None, :]
    decay = jnp.where(lower, jnp.exp(jnp.where(lower, diff, 0.0)), 0.0)
    kb = k * beta[..., None]
    a_mat = jnp.where(strict, jnp.einsum('bhnid,bhnjd->bhnij', kb, k) * decay, 0.0)
    eye = jnp.eye(c, dtype=q.dtype)
    rhs = jnp.concatenate([v * beta[..., None], kb * jnp.exp(gc)[..., None]], axis=-1)
    sol = lax.linalg.triangular_solve(a_mat + eye, rhs, left_side=True, lower=True, unit_diagonal=True)
    u, w = sol[..., :dv], sol[..., dv:]
    qk = jnp.einsum('bhnid,bhnjd->bhnij', q, k) * decay
    q_dec = q * jnp.exp(gc)[..., None]
    k_dec = k * jnp.exp(gc[..., -1:] - gc)[..., None]
    g_last = jnp.exp(gc[..., -1])

    def step(s, xs):
        q_c, k_c, u_c, w_c, qk_c, gl_c = xs
        v_new = u_c - jnp.einsum('bhck,bhkv->bhcv', w_c, s)
        o = jnp.einsum('bhck,bhkv->bhcv', q_c, s) + jnp.einsum('bhij,bhjv->bhiv', qk_c, v_new)
        s = s * gl_c[..., None, None] + jnp.einsum('bhck,bhcv->bhkv', k_c, v_new)
        return s, o

    xs = tuple(jnp.moveaxis(a, 2, 0) for a in (q_dec, k_dec, u, w, qk, g_last))
    s, o = lax.scan(step, s0, xs)
    o = jnp.transpose(o, (1, 0, 3, 2, 4)).reshape(bsz, tp, nh, dv)[:, :t]
    return o, s

def gdn_branch(qkv, z, a, b, conv_buf, s0, conv_w, a_log, dt_bias, out_gain):
    bsz, t, _ = qkv.shape
    c, new_buf = causal_dwconv(qkv, conv_buf, conv_w)
    c = jax.nn.silu(c)
    q, k, v = jnp.split(c, [GDN_QK, 2 * GDN_QK], axis=-1)
    q = l2_normalize(q.reshape(bsz, t, GDN_HEADS, GDN_DK)) * (GDN_DK ** -0.5)
    k = l2_normalize(k.reshape(bsz, t, GDN_HEADS, GDN_DK))
    v = v.reshape(bsz, t, GDN_HEADS, GDN_DV).astype(jnp.float32)
    g = -jnp.exp(a_log.astype(jnp.float32)) * jax.nn.softplus(a.astype(jnp.float32) + dt_bias.astype(jnp.float32))
    beta = jax.nn.sigmoid(b.astype(jnp.float32))
    o, s = gated_delta_chunked(q, k, v, g, beta, s0.astype(jnp.float32))
    o = rms_norm(o, out_gain) * jax.nn.silu(z.reshape(bsz, t, GDN_HEADS, GDN_DV).astype(jnp.float32))
    return o.reshape(bsz, t, GDN_V).astype(qkv.dtype), new_buf, s.astype(qkv.dtype)

def gather_rows(rows, idx):
    return jax.vmap(lambda r, i: r[i])(rows, idx)

def paged_gather(pool, page_table, new_rows, sel):
    past_len = page_table.shape[1] * PAGE_SIZE
    li = jnp.minimum(sel, past_len - 1)
    page = jax.vmap(lambda pt, p: pt[p])(page_table, li // PAGE_SIZE)
    from_pool = pool[page * PAGE_SIZE + li % PAGE_SIZE]
    from_new = gather_rows(new_rows, jnp.clip(sel - past_len, 0, new_rows.shape[1] - 1))
    is_past = (sel < past_len).reshape(sel.shape + (1,) * (new_rows.ndim - 2))
    return jnp.where(is_past, from_pool.astype(new_rows.dtype), from_new)

def dsa_attend(q_pos, q, iq, iw, ik_all, gather_kv, n_sel, rel_bias):
    bsz, tq = q.shape[:2]
    k_pos = jnp.arange(ik_all.shape[1], dtype=jnp.int32)
    rel = jax.nn.relu(jnp.einsum('bthd,bsd->bths', iq, ik_all).astype(jnp.float32))
    score = jnp.einsum('bths,bth->bts', rel, iw.astype(jnp.float32))
    score = jnp.where(k_pos[None, None, :] <= q_pos[None, :, None], score, -jnp.inf)
    _, sel = lax.top_k(score, n_sel)
    k_sel, v_sel = gather_kv(sel)
    qg = q.reshape(bsz, tq, DSA_KV_HEADS, DSA_GROUP, HEAD_DIM)
    logits = jnp.einsum('btkgd,btskd->btkgs', qg, k_sel).astype(jnp.float32) * (HEAD_DIM ** -0.5)
    bias = rel_bias[t5_bucket(q_pos[None, :, None] - sel)]
    bias = bias.reshape(bsz, tq, n_sel, DSA_KV_HEADS, DSA_GROUP).transpose(0, 1, 3, 4, 2)
    logits = logits + bias.astype(jnp.float32)
    valid = (sel <= q_pos[None, :, None])[:, :, None, None, :]
    p = jax.nn.softmax(jnp.where(valid, logits, -jnp.inf), axis=-1)
    o = jnp.einsum('btkgs,btskd->btkgd', p.astype(v_sel.dtype), v_sel)
    return o.reshape(bsz, tq, DSA_Q)

def over_query_blocks(fn, q_pos, *arrs):
    bsz, t = arrs[0].shape[:2]
    if t <= Q_BLOCK or t % Q_BLOCK:
        return fn(q_pos, *arrs)
    nb = t // Q_BLOCK

    def split(a):
        return jnp.moveaxis(a.reshape((a.shape[0], nb, Q_BLOCK) + a.shape[2:]), 1, 0)

    out = lax.map(lambda xs: fn(*xs), (q_pos.reshape(nb, Q_BLOCK),) + tuple(split(a) for a in arrs))
    return jnp.moveaxis(out, 0, 1).reshape((bsz, t) + out.shape[3:])

def setup_inputs(seed: int = 0) -> dict:
    key = jax.random.key(seed)
    ks = jax.random.split(key, 24)
    f32 = jnp.float32
    n_pages = PAST_LEN // PAGE_SIZE
    n_used = DEC_BATCH * n_pages
    n_pool = (n_used * 5) // 4

    def nrm(k, shape, scale=1.0):
        return jax.random.normal(k, shape, f32) * scale

    def gain(k, shape):
        return 1.0 + 0.02 * jax.random.normal(k, shape, f32)

    dt = jnp.exp(jax.random.uniform(ks[14], (DEPTH, GDN_HEADS), f32, math.log(1e-3), math.log(1e-1)))
    return {
        'x_prompt': nrm(ks[0], (BATCH, SEQ, D_MODEL)),
        'x_sample': nrm(ks[1], (DEC_BATCH, DEC_SEQ, D_MODEL)),
        'cache_k': nrm(ks[2], (DEPTH, n_pool, PAGE_SIZE, DSA_KV_HEADS, HEAD_DIM)),
        'cache_v': nrm(ks[3], (DEPTH, n_pool, PAGE_SIZE, DSA_KV_HEADS, HEAD_DIM)),
        'cache_idx_k': nrm(ks[4], (DEPTH, n_pool, PAGE_SIZE, IDX_DIM)),
        'state_gdn': nrm(ks[5], (DEPTH, DEC_BATCH, GDN_HEADS, GDN_DK, GDN_DV), 0.1),
        'state_gdn_conv': nrm(ks[6], (DEPTH, DEC_BATCH, GDN_CONV - 1, GDN_CONV_CH)),
        'state_ffn_conv': nrm(ks[7], (DEPTH, DEC_BATCH, FFN_CONV - 1, 2 * D_FF)),
        'page_table': jax.random.permutation(ks[8], n_pool)[:n_used].reshape(DEC_BATCH, n_pages).astype(jnp.int32),
        'rel_bias': nrm(ks[9], (NUM_BUCKETS, DSA_HEADS), 0.5),
        'norm_mix': gain(ks[10], (DEPTH, D_MODEL)),
        'w_in': nrm(ks[11], (DEPTH, D_MODEL, D_IN), D_MODEL ** -0.5),
        'gdn_conv_w': nrm(ks[12], (DEPTH, GDN_CONV, GDN_CONV_CH), GDN_CONV ** -0.5),
        'gdn_a_log': jnp.log(jax.random.uniform(ks[13], (DEPTH, GDN_HEADS), f32, 1.0, 16.0)),
        'gdn_dt_bias': dt + jnp.log(-jnp.expm1(-dt)),
        'gdn_out_norm': gain(ks[15], (DEPTH, GDN_DV)),
        'q_norm': gain(ks[16], (DEPTH, HEAD_DIM)),
        'k_norm': gain(ks[17], (DEPTH, HEAD_DIM)),
        'w_out': nrm(ks[18], (DEPTH, MIX_WIDTH, D_MODEL), MIX_WIDTH ** -0.5),
        'norm_ffn': gain(ks[19], (DEPTH, D_MODEL)),
        'w_up': nrm(ks[20], (DEPTH, D_MODEL, 2 * D_FF), D_MODEL ** -0.5),
        'ffn_conv_w': nrm(ks[21], (DEPTH, FFN_CONV, 2 * D_FF), FFN_CONV ** -0.5),
        'ffn_conv_b': nrm(ks[22], (DEPTH, 2 * D_FF), 0.02),
        'w_down': nrm(ks[23], (DEPTH, D_FF, D_MODEL), D_FF ** -0.5),
    }

def reference(x_prompt, x_sample, cache_k, cache_v, cache_idx_k, state_gdn, state_gdn_conv, state_ffn_conv,
              page_table, rel_bias, norm_mix, w_in, gdn_conv_w, gdn_a_log, gdn_dt_bias, gdn_out_norm,
              q_norm, k_norm, w_out, norm_ffn, w_up, ffn_conv_w, ffn_conv_b, w_down):

    def layer(l, x, gdn_buf, gdn_s, ffn_buf, dsa_fn):
        bsz, t, _ = x.shape
        h = rms_norm(x, norm_mix[l])
        proj = jnp.einsum('btd,de->bte', h, w_in[l])
        qkv, z, a, b, dq, dk, dv, iq, ik, iw = jnp.split(proj, SPLIT_POINTS, axis=-1)
        o_gdn, gdn_buf, gdn_s = gdn_branch(qkv, z, a, b, gdn_buf, gdn_s, gdn_conv_w[l], gdn_a_log[l],
                                           gdn_dt_bias[l], gdn_out_norm[l])
        q = rms_norm(dq.reshape(bsz, t, DSA_HEADS, HEAD_DIM), q_norm[l])
        k = rms_norm(dk.reshape(bsz, t, DSA_KV_HEADS, HEAD_DIM), k_norm[l])
        v = dv.reshape(bsz, t, DSA_KV_HEADS, HEAD_DIM)
        iq = iq.reshape(bsz, t, IDX_HEADS, IDX_DIM)
        iw = iw * INDEX_W_SCALE
        o_dsa = dsa_fn(l, q, k, v, iq, ik, iw)
        mixed = jnp.concatenate([o_gdn, o_dsa.astype(o_gdn.dtype)], axis=-1)
        x = x + jnp.einsum('bte,ed->btd', mixed, w_out[l])
        h = rms_norm(x, norm_ffn[l])
        u, ffn_buf = causal_dwconv(jnp.einsum('btd,df->btf', h, w_up[l]), ffn_buf, ffn_conv_w[l])
        gate, up = jnp.split(u + ffn_conv_b[l], 2, axis=-1)
        x = x + jnp.einsum('btf,fd->btd', jax.nn.silu(gate) * up, w_down[l])
        return x, (k, v, ik, gdn_s, gdn_buf, ffn_buf)

    def run_group(x, gdn_bufs, gdn_states, ffn_bufs, dsa_fn):
        outs = []
        for l in range(DEPTH):
            x, new = layer(l, x, gdn_bufs[l], gdn_states[l], ffn_bufs[l], dsa_fn)
            outs.append(new)
        return x, [jnp.stack(col) for col in zip(*outs)]

    def dsa_prompt(l, q, k, v, iq, ik, iw):
        t = q.shape[1]
        n_sel = min(TOPK_MAX, t // 4)
        pos = jnp.arange(t, dtype=jnp.int32)
        gather = lambda sel: (gather_rows(k, sel), gather_rows(v, sel))
        fn = lambda qp, qb, iqb, iwb: dsa_attend(qp, qb, iqb, iwb, ik, gather, n_sel, rel_bias)
        return over_query_blocks(fn, pos, q, iq, iw)

    def dsa_sample(l, q, k, v, iq, ik, iw):
        db, t = q.shape[:2]
        past_len = page_table.shape[1] * PAGE_SIZE
        n_sel = min(TOPK_MAX, (past_len + t) // 4)
        pos = past_len + jnp.arange(t, dtype=jnp.int32)
        ik_past = cache_idx_k[l][page_table].reshape(db, past_len, IDX_DIM)
        ik_all = jnp.concatenate([ik_past.astype(ik.dtype), ik], axis=1)
        pool_k = cache_k[l].reshape(-1, DSA_KV_HEADS, HEAD_DIM)
        pool_v = cache_v[l].reshape(-1, DSA_KV_HEADS, HEAD_DIM)
        gather = lambda sel: (paged_gather(pool_k, page_table, k, sel), paged_gather(pool_v, page_table, v, sel))
        fn = lambda qp, qb, iqb, iwb: dsa_attend(qp, qb, iqb, iwb, ik_all, gather, n_sel, rel_bias)
        return over_query_blocks(fn, pos, q, iq, iw)

    bp = x_prompt.shape[0]
    zg = jnp.zeros((bp, GDN_CONV - 1, GDN_CONV_CH), x_prompt.dtype)
    zs = jnp.zeros((bp, GDN_HEADS, GDN_DK, GDN_DV), x_prompt.dtype)
    zf = jnp.zeros((bp, FFN_CONV - 1, 2 * D_FF), x_prompt.dtype)
    y_prompt, (p_k, p_v, p_idx_k, p_gdn, p_gdn_conv, p_ffn_conv) = run_group(
        x_prompt, [zg] * DEPTH, [zs] * DEPTH, [zf] * DEPTH, dsa_prompt)
    y_sample, (s_k, s_v, s_idx_k, s_gdn, s_gdn_conv, s_ffn_conv) = run_group(
        x_sample, state_gdn_conv, state_gdn, state_ffn_conv, dsa_sample)
    return (y_prompt, y_sample, p_k, p_v, p_idx_k, p_gdn, p_gdn_conv, p_ffn_conv,
            s_k, s_v, s_idx_k, s_gdn, s_gdn_conv, s_ffn_conv)


_drawn_inputs = setup_inputs


def setup_inputs(seed=0):
    import zlib

    import numpy as np

    out = dict(_drawn_inputs(seed))
    spreads = {}
    factors = {'gdn_out_norm': 6.801,
     'q_norm': 8.0,
     'k_norm': 2.88,
     'norm_ffn': 2.784,
     'ffn_conv_b': 4.188,
     'rel_bias': 2.837}
    for name, (base, spread) in spreads.items():
        noise = np.random.default_rng([zlib.crc32(name.encode()), seed]).standard_normal(out[name].shape)
        drawn = base * np.exp(spread * noise) if base else spread * noise
        out[name] = jnp.asarray(drawn.astype(out[name].dtype))
    for name, factor in factors.items():
        out[name] = (out[name] * factor).astype(out[name].dtype)
    return out
```

```python
from contextlib import ExitStack, contextmanager
import math

import numpy as np

import concourse.bass as bass
from concourse import mybir

F32 = mybir.dt.float32
BF16 = mybir.dt.bfloat16
I32 = mybir.dt.int32
U32 = mybir.dt.uint32
ALU = mybir.AluOpType
ACT = mybir.ActivationFunctionType
AX = mybir.AxisListType
ds = bass.ds

P = 128
SEQ, DEC, D = 2048, 8, 1024
KD = D // P
NT = SEQ // P
TILES = NT + 1
COLS = TILES * P
TOK = SEQ + DEC
HD = 128
GH = 4
QH, KVH = 4, 2
GROUP = QH // KVH
IH, ID = 8, 64
CONV_CH = 3 * GH * HD
C_Z = CONV_CH
C_AB = C_Z + GH * HD
C_Q = C_AB + 2 * GH
C_K = C_Q + QH * HD
C_V = C_K + KVH * HD
C_IQ = C_V + KVH * HD
C_IK = C_IQ + IH * ID
C_IW = C_IK + ID
D_IN = C_IW + IH
SMALL = 2 * GH + ID + IH
GROUPS = SEQ // 512
FF = 2816
NF = FF // P
CONVW = CONV_CH // P
NSEL = 256
PAST, PAGE = 8192, 128
NPAGE = PAST // PAGE
KCOL = NPAGE + 1
NPOOL = DEC * NPAGE * 5 // 4
EPS = 1e-6
BIG = 3.4028234663852886e38
NEG = -1.0e30
INDEX_SCALE = (IH * ID) ** -0.5
SCALE = HD ** -0.5
BUCKETS = 32


def bucket_starts():
    n = np.arange(1, 256)
    half = BUCKETS // 2
    large = half + (np.log(np.maximum(n, 1).astype(np.float32) / np.float32(half)) / np.float32(math.log(128 / half))
                    * np.float32(BUCKETS - half)).astype(np.int32)
    bucket = np.where(n < half, n, np.minimum(large, BUCKETS - 1))
    return [0] + [int(n[np.argmax(bucket >= b)]) for b in range(1, BUCKETS)]


class Steps:

    def __init__(self, eng, sem):
        self.eng, self.sem, self.n, self.base, self.per = eng, sem, 0, 0, None
        self.total = 0

    def link(self, ins):
        self.n += 1
        ins.then_inc(self.sem, 1)
        self.eng.wait_ge(self.sem, 4 + self.base + self.n)

    def enter(self, i, per, count):
        self.start = self.total + self.n
        self.base, self.n, self.per, self.count = self.start + i * per, 0, per, count

    def leave(self):
        assert self.n == self.per, f"{self.n} steps in a turn, not {self.per}"
        self.total = self.base = self.start + self.per * self.count
        self.total, self.n = self.start + self.per * self.count, 0
        self.base = self.total


class Ctx:

    def __init__(self, nc, stack, name):
        self.nc, self.stack, self.name, self.all = nc, stack, name, []
        self.own = []

    def sb(self, name, shape, dt=F32):
        return self.stack.enter_context(self.nc.sbuf_tensor(f"{self.name}_{name}", shape, dt))

    def ps(self, name, shape, dt=F32):
        return self.stack.enter_context(self.nc.psum_tensor(f"{self.name}_p_{name}", shape, dt))

    def sem(self, name):
        s = self.stack.enter_context(self.nc.semaphore(f"{self.name}_{name}"))
        self.all.append(s)
        return s

    def own_sems(self, name, n=2):
        self.own += [self.stack.enter_context(self.nc.semaphore(f"{self.name}_{name}{i}")) for i in range(n)]
        return self.own[-n:]

    def sems(self, name, n=2):
        return [self.sem(f"{name}{i}") for i in range(n)]


@contextmanager
def phase(nc, name):
    with ExitStack() as stack:
        yield Ctx(nc, stack, name), stack


def credit(sp, c):
    for s in c.all:
        sp.sem_inc(s, 4)


def open_block(nc, stack, c):
    def clear():
        for s in c.all:
            nc.sync.sem_clear(s)
        for s in c.own:
            nc.gpsimd.sem_clear(s)
    stack.callback(clear)
    return stack.enter_context(nc.Block())


def constants(nc, K, rel_bias):
    with phase(nc, "const") as (c, stack):
        s_base = c.sem("base")
        s_load = c.sem("load")
        s_rel = c.sem("rel")
        s_step = c.sem("step")
        dist = c.sb("dist", [P, 256])
        ge = c.sb("ge", [P, 256])
        diff = c.sb("diff", [P, BUCKETS, QH])
        tmp = c.sb("tmp", [P, QH, 256])
        starts = bucket_starts()
        block = open_block(nc, stack, c)

        @block.gpsimd
        def _(pool):
            pool.memset(K.ident[:, :], 0.0).then_inc(s_base, 1)
            pool.memset(K.ones[:, :], 1.0).then_inc(s_base, 1)
            pool.memset(K.below[:, :], BIG).then_inc(s_base, 1)
            pool.wait_ge(s_base, 4 + 3)
            pool.affine_select(out=K.ident[:, :], in_=K.ident[:, :], compare_op=ALU.not_equal, fill=1.0,
                               base=0, pattern=[[-1, P]], channel_multiplier=1)
            pool.affine_select(out=K.upto[:, :], in_=K.ones[:, :], compare_op=ALU.is_ge, fill=0.0,
                               base=0, pattern=[[1, P]], channel_multiplier=-1)
            pool.affine_select(out=K.before[:, :], in_=K.ones[:, :], compare_op=ALU.is_gt, fill=0.0,
                               base=0, pattern=[[1, P]], channel_multiplier=-1)
            pool.affine_select(out=K.after[:, :], in_=K.ones[:, :], compare_op=ALU.is_gt, fill=0.0,
                               base=0, pattern=[[-1, P]], channel_multiplier=1)
            pool.affine_select(out=K.below[:, :], in_=K.below[:, :], compare_op=ALU.is_ge, fill=-BIG,
                               base=384, pattern=[[-1, 896]], channel_multiplier=1)
            pool.iota(dist[:, :], pattern=[[-1, 256]], base=P, channel_multiplier=1,
                      allow_small_or_imprecise_dtypes=True).then_inc(s_rel, 1)
            pool.drain()

        @block.sync
        def _(sp):
            credit(sp, c)
            sp.dma_start(K.rb[:, :, :], rel_bias.rearrange("(o b) h -> o b h", o=1).broadcast_to([P, BUCKETS, QH]))\
              .then_inc(s_load, 16)
            sp.wait_ge(s_load, 4 + 16)

        @block.vector
        def _(dve):
            step = Steps(dve, s_step)
            dve.wait_ge(s_load, 4 + 16)
            step.link(dve.tensor_tensor(diff[:, 1:, :], K.rb[:, 1:, :], K.rb[:, :-1, :], ALU.subtract))
            step.link(dve.tensor_tensor(diff[:, 0, :], K.rb[:, 0, :], K.rb[:, BUCKETS - 1, :], ALU.subtract))
            dve.wait_ge(s_rel, 4 + 1)
            step.link(dve.tensor_scalar(ge[:, :], dist[:, :], -1.0e9, None, ALU.is_ge))
            for h in range(QH):
                last = dve.tensor_scalar(K.near[:, h, :], ge[:, :], diff[:, 0, h:h + 1], None, ALU.mult)
            step.link(last)
            for b in range(1, BUCKETS):
                step.link(dve.tensor_scalar(ge[:, :], dist[:, :], float(starts[b]), None, ALU.is_ge))
                for h in range(QH):
                    last = dve.scalar_tensor_tensor(out=K.near[:, h, :], in0=ge[:, :], scalar=diff[:, b, h:h + 1],
                                                    in1=K.near[:, h, :], op0=ALU.mult, op1=ALU.add)
                step.link(last)


def project(nc, K, x_prompt, x_sample, norm_mix, w_in):
    with phase(nc, "proj") as (c, stack):
        x = [c.sb(f"x{b}", [P, D]) for b in range(2)]
        junk = c.sb("junk", [P, D])
        stat = [c.sb(f"stat{b}", [P, 4]) for b in range(2)]
        ht = [c.sb(f"ht{b}", [P, KD, P]) for b in range(2)]
        gain = c.sb("gain", [P, KD])
        w_kv = c.sb("w_kv", [P, KD, 2 * KVH * HD])
        w_small = c.sb("w_small", [P, KD, SMALL])
        p_t = [c.ps(f"t{b}", [P, KD, P]) for b in range(2)]
        p_kv = [c.ps(f"kv{b}", [P, 512]) for b in range(2)]
        p_sm = [c.ps(f"sm{b}", [P, 512]) for b in range(2)]
        s_w = c.sem("w")
        s_load = c.sems("load")
        s_sum = c.sems("sum")
        s_mean = c.sems("mean")
        s_root = c.sems("root")
        s_inv = c.sems("inv")
        s_norm = c.sems("norm")
        s_turn = c.sems("turn")
        s_ht = c.sems("ht")
        s_kept = c.sems("kept")
        s_mm = c.sems("mm")
        s_out = c.sems("out")
        rows = w_in.rearrange("(k p) n -> p k n", p=P)
        block = open_block(nc, stack, c)

        def turns(eng, body):
            with eng.Fori(0, NT // 2) as j:
                for b in range(2):
                    body(j, b, j * 256 + b * P, j * 2 + b)
            body(NT // 2, 0, SEQ, NT)

        @block.sync
        def _(sp):
            credit(sp, c)
            sp.dma_start(gain[:, :], norm_mix.rearrange("(k p) -> p k", p=P), allow_slow_non_contiguous=True)\
              .then_inc(s_w, 16)

            def load(j, b, col, t):
                sp.wait_ge(s_turn[b], 4 + j)
                if t is NT or isinstance(t, int):
                    sp.dma_start(x[b][0:DEC, :], x_sample).then_inc(s_load[b], 16)
                else:
                    sp.dma_start(x[b][:, :], x_prompt[ds(col, P), :]).then_inc(s_load[b], 16)
            turns(sp, load)

        @block.gpsimd
        def _(pool):
            def keep(j, b, col, t):
                pool.wait_ge(s_ht[b], 4 + j + 1)
                pool.tensor_copy(K.ht[:, :, ds(col, P)], ht[b][:, :, :]).then_inc(s_kept[b], 1)
            turns(pool, keep)

        @block.scalar
        def _(act):
            act.dma_start(w_kv[:, :, :], rows[:, :, C_K:C_IQ]).then_inc(s_w, 16)
            act.dma_start(w_small[:, :, 0:2 * GH], rows[:, :, C_AB:C_Q]).then_inc(s_w, 16)
            act.dma_start(w_small[:, :, 2 * GH:], rows[:, :, C_IK:D_IN]).then_inc(s_w, 16)

            def stats(j, b, col, t):
                act.wait_ge(s_load[b], 4 + j * 16 + 16)
                act.activation(junk[:, :], x[b][:, :], ACT.Square, accum_out=stat[b][:, 0:1]).then_inc(s_sum[b], 1)
                act.wait_ge(s_mean[b], 4 + j + 1)
                act.activation(stat[b][:, 2:3], stat[b][:, 1:2], ACT.Sqrt).then_inc(s_root[b], 1)

            def copy_out(j, b, col, t):
                act.wait_ge(s_mm[b], 4 + j + 1)
                act.activation(K.k[:, t, :] if isinstance(t, int) else K.k[:, ds(t, 1), :], p_kv[b][:, 0:KVH * HD], ACT.Copy)
                act.activation(K.v[:, t, :] if isinstance(t, int) else K.v[:, ds(t, 1), :], p_kv[b][:, KVH * HD:], ACT.Copy)
                act.activation(K.small[:, t, :] if isinstance(t, int) else K.small[:, ds(t, 1), :], p_sm[b][:, 0:SMALL], ACT.Copy)\
                   .then_inc(s_out[b], 1)
            stats(0, 0, 0, 0)
            with act.Fori(0, NT // 2) as j:
                stats(j, 1, 0, 0)
                copy_out(j, 0, 0, j * 2)
                stats(j + 1, 0, 0, 0)
                copy_out(j, 1, 0, j * 2 + 1)
            copy_out(NT // 2, 0, 0, NT)

        @block.vector
        def _(dve):
            dve.wait_ge(s_w, 4 + 64)

            def norm(j, b, col, t):
                dve.wait_ge(s_sum[b], 4 + j + 1)
                dve.tensor_scalar(stat[b][:, 1:2], stat[b][:, 0:1], 1.0 / D, EPS, ALU.mult, ALU.add).then_inc(s_mean[b], 1)
                dve.wait_ge(s_root[b], 4 + j + 1)
                dve.reciprocal(stat[b][:, 3:4], stat[b][:, 2:3]).then_inc(s_inv[b], 1)
                dve.wait_ge(s_inv[b], 4 + j + 1)
                dve.tensor_scalar(x[b][:, :], x[b][:, :], stat[b][:, 3:4], None, ALU.mult).then_inc(s_norm[b], 1)

            def scale(j, b, col, t):
                dve.wait_ge(s_turn[b], 4 + j + 1)
                dve.wait_ge(s_kept[b], 4 + j)
                dve.wait_ge(s_mm[b], 4 + j)
                dve.tensor_tensor(ht[b][:, :, :], p_t[b][:, :, :],
                                  gain[:, :].unsqueeze(2).broadcast_to([P, KD, P]), ALU.mult).then_inc(s_ht[b], 1)
            norm(0, 0, 0, 0)
            with dve.Fori(0, NT // 2) as j:
                norm(j, 1, 0, 0)
                scale(j, 0, 0, 0)
                norm(j + 1, 0, 0, 0)
                scale(j, 1, 0, 0)
            scale(NT // 2, 0, 0, 0)

        @block.tensor
        def _(pe):
            pe.wait_ge(s_w, 4 + 64)

            def turn(j, b):
                pe.wait_ge(s_norm[b], 4 + j + 1)
                pe.wait_ge(s_ht[b], 4 + j)
                for k in range(KD):
                    last = pe.transpose(p_t[b][:, k, :], x[b][:, k * P:(k + 1) * P], K.ident[:, :])
                last.then_inc(s_turn[b], 1)

            def multiply(j, b):
                pe.wait_ge(s_ht[b], 4 + j + 1)
                pe.wait_ge(s_out[b], 4 + j)
                for k in range(KD):
                    pe.matmul(p_kv[b][:, :], ht[b][:, k, :], w_kv[:, k, :], start=(k == 0), stop=(k == KD - 1))
                for k in range(KD):
                    last = pe.matmul(p_sm[b][:, 0:SMALL], ht[b][:, k, :], w_small[:, k, :],
                                     start=(k == 0), stop=(k == KD - 1))
                last.then_inc(s_mm[b], 1)
            turn(0, 0)
            with pe.Fori(0, NT // 2) as j:
                turn(j, 1)
                multiply(j, 0)
                turn(j + 1, 0)
                multiply(j, 1)
            multiply(NT // 2, 0)


def keys(nc, K, k_norm, outs):
    with phase(nc, "keys") as (c, stack):
        sq = c.sb("sq", [P, TILES * KVH, HD])
        stat = c.sb("stat", [P, 4, TILES * KVH])
        gain = c.sb("gain", [P, HD])
        st = [c.sb(f"st{b}", [P, 3, P]) for b in range(2)]
        p_t = [c.ps(f"t{b}", [P, 4, P]) for b in range(2)]
        s_w, s_step, s_mean, s_root, s_normed, s_store = (c.sem(n) for n in
                                                          ("w", "step", "mean", "root", "normed", "store"))
        s_st, s_turn, s_out = c.sems("st"), c.sems("turn"), c.sems("out")
        kk = K.k[:, :, :].rearrange("p t (g d) -> p (t g) d", g=KVH)
        block = open_block(nc, stack, c)

        @block.sync
        def _(sp):
            credit(sp, c)
            sp.dma_start(gain[:, :], k_norm.rearrange("(o d) -> o d", o=1).broadcast_to([P, HD])).then_inc(s_w, 16)
            small = K.small[:, :, 2 * GH:2 * GH + ID]
            sp.dma_start(outs["p_idx"].rearrange("(t p) c -> p t c", p=P), small[:, 0:NT, :]).then_inc(s_store, 16)
            sp.dma_start(outs["s_idx"], K.small[0:DEC, NT, 2 * GH:2 * GH + ID]).then_inc(s_store, 16)
            sp.dma_start(outs["p_v"].rearrange("(t p) c -> p t c", p=P), K.v[:, 0:NT, :]).then_inc(s_store, 16)
            sp.dma_start(outs["s_v"], K.v[0:DEC, NT, :]).then_inc(s_store, 16)
            sp.wait_ge(s_normed, 4 + 1)
            sp.dma_start(outs["p_k"].rearrange("(t p) c -> p t c", p=P), K.k[:, 0:NT, :]).then_inc(s_store, 16)
            sp.dma_start(outs["s_k"], K.k[0:DEC, NT, :]).then_inc(s_store, 16)
            sp.wait_ge(s_store, 4 + 96)

        @block.vector
        def _(dve):
            step = Steps(dve, s_step)
            step.link(dve.tensor_tensor(sq[:, :, :], kk, kk, ALU.mult))
            step.link(dve.tensor_reduce(stat[:, 0, :], sq[:, :, :], AX.X, ALU.add))
            dve.tensor_scalar(stat[:, 1, :], stat[:, 0, :], 1.0 / HD, EPS, ALU.mult, ALU.add).then_inc(s_mean, 1)
            dve.wait_ge(s_root, 4 + 1)
            step.link(dve.reciprocal(stat[:, 3, :], stat[:, 2, :]))
            step.link(dve.tensor_tensor(kk, kk, stat[:, 3, :].unsqueeze(2).broadcast_to([P, TILES * KVH, HD]), ALU.mult))
            dve.wait_ge(s_w, 4 + 16)
            dve.tensor_tensor(kk, kk, gain[:, :].unsqueeze(1).broadcast_to([P, TILES * KVH, HD]), ALU.mult)\
               .then_inc(s_normed, 1)

            dve.wait_ge(s_normed, 4 + 1)
            dve.tensor_copy(K.knew[:, :], K.k[:, NT, :])

            def out(j, b, col):
                dve.wait_ge(s_turn[b], 4 + j + 1)
                dve.tensor_copy(K.kt[:, :, ds(col, P)], p_t[b][:, 0:KVH, :])
                dve.tensor_copy(K.ikt[:, ds(col, P)], p_t[b][:, KVH, :]).then_inc(s_out[b], 1)
            with dve.Fori(0, NT // 2) as j:
                out(j, 0, j * 256)
                out(j, 1, j * 256 + P)
            out(NT // 2, 0, SEQ)

        @block.scalar
        def _(act):
            act.wait_ge(s_mean, 4 + 1)
            act.activation(stat[:, 2, :], stat[:, 1, :], ACT.Sqrt).then_inc(s_root, 1)

        @block.gpsimd
        def _(pool):
            pool.wait_ge(s_normed, 4 + 1)

            def stage(j, b, t):
                pool.wait_ge(s_turn[b], 4 + j)
                pool.tensor_copy(st[b][:, 0:KVH, :], K.k[:, ds(t, 1), :].rearrange("p o (g d) -> p (o g) d", g=KVH))
                for half in range(2):
                    last = pool.tensor_copy(st[b][:, KVH, half * ID:(half + 1) * ID],
                                            K.small[:, ds(t, 1), 2 * GH:2 * GH + ID])
                last.then_inc(s_st[b], 1)
            with pool.Fori(0, NT // 2) as j:
                stage(j, 0, j * 2)
                stage(j, 1, j * 2 + 1)
            stage(NT // 2, 0, NT)

        @block.tensor
        def _(pe):
            def turn(j, b):
                pe.wait_ge(s_st[b], 4 + j + 1)
                pe.wait_ge(s_out[b], 4 + j)
                for g in range(3):
                    last = pe.transpose(p_t[b][:, g, :], st[b][:, g, :], K.ident[:, :])
                last.then_inc(s_turn[b], 1)
            with pe.Fori(0, NT // 2) as j:
                turn(j, 0)
                turn(j, 1)
            turn(NT // 2, 0)


def channels(nc, K, w_in, conv_w, conv_state, q_norm, outs):
    with phase(nc, "chan") as (c, stack):
        w = [c.sb(f"w{b}", [P, KD, P]) for b in range(2)]
        pre = [c.sb(f"pre{b}", [P, 3 + SEQ]) for b in range(2)]
        new = [c.sb(f"new{b}", [P, 3 + DEC]) for b in range(2)]
        acc = [c.sb(f"acc{b}", [P, TOK]) for b in range(2)]
        res = [c.sb(f"res{b}", [P, TOK]) for b in range(2)]
        past = [c.sb(f"past{b}", [P, P]) for b in range(2)]
        taps = c.sb("taps", [P, 4, CONVW])
        rows = c.sb("rows", [3 + DEC, CONV_CH])
        p_g = [c.ps(f"g{g}", [P, 512]) for g in range(GROUPS)]
        p_s = c.ps("s", [P, 512])
        p_past = c.ps("past", [P, P])
        p_rows = c.ps("rows", [3 + DEC, P])
        s_taps, s_zero, s_step, s_state = (c.sem(n) for n in ("taps", "zero", "step", "state"))
        s_w = c.sems("w")
        s_past = c.sems("past")
        s_mm = c.sem("mm")
        s_free = c.sems("free", GROUPS)
        s_used = c.sems("used")
        s_sfree = c.sem("sfree")
        s_pre = c.sems("pre")
        s_acc = c.sems("acc")
        s_res = c.sems("res")
        s_st = c.sems("st")
        s_hist = c.sem("hist")
        s_back = c.sem("back")
        s_rows = c.sem("rows")
        wv = w_in.rearrange("(k p) n -> p k n", p=P)
        parts = [(0, CONVW, K.d_qkv, "conv"), (C_Z, 4, K.d_z, "silu"), (C_Q, 4, K.d_q, "copy"), (C_IQ, 4, K.d_iq, "copy")]
        block = open_block(nc, stack, c)

        def each(eng, body):
            n2 = 0
            for first, n, scratch, kind in parts:
                with eng.Fori(0, n // 2) as j:
                    for b in range(2):
                        body(j + n2, b, j * 256 + first + b * P, scratch, kind, j * 2 + b)
                n2 += n // 2

        @block.sync
        def _(sp):
            credit(sp, c)
            for i in range(4):
                sp.dma_start(taps[:, i, :], conv_w[i, :].rearrange("(m p) -> p m", p=P), allow_slow_non_contiguous=True)\
                  .then_inc(s_taps, 16)

            def load(j, b, col, scratch, kind, m):
                sp.wait_ge(s_used[b], 4 + j)
                sp.dma_start(w[b][:, :, :], wv[:, :, ds(col, P)]).then_inc(s_w[b], 16)
                if kind == "conv":
                    sp.wait_ge(s_hist, 4 + j * 2)
                    sp.dma_start(past[b][0:DEC * 3, :], conv_state[:, ds(col, P)]).then_inc(s_past[b], 16)
            sp.wait_ge(s_zero, 4 + 4)
            each(sp, load)
            sp.wait_ge(s_rows, 4 + CONVW)
            sp.dma_start(outs["p_gconv"], rows[0:3, :]).then_inc(s_state, 16)
            sp.dma_start(outs["s_gconv"][:, 2, :], rows[3:3 + DEC, :]).then_inc(s_state, 16)
            sp.dma_start(outs["s_gconv"][:, 0:2, :], conv_state.rearrange("(b j) n -> b j n", j=3)[:, 1:3, :])\
              .then_inc(s_state, 16)
            sp.wait_ge(s_state, 4 + 48)

        @block.tensor
        def _(pe):
            def multiply(j, b, col, scratch, kind, m):
                chunk = j * 2 + b
                pe.wait_ge(s_w[b], 4 + j * 16 + 16)
                for g in range(GROUPS):
                    pe.wait_ge(s_free[g], 4 + chunk)
                    for k in range(KD):
                        last = pe.matmul(p_g[g][:, :], w[b][:, k, :], K.ht[:, k, g * 512:(g + 1) * 512],
                                         start=(k == 0), stop=(k == KD - 1))
                    last.then_inc(s_mm, 1)
                pe.wait_ge(s_sfree, 4 + chunk)
                for k in range(KD):
                    last = pe.matmul(p_s[:, 0:DEC], w[b][:, k, :], K.ht[:, k, SEQ:SEQ + DEC],
                                     start=(k == 0), stop=(k == KD - 1))
                last.then_inc(s_used[b], 1)
                if kind == "conv":
                    pe.wait_ge(s_past[b], 4 + j * 16 + 16)
                    pe.wait_ge(s_step, 4 + chunk * 7)
                    pe.transpose(p_past[:, :], past[b][:, :], K.ident[:, :]).then_inc(s_hist, 1)
                    pe.wait_ge(s_pre[b], 4 + j + 1)
                    pe.wait_ge(s_rows, 4 + chunk)
                    pe.transpose(p_rows[:, :], new[b][:, :], K.ident[:, :]).then_inc(s_back, 1)
            each(pe, multiply)

        @block.scalar
        def _(act):
            def store(j, b, scratch, m, ready, n):
                act.wait_ge(ready, 4 + n)
                act.dma_start(scratch[ds(m, 1), :, :].rearrange("o p n -> (o p) n"), res[b][:, :])\
                   .then_inc(s_st[b], 16)

            def copies(j, b, col, kind):
                chunk = j * 2 + b
                if kind == "conv":
                    act.wait_ge(s_acc[b], 4 + j)
                else:
                    act.wait_ge(s_st[b], 4 + j * 16)
                dst = pre[b][:, 3:] if kind == "conv" else res[b]
                f = ACT.Silu if kind == "silu" else ACT.Copy
                for g in range(GROUPS):
                    act.wait_ge(s_mm, 4 + chunk * 4 + g + 1)
                    act.activation(dst[:, g * 512:(g + 1) * 512], p_g[g][:, :], f).then_inc(s_free[g], 1)
                act.wait_ge(s_used[b], 4 + j + 1)
                if kind == "conv":
                    act.activation(new[b][:, 3:], p_s[:, 0:DEC], ACT.Copy).then_inc(s_sfree, 1)
                    act.wait_ge(s_free[GROUPS - 1], 4 + chunk + 1)
                    act.activation(new[b][:, 0:3], pre[b][:, SEQ:], ACT.Copy).then_inc(s_pre[b], 1)
                    act.wait_ge(s_back, 4 + chunk + 1)
                    act.activation(rows[:, ds(col, P)], p_rows[:, :], ACT.Copy).then_inc(s_rows, 1)
                else:
                    act.activation(res[b][:, SEQ:], p_s[:, 0:DEC], f).then_inc(s_sfree, 1)

            def silu(j, b):
                act.wait_ge(s_acc[b], 4 + j + 1)
                act.wait_ge(s_st[b], 4 + j * 16)
                act.activation(res[b][:, :], acc[b][:, :], ACT.Silu).then_inc(s_res[b], 1)
            n2 = 0
            for _, n, scratch, kind in parts:
                if kind == "conv":
                    copies(0, 0, 0, kind)
                    with act.Fori(0, n // 2 - 1) as j:
                        copies(j, 1, j * 256 + P, kind)
                        silu(j, 0)
                        store(j, 0, K.d_qkv, j * 2, s_res[0], j + 1)
                        copies(j + 1, 0, j * 256 + 256, kind)
                        silu(j, 1)
                        store(j, 1, K.d_qkv, j * 2 + 1, s_res[1], j + 1)
                    last = n // 2 - 1
                    copies(last, 1, last * 256 + P, kind)
                    silu(last, 0)
                    silu(last, 1)
                    store(last, 1, K.d_qkv, n - 1, s_res[1], last + 1)
                    store(last, 0, K.d_qkv, n - 2, s_res[0], last + 1)
                else:
                    with act.Fori(0, n // 2) as j:
                        for b in range(2):
                            copies(j + n2, b, 0, kind)
                            store(j, b, scratch, j * 2 + b, s_sfree, (j + n2) * 2 + b + 1)
                n2 += n // 2
            for b in range(2):
                act.wait_ge(s_st[b], 4 + n2 * 16)

        @block.vector
        def _(dve):
            for b in range(2):
                dve.memset(pre[b][:, 0:3], 0.0).then_inc(s_zero, 1)
                dve.memset(past[b][:, :], 0.0).then_inc(s_zero, 1)
            dve.wait_ge(s_zero, 4 + 4)
            dve.wait_ge(s_taps, 4 + 64)
            step = Steps(dve, s_step)
            with dve.Fori(0, CONVW // 2) as j:
                step.enter(j, 14, CONVW // 2)
                for b in range(2):
                    chunk = j * 2 + b
                    tap = [taps[:, i, ds(chunk, 1)] for i in range(4)]
                    dve.wait_ge(s_pre[b], 4 + j + 1)
                    dve.wait_ge(s_res[b], 4 + j)
                    a = acc[b][:, 0:SEQ]
                    step.link(dve.tensor_scalar(a, pre[b][:, 0:SEQ], tap[0], None, ALU.mult))
                    for i in range(1, 4):
                        step.link(dve.scalar_tensor_tensor(out=a, in0=pre[b][:, i:SEQ + i], scalar=tap[i], in1=a,
                                                           op0=ALU.mult, op1=ALU.add))
                    old = p_past[:, 0:DEC * 3].rearrange("p (b j) -> p b j", j=3)
                    a = acc[b][:, SEQ:]
                    dve.wait_ge(s_hist, 4 + chunk + 1)
                    step.link(dve.tensor_scalar(a, old[:, :, 0], tap[0], None, ALU.mult))
                    for i in range(1, 3):
                        step.link(dve.scalar_tensor_tensor(out=a, in0=old[:, :, i], scalar=tap[i], in1=a,
                                                           op0=ALU.mult, op1=ALU.add))
                    dve.scalar_tensor_tensor(out=a, in0=new[b][:, 3:], scalar=tap[3], in1=a,
                                             op0=ALU.mult, op1=ALU.add).then_inc(s_acc[b], 1)
                step.leave()


LEVELS = 7


def gates(nc, K, a_log, dt_bias):
    with phase(nc, "gate") as (c, stack):
        x = c.sb("x", [P, TILES, GH])
        pos = c.sb("pos", [P, TILES, GH])
        e = c.sb("e", [P, TILES, GH])
        bias = c.sb("bias", [P, 2, GH])
        rowi, coli = c.sb("rowi", [P, P], I32), c.sb("coli", [P, P], I32)
        both, shifted = c.sb("both", [P, P], I32), c.sb("shifted", [P, P], I32)
        p_cum, p_all = c.ps("cum", [P, TILES * GH]), c.ps("all", [P, TILES * GH])
        s_load, s_step, s_abs, s_exp, s_one, s_ln, s_g, s_cum, s_cum_exp, s_iota, s_sig, s_alog, s_diff = (
            c.sem(n) for n in ("load", "step", "abs", "exp", "one", "ln", "g", "cum", "cum_exp", "iota", "sig", "alog", "diff"))
        a, b = K.small[:, :, 0:GH], K.small[:, :, GH:2 * GH]
        flat = lambda t: t[:, :, :].rearrange("p t h -> p (t h)")
        block = open_block(nc, stack, c)

        @block.sync
        def _(sp):
            credit(sp, c)
            sp.dma_start(bias[:, 0, :], dt_bias.broadcast_to([P, GH])).then_inc(s_load, 16)
            sp.dma_start(bias[:, 1, :], a_log.broadcast_to([P, GH])).then_inc(s_load, 16)

        @block.gpsimd
        def _(pool):
            pool.iota(rowi[:, :], pattern=[[0, P]], base=0, channel_multiplier=1)
            pool.iota(coli[:, :], pattern=[[1, P]], base=0, channel_multiplier=0).then_inc(s_iota, 1)

        @block.vector
        def _(dve):
            step = Steps(dve, s_step)
            dve.wait_ge(s_load, 4 + 32)
            step.link(dve.tensor_tensor(x[:, :, :], a, bias[:, 0, :].unsqueeze(1).broadcast_to([P, TILES, GH]), ALU.add))
            step.link(dve.tensor_scalar(pos[:, :, :], x[:, :, :], 0.0, None, ALU.max))
            dve.scalar_tensor_tensor(out=x[:, :, :], in0=pos[:, :, :], scalar=-2.0, in1=x[:, :, :],
                                     op0=ALU.mult, op1=ALU.add).then_inc(s_abs, 1)
            dve.wait_ge(s_exp, 4 + 1)
            dve.tensor_scalar(e[:, :, :], e[:, :, :], 1.0, None, ALU.add).then_inc(s_one, 1)
            dve.wait_ge(s_ln, 4 + 1)
            step.link(dve.tensor_tensor(x[:, :, :], pos[:, :, :], e[:, :, :], ALU.add))
            dve.wait_ge(s_alog, 4 + 1)
            dve.scalar_tensor_tensor(out=K.g[:, :, :], in0=x[:, :, :], scalar=-1.0,
                                     in1=bias[:, 1, :].unsqueeze(1).broadcast_to([P, TILES, GH]),
                                     op0=ALU.mult, op1=ALU.mult).then_inc(s_g, 1)
            dve.wait_ge(s_sig, 4 + 1)
            step.link(dve.tensor_scalar(K.beta[:, :, :], K.beta[:, :, :], 1.0, None, ALU.add))
            step.link(dve.reciprocal(K.beta[:, :, :], K.beta[:, :, :]))
            dve.wait_ge(s_cum, 4 + 1)
            step.link(dve.tensor_copy(flat(K.decay_sum), p_cum[:, :]))
            step.link(dve.tensor_copy(flat(K.glast), p_all[:, :]))
            dve.tensor_tensor(flat(K.kdec), flat(K.glast), flat(K.decay_sum), ALU.subtract).then_inc(s_diff, 1)
            dve.wait_ge(s_cum_exp, 4 + 3)
            step.link(dve.tensor_tensor(K.bexp[:, :, :], K.bexp[:, :, :], K.beta[:, :, :], ALU.mult))
            dve.wait_ge(s_iota, 4 + 1)
            step.link(dve.tensor_tensor(both[:, :], rowi[:, :], coli[:, :], ALU.bitwise_xor))
            for l in range(LEVELS):
                step.link(dve.tensor_scalar(shifted[:, :], both[:, :], l, None, ALU.logical_shift_right))
                for m, half in ((K.join, K.after), (K.join_t, K.before)):
                    last = dve.scalar_tensor_tensor(out=m[:, l, :], in0=shifted[:, :], scalar=1.0, in1=half[:, :],
                                                    op0=ALU.is_equal, op1=ALU.mult)
                step.link(last)

        @block.scalar
        def _(act):
            act.wait_ge(s_load, 4 + 32)
            act.activation(bias[:, 1, :], bias[:, 1, :], ACT.Exp).then_inc(s_alog, 1)
            act.activation(K.beta[:, :, :], b, ACT.Exp, scale=-1.0).then_inc(s_sig, 1)
            act.wait_ge(s_abs, 4 + 1)
            act.activation(e[:, :, :], x[:, :, :], ACT.Exp).then_inc(s_exp, 1)
            act.wait_ge(s_one, 4 + 1)
            act.activation(e[:, :, :], e[:, :, :], ACT.Ln).then_inc(s_ln, 1)
            act.wait_ge(s_diff, 4 + 1)
            act.activation(flat(K.bexp), flat(K.decay_sum), ACT.Exp).then_inc(s_cum_exp, 1)
            act.activation(flat(K.glast), flat(K.glast), ACT.Exp).then_inc(s_cum_exp, 1)
            act.activation(K.kdec[:, :, :], K.kdec[:, :, :], ACT.Exp).then_inc(s_cum_exp, 1)

        @block.tensor
        def _(pe):
            pe.wait_ge(s_g, 4 + 1)
            pe.matmul(p_cum[:, :], K.upto[:, :], flat(K.g), start=True, stop=True)
            pe.matmul(p_all[:, :], K.ones[:, :], flat(K.g), start=True, stop=True).then_inc(s_cum, 1)


def delta(nc, K, out_gain, outs):
    N = NT
    with phase(nc, "delta") as (c, stack):
        two = lambda name, shape: [c.sb(f"{name}{b}", shape) for b in range(2)]
        HW = [P, GH, P]
        raw = two("raw", [P, 3 * GH, P])
        z = two("z", HW)
        tmp = two("tmp", [P, 2 * GH, P])
        kq = two("kq", [P, GH, 2, P])
        qd = two("qd", HW)
        kw, kd, vb = two("kw", HW), two("kd", HW), two("vb", HW)
        gb = two("gb", HW)
        er = two("er", HW)
        et, el = two("et", HW), two("el", HW)
        am, at = two("am", HW), two("at", HW)
        qk = two("qk", HW)
        x, xt = two("x", HW), two("xt", HW)
        atm = two("atm", HW)
        y = two("y", HW)
        wt, vn = two("wt", HW), two("vn", HW)
        osb, orr = two("osb", HW), two("orr", HW)
        gain = c.sb("gain", [P, 1])
        bank = [[c.ps(f"bank{b}{i}", [P, GH, P]) for i in range(4)] for b in range(2)]
        names = ("gain zero qkv z gb sq ss inv rs norm turn tok row er dif dec eda gram attn sys syst first mask ycopy "
                 "yv prod upd wt wtc vnew vnc o oread kv state osq oss oinv ors ogain res").split()
        S = {n: c.sem(n) for n in names}
        s_ld, s_st, s_step = c.sems("ld"), c.sems("st"), c.sem("step")
        flat = lambda t: t[:, :, :].rearrange("p a b -> p (a b)")
        wide = lambda m: m.unsqueeze(1).broadcast_to(HW)
        block = open_block(nc, stack, c)

        def turns(eng, *bodies):
            with eng.Fori(0, N // 2) as j:
                for body in bodies:
                    for b in range(2):
                        body(j, b, j * 2 + b)

        @block.sync
        def _(sp):
            credit(sp, c)
            sp.dma_start(gain[:, :], out_gain.rearrange("(p o) -> p o", o=1)).then_inc(S["gain"], 16)

            def load(j, b, n):
                sp.wait_ge(S["tok"], 4 + n - 1)
                sp.dma_start(raw[b][:, :, :], K.d_qkv[:, :, ds(n * P, P)].rearrange("m p n -> p m n")).then_inc(s_ld[b], 16)
                sp.wait_ge(S["res"], 4 + n - 1)
                sp.dma_start(z[b][:, :, :], K.d_z[:, :, ds(n * P, P)].rearrange("m p n -> p m n")).then_inc(s_ld[b], 16)

            def store(j, b, n):
                sp.wait_ge(S["res"], 4 + n + 1)
                sp.dma_start(K.d_mix[0:GH, :, ds(n * P, P)].rearrange("m p n -> p m n"), orr[b][:, :, :]).then_inc(s_st[b], 16)
            turns(sp, load, store)
            sp.wait_ge(S["state"], 4 + N)
            sp.dma_start(outs["p_gdn"].rearrange("h k v -> k h v"), K.state[:, :, :]).then_inc(S["gain"], 16)
            sp.wait_ge(S["gain"], 4 + 32)
            for b in range(2):
                sp.wait_ge(s_st[b], 4 + N // 2 * 16)

        @block.tensor
        def _(pe):
            def norms(j, b, n):
                pe.wait_ge(S["sq"], 4 + n + 1)
                pe.wait_ge(S["state"], 4 + n - 1)
                for i in range(2):
                    last = pe.matmul(bank[b][i][:, :, :], K.ones[:, :], tmp[b][:, i * GH:(i + 1) * GH, :],
                                     start=True, stop=True)
                last.then_inc(S["ss"], 1)

            def rows(j, b, n):
                pe.wait_ge(S["gb"], 4 + n + 1)
                pe.wait_ge(S["vnc"], 4 + n - 1)
                for h in range(GH):
                    last = pe.matmul(bank[b][2][:, h, :], gb[b][:, h, :], K.upto[:, :], start=True, stop=True)
                last.then_inc(S["row"], 1)

            def turn(j, b, n):
                pe.wait_ge(S["norm"], 4 + n + 1)
                for h in range(GH):
                    pe.transpose(bank[b][0][:, h, :], kq[b][:, h, 0, :], K.ident[:, :])
                for h in range(GH):
                    last = pe.transpose(bank[b][1][:, h, :], raw[b][:, 2 * GH + h, :], K.ident[:, :])
                last.then_inc(S["turn"], 1)

            def gram(j, b, n):
                pe.wait_ge(S["dif"], 4 + n + 1)
                pe.wait_ge(S["er"], 4 + n + 1)
                pe.wait_ge(S["oinv"], 4 + n - 1)
                for h in range(GH):
                    last = pe.matmul(bank[b][2 + h // 2][:, (h % 2) * 2:(h % 2) * 2 + 2, :], kq[b][:, h, 0, :],
                                     kq[b][:, h, :, :], start=True, stop=True)
                last.then_inc(S["gram"], 1)

            def system(j, b, n):
                pe.wait_ge(S["sys"], 4 + n + 1)
                pe.wait_ge(S["tok"], 4 + n + 1)
                for h in range(GH):
                    last = pe.transpose(bank[b][0][:, h, :], am[b][:, h, :], K.ident[:, :])
                last.then_inc(S["syst"], 1)

            with pe.Fori(0, N // 2) as j:
                for body in (norms, rows, turn, gram, system):
                    for b in range(2):
                        body(j, b, j * 2 + b)
                for l in range(1, LEVELS):
                    for b in range(2):
                        m = j * 2 * (LEVELS - 1) + (l - 1) * 2 + b
                        pe.wait_ge(S["mask"], 4 + m + 1)
                        if l == 1:
                            pe.wait_ge(S["first"], 4 + j * 2 + b + 1)
                        else:
                            pe.wait_ge(S["upd"], 4 + m - 1)
                        for h in range(GH):
                            last = pe.matmul(bank[b][1][:, h, :], atm[b][:, h, :], x[b][:, h, :], start=True, stop=True)
                        last.then_inc(S["yv"], 1)
                    for b in range(2):
                        m = j * 2 * (LEVELS - 1) + (l - 1) * 2 + b
                        pe.wait_ge(S["ycopy"], 4 + m + 1)
                        for h in range(GH):
                            pe.matmul(bank[b][0][:, h, :], xt[b][:, h, :], y[b][:, h, :], start=True, stop=True)
                        for h in range(GH):
                            last = pe.matmul(bank[b][2][:, h, :], y[b][:, h, :], xt[b][:, h, :], start=True, stop=True)
                        last.then_inc(S["prod"], 1)
                for b in range(2):
                    m = j * 2 * (LEVELS - 1) + (LEVELS - 2) * 2 + b
                    pe.wait_ge(S["upd"], 4 + m + 1)
                    for h in range(GH):
                        last = pe.matmul(bank[b][3][:, h, :], kw[b][:, h, :], xt[b][:, h, :], start=True, stop=True)
                    last.then_inc(S["wt"], 1)
                for b in range(2):
                    n = j * 2 + b
                    pe.wait_ge(S["wtc"], 4 + n + 1)
                    pe.wait_ge(S["state"], 4 + n)
                    for h in range(GH):
                        pe.matmul(bank[b][1][:, h, :], xt[b][:, h, :], vb[b][:, h, :], start=True, stop=False)
                        last = pe.matmul(bank[b][1][:, h, :], wt[b][:, h, :], K.state[:, h, :], start=False, stop=True)
                    last.then_inc(S["vnew"], 1)
                    pe.wait_ge(S["vnc"], 4 + n + 1)
                    pe.wait_ge(S["eda"], 4 + n + 1)
                    for h in range(GH):
                        last = pe.matmul(bank[b][0][:, h, :], kd[b][:, h, :], vn[b][:, h, :], start=True, stop=True)
                    last.then_inc(S["kv"], 1)
                    for h in range(GH):
                        pe.matmul(bank[b][2][:, h, :], K.state[:, h, :], qd[b][:, h, :], start=True, stop=False)
                        last = pe.matmul(bank[b][2][:, h, :], vn[b][:, h, :], qk[b][:, h, :], start=False, stop=True)
                    last.then_inc(S["o"], 1)
                for b in range(2):
                    n = j * 2 + b
                    pe.wait_ge(S["osq"], 4 + n + 1)
                    pe.matmul(bank[b][3][:, :, :], K.ones[:, :], tmp[b][:, 0:GH, :], start=True, stop=True)\
                      .then_inc(S["oss"], 1)

        @block.scalar
        def _(act):
            with act.Fori(0, N // 2) as j:
                for b in range(2):
                    n = j * 2 + b
                    act.wait_ge(s_ld[b], 4 + j * 32 + 32)
                    act.wait_ge(S["ogain"], 4 + n - 1)
                    act.activation(tmp[b][:, :, :], raw[b][:, 0:2 * GH, :], ACT.Square).then_inc(S["sq"], 1)
                for b in range(2):
                    act.wait_ge(S["inv"], 4 + j * 2 + b + 1)
                    act.activation(tmp[b][:, :, :], tmp[b][:, :, :], ACT.Sqrt).then_inc(S["rs"], 1)
                for b in range(2):
                    act.wait_ge(S["row"], 4 + j * 2 + b + 1)
                    act.activation(er[b][:, :, :], bank[b][2][:, :, :], ACT.Exp).then_inc(S["er"], 1)
                for b in range(2):
                    act.wait_ge(S["dif"], 4 + j * 2 + b + 1)
                    act.activation(et[b][:, :, :], et[b][:, :, :], ACT.Exp)
                    act.activation(el[b][:, :, :], el[b][:, :, :], ACT.Exp, scale=-1.0).then_inc(S["dec"], 1)
                for l in range(1, LEVELS):
                    for b in range(2):
                        m = j * 2 * (LEVELS - 1) + (l - 1) * 2 + b
                        act.wait_ge(S["yv"], 4 + m + 1)
                        act.activation(y[b][:, :, :], bank[b][1][:, :, :], ACT.Copy).then_inc(S["ycopy"], 1)
                for b in range(2):
                    act.wait_ge(S["wt"], 4 + j * 2 + b + 1)
                    act.activation(wt[b][:, :, :], bank[b][3][:, :, :], ACT.Copy, scale=-1.0).then_inc(S["wtc"], 1)
                for b in range(2):
                    n = j * 2 + b
                    act.wait_ge(S["vnew"], 4 + n + 1)
                    act.activation(vn[b][:, :, :], bank[b][1][:, :, :], ACT.Copy).then_inc(S["vnc"], 1)
                    act.wait_ge(S["o"], 4 + n + 1)
                    act.activation(tmp[b][:, 0:GH, :], bank[b][2][:, :, :], ACT.Square)
                    act.activation(osb[b][:, :, :], bank[b][2][:, :, :], ACT.Copy).then_inc(S["osq"], 1)
                for b in range(2):
                    act.wait_ge(S["oinv"], 4 + j * 2 + b + 1)
                    act.activation(tmp[b][:, GH:, :], tmp[b][:, GH:, :], ACT.Sqrt).then_inc(S["ors"], 1)

        @block.gpsimd
        def _(pool):
            pool.memset(K.state[:, :, :], 0.0).then_inc(S["zero"], 1)
            with pool.Fori(0, N // 2) as j:
                for b in range(2):
                    n = j * 2 + b
                    pool.wait_ge(S["row"], 4 + n - 1)
                    pool.tensor_copy(gb[b][:, :, :], K.g[:, ds(n, 1), :].rearrange("p o h -> p (o h)").unsqueeze(2).broadcast_to(HW))\
                        .then_inc(S["gb"], 1)
                for b in range(2):
                    n = j * 2 + b
                    pool.wait_ge(S["er"], 4 + n + 1)
                    pool.wait_ge(S["norm"], 4 + n + 1)
                    pool.wait_ge(S["o"], 4 + n - 1)
                    pool.tensor_tensor(qd[b][:, :, :], kq[b][:, :, 1, :], er[b][:, :, :], ALU.mult)
                    pool.wait_ge(S["dec"], 4 + n + 1)
                    pool.tensor_tensor(et[b][:, :, :], et[b][:, :, :], wide(K.upto[:, :]), ALU.mult)
                    pool.tensor_tensor(el[b][:, :, :], el[b][:, :, :], wide(K.after[:, :]), ALU.mult).then_inc(S["eda"], 1)
                for l in range(1, LEVELS):
                    for b in range(2):
                        n = j * 2 + b
                        m = j * 2 * (LEVELS - 1) + (l - 1) * 2 + b
                        pool.wait_ge(S["first"], 4 + n + 1)
                        if l > 1:
                            pool.wait_ge(S["yv"], 4 + m - 1)
                        pool.tensor_tensor(atm[b][:, :, :], at[b][:, :, :], wide(K.join_t[:, l, :]), ALU.mult)\
                            .then_inc(S["mask"], 1)
                for b in range(2):
                    n = j * 2 + b
                    pool.wait_ge(S["ogain"], 4 + n + 1)
                    pool.wait_ge(s_ld[b], 4 + j * 32 + 32)
                    pool.tensor_tensor(orr[b][:, :, :], orr[b][:, :, :], z[b][:, :, :], ALU.mult).then_inc(S["res"], 1)

        @block.vector
        def _(dve):
            dve.wait_ge(S["gain"], 4 + 16)
            dve.wait_ge(S["zero"], 4 + 1)
            step = Steps(dve, s_step)
            with dve.Fori(0, N // 2) as j:
                step.enter(j, 8, N // 2)
                for b in range(2):
                    n = j * 2 + b
                    dve.wait_ge(S["ss"], 4 + n + 1)
                    for i in range(2):
                        last = dve.tensor_scalar(tmp[b][:, i * GH:(i + 1) * GH, :], bank[b][i][:, :, :], EPS, None, ALU.add)
                    step.link(last)
                    dve.reciprocal(tmp[b][:, :, :], tmp[b][:, :, :]).then_inc(S["inv"], 1)
                for b in range(2):
                    n = j * 2 + b
                    dve.wait_ge(S["er"], 4 + n + 1)
                    for h in range(GH):
                        gc = K.decay_sum[:, ds(n, 1), h]
                        dve.tensor_scalar(et[b][:, h, :], bank[b][2][:, h, :], gc, 0.0, ALU.subtract, ALU.min)
                        last = dve.tensor_scalar(el[b][:, h, :], bank[b][2][:, h, :], gc, 0.0, ALU.subtract, ALU.max)
                    last.then_inc(S["dif"], 1)
                for b in range(2):
                    n = j * 2 + b
                    dve.wait_ge(S["rs"], 4 + n + 1)
                    dve.tensor_tensor(kq[b][:, :, 0, :], raw[b][:, GH:2 * GH, :], tmp[b][:, GH:, :], ALU.mult)
                    dve.scalar_tensor_tensor(out=kq[b][:, :, 1, :], in0=raw[b][:, 0:GH, :], scalar=HD ** -0.5,
                                             in1=tmp[b][:, 0:GH, :], op0=ALU.mult, op1=ALU.mult).then_inc(S["norm"], 1)
                for b in range(2):
                    n = j * 2 + b
                    col = lambda t: t[:, ds(n, 1), :].rearrange("p o h -> p (o h)").unsqueeze(2).broadcast_to(HW)
                    dve.wait_ge(S["turn"], 4 + n + 1)
                    dve.tensor_tensor(kw[b][:, :, :], bank[b][0][:, :, :], col(K.bexp), ALU.mult)
                    dve.tensor_tensor(kd[b][:, :, :], bank[b][0][:, :, :], col(K.kdec), ALU.mult)
                    dve.tensor_tensor(vb[b][:, :, :], bank[b][1][:, :, :], col(K.beta), ALU.mult).then_inc(S["tok"], 1)
                for b in range(2):
                    n = j * 2 + b
                    dve.wait_ge(S["gram"], 4 + n + 1)
                    dve.wait_ge(S["eda"], 4 + n + 1)
                    for h in range(GH):
                        bk, o = bank[b][2 + h // 2], (h % 2) * 2
                        dve.tensor_tensor(qk[b][:, h, :], bk[:, o + 1, :], et[b][:, h, :], ALU.mult)
                        last = dve.scalar_tensor_tensor(out=am[b][:, h, :], in0=bk[:, o, :], scalar=K.beta[:, ds(n, 1), h],
                                                        in1=el[b][:, h, :], op0=ALU.mult, op1=ALU.mult)
                    last.then_inc(S["sys"], 1)
                for b in range(2):
                    n = j * 2 + b
                    dve.wait_ge(S["sys"], 4 + n + 1)
                    step.link(dve.tensor_tensor(x[b][:, :, :], am[b][:, :, :], wide(K.join[:, 0, :]), ALU.mult))
                    dve.tensor_tensor(x[b][:, :, :], wide(K.ident[:, :]), x[b][:, :, :], ALU.subtract)
                    dve.wait_ge(S["syst"], 4 + n + 1)
                    step.link(dve.tensor_copy(at[b][:, :, :], bank[b][0][:, :, :]))
                    dve.tensor_tensor(xt[b][:, :, :], at[b][:, :, :], wide(K.join_t[:, 0, :]), ALU.mult).then_inc(S["attn"], 1)
                    dve.wait_ge(S["attn"], 4 + n + 1)
                    dve.tensor_tensor(xt[b][:, :, :], wide(K.ident[:, :]), xt[b][:, :, :], ALU.subtract).then_inc(S["first"], 1)
                for l in range(1, LEVELS):
                    for b in range(2):
                        m = j * 2 * (LEVELS - 1) + (l - 1) * 2 + b
                        dve.wait_ge(S["prod"], 4 + m + 1)
                        dve.tensor_tensor(x[b][:, :, :], x[b][:, :, :], bank[b][0][:, :, :], ALU.subtract)
                        dve.tensor_tensor(xt[b][:, :, :], xt[b][:, :, :], bank[b][2][:, :, :], ALU.subtract).then_inc(S["upd"], 1)
                for b in range(2):
                    n = j * 2 + b
                    dve.wait_ge(S["o"], 4 + n + 1)
                    for h in range(GH):
                        last = dve.scalar_tensor_tensor(out=K.state[:, h, :], in0=K.state[:, h, :], scalar=K.glast[:, ds(n, 1), h],
                                                        in1=bank[b][0][:, h, :], op0=ALU.mult, op1=ALU.add)
                    last.then_inc(S["state"], 1)
                for b in range(2):
                    n = j * 2 + b
                    dve.wait_ge(S["oss"], 4 + n + 1)
                    step.link(dve.tensor_scalar(tmp[b][:, GH:, :], bank[b][3][:, :, :], 1.0 / HD, EPS, ALU.mult, ALU.add))
                    dve.reciprocal(tmp[b][:, GH:, :], tmp[b][:, GH:, :]).then_inc(S["oinv"], 1)
                for b in range(2):
                    n = j * 2 + b
                    dve.wait_ge(S["ors"], 4 + n + 1)
                    dve.wait_ge(s_st[b], 4 + j * 16)
                    dve.scalar_tensor_tensor(out=orr[b][:, :, :], in0=osb[b][:, :, :], scalar=gain[:, 0:1],
                                             in1=tmp[b][:, GH:, :], op0=ALU.mult, op1=ALU.mult).then_inc(S["ogain"], 1)
                step.leave()


class Events(dict):

    def __init__(self, c):
        super().__init__()
        self.c = c

    def __missing__(self, name):
        self[name] = self.c.sem(name)
        return self[name]


class Chain:

    def __init__(self, eng, sem):
        self.eng, self.sem, self.n = eng, sem, 0

    def __call__(self, ins):
        self.n += 1
        ins.then_inc(self.sem, 1)
        self.eng.wait_ge(self.sem, self.n)


def delta_step(nc, K, state_in, out_gain, outs):
    R = GH * DEC
    with phase(nc, "dstep") as (c, stack):
        raw, z = c.sb("raw", [P, 3 * GH, DEC]), c.sb("z", [P, GH, DEC])
        st = c.sb("st", [P, R, HD])
        sq = c.sb("sq", [P, 2 * GH, DEC])
        dg = c.sb("dg", [DEC, 2, GH, DEC])
        eg, beta = c.sb("eg", [P, R]), c.sb("beta", [P, R])
        kn, kq = c.sb("kn", [P, R]), c.sb("kq", [P, R, 2])
        qn, prod, vn = c.sb("qn", [P, R]), c.sb("prod", [P, R]), c.sb("vn", [P, R])
        tmp, o, osq, inv = c.sb("tmp", [P, R]), c.sb("o", [P, R]), c.sb("osq", [P, R]), c.sb("inv", [P, R])
        kt, vt = c.sb("kt", [R, P]), c.sb("vt", [R, P])
        vm = c.sb("vm", [R, R, HD])
        gain = c.sb("gain", [P, 1])
        p_ss, p_g, p_s = c.ps("ss", [P, 2 * R]), c.ps("g", [P, 2 * R]), c.ps("s", [P, R, 2])
        p_qk, p_t, p_oss = c.ps("qk", [P, R]), c.ps("t", [R, 2, P]), c.ps("oss", [P, R])
        p_u = [c.ps(f"u{i}", [P, 4, HD]) for i in range(2)]
        E = Events(c)
        s_upd = c.sem("upd")
        s_sum = c.sem("usum")
        flat = lambda t: t[:, :, :].rearrange("p h r -> p (h r)")
        block = open_block(nc, stack, c)

        @block.sync
        def _(sp):
            sp.dma_start(raw[:, :, :], K.d_qkv[:, :, SEQ:TOK].rearrange("m p r -> p m r")).then_inc(E["load"], 16)
            sp.dma_start(z[:, :, :], K.d_z[:, :, SEQ:TOK].rearrange("m p r -> p m r")).then_inc(E["load"], 16)
            sp.dma_start(gain[:, :], out_gain.rearrange("(p o) -> p o", o=1)).then_inc(E["load"], 16)
            for h in range(GH):
                sp.dma_start(st[:, h * DEC:(h + 1) * DEC, :], state_in[:, h, :, :].rearrange("b k v -> k b v"))\
                  .then_inc(E["state"], 16)
            sp.wait_ge(s_sum, R // 4)
            for h in range(GH):
                sp.dma_start(outs["s_gdn"][:, h, :, :].rearrange("b k v -> k b v"), st[:, h * DEC:(h + 1) * DEC, :])\
                  .then_inc(E["stored"], 16)
            sp.wait_ge(E["mixed"], 1)
            sp.dma_start(K.d_mix[0:GH, :, SEQ:TOK].rearrange("m p r -> p m r"), o[:, :].rearrange("p (h r) -> p h r", h=GH))\
              .then_inc(E["stored"], 16)
            sp.wait_ge(E["stored"], 80)

        @block.vector
        def _(dve):
            step = Chain(dve, E["dve"])
            for i, src in enumerate((K.g, K.beta)):
                last = dve.tensor_tensor(dg[:, i, :, :], src[0:DEC, NT, :].unsqueeze(2).broadcast_to([DEC, GH, DEC]),
                                         K.ident[0:DEC, 0:DEC].unsqueeze(1).broadcast_to([DEC, GH, DEC]), ALU.mult)
            last.then_inc(E["diagonal"], 1)
            dve.wait_ge(E["ss"], 1)
            step(dve.tensor_scalar(flat(sq), p_ss[:, :], EPS, None, ALU.add))
            dve.reciprocal(flat(sq), flat(sq)).then_inc(E["inv"], 1)
            dve.wait_ge(E["eg"], 1)
            step(dve.tensor_copy(beta[:, :], p_g[:, R:]))
            dve.wait_ge(E["rs"], 1)
            step(dve.tensor_tensor(kn[:, :], raw[:, GH:2 * GH, :].rearrange("p h r -> p (h r)"), flat(sq)[:, R:], ALU.mult))
            step(dve.scalar_tensor_tensor(out=qn[:, :], in0=raw[:, 0:GH, :].rearrange("p h r -> p (h r)"), scalar=HD ** -0.5,
                                          in1=flat(sq)[:, 0:R], op0=ALU.mult, op1=ALU.mult))
            dve.tensor_tensor(kq[:, :, 0], kn[:, :], eg[:, :], ALU.mult)
            dve.tensor_tensor(kq[:, :, 1], qn[:, :], eg[:, :], ALU.mult)
            dve.tensor_tensor(prod[:, :], qn[:, :], kn[:, :], ALU.mult).then_inc(E["columns"], 1)
            dve.wait_ge(E["read"], 1)
            step(dve.tensor_tensor(tmp[:, :], raw[:, 2 * GH:, :].rearrange("p h r -> p (h r)"), p_s[:, :, 0], ALU.subtract))
            dve.tensor_tensor(vn[:, :], tmp[:, :], beta[:, :], ALU.mult).then_inc(E["vnew"], 1)
            dve.wait_ge(E["vnew"], 1)
            step(dve.tensor_tensor(tmp[:, :], p_qk[:, :], vn[:, :], ALU.mult))
            step(dve.tensor_tensor(o[:, :], p_s[:, :, 1], tmp[:, :], ALU.add))
            dve.tensor_tensor(osq[:, :], o[:, :], o[:, :], ALU.mult).then_inc(E["osq"], 1)
            dve.wait_ge(E["turned"], 1)
            dve.tensor_copy(kt[:, :], p_t[:, 0, :])
            step(dve.tensor_copy(vt[:, :], p_t[:, 1, :]))
            dve.tensor_tensor(vm[:, :, :], vt[:, :].unsqueeze(1).broadcast_to([R, R, HD]),
                              K.ident[0:R, 0:R].unsqueeze(2).broadcast_to([R, R, HD]), ALU.mult).then_inc(E["apart"], 1)
            dve.wait_ge(E["state"], 64)
            dve.wait_ge(E["read"], 1)
            step(dve.tensor_tensor(st[:, :, :], st[:, :, :], eg[:, :].unsqueeze(2).broadcast_to([P, R, HD]), ALU.mult))
            for i in range(R // 4):
                dve.wait_ge(s_upd, i + 1)
                part = st[:, i * 4:(i + 1) * 4, :]
                dve.tensor_tensor(part, part, p_u[i % 2][:, :, :], ALU.add).then_inc(s_sum, 1)
            dve.wait_ge(E["oss"], 1)
            step(dve.tensor_scalar(inv[:, :], p_oss[:, :], 1.0 / HD, EPS, ALU.mult, ALU.add))
            dve.reciprocal(inv[:, :], inv[:, :]).then_inc(E["oinv"], 1)
            dve.wait_ge(E["ors"], 1)
            step(dve.scalar_tensor_tensor(out=o[:, :], in0=o[:, :], scalar=gain[:, 0:1], in1=inv[:, :], op0=ALU.mult, op1=ALU.mult))
            dve.tensor_tensor(o[:, :], o[:, :], flat(z), ALU.mult).then_inc(E["mixed"], 1)

        @block.scalar
        def _(act):
            act.wait_ge(E["load"], 48)
            act.activation(sq[:, :, :], raw[:, 0:2 * GH, :], ACT.Square).then_inc(E["sq"], 1)
            act.wait_ge(E["gates"], 1)
            act.activation(eg[:, :], p_g[:, 0:R], ACT.Exp).then_inc(E["eg"], 1)
            act.wait_ge(E["inv"], 1)
            act.activation(sq[:, :, :], sq[:, :, :], ACT.Sqrt).then_inc(E["rs"], 1)
            act.wait_ge(E["oinv"], 1)
            act.activation(inv[:, :], inv[:, :], ACT.Sqrt).then_inc(E["ors"], 1)

        @block.tensor
        def _(pe):
            pe.wait_ge(E["diagonal"], 1)
            pe.matmul(p_g[:, :], K.ones[0:DEC, :], dg[:, :, :, :].rearrange("r i h s -> r (i h s)"), start=True, stop=True)\
              .then_inc(E["gates"], 1)
            pe.wait_ge(E["sq"], 1)
            pe.matmul(p_ss[:, :], K.ones[:, :], flat(sq), start=True, stop=True).then_inc(E["ss"], 1)
            pe.wait_ge(E["columns"], 1)
            pe.wait_ge(E["state"], 64)
            for i in range(R):
                pe.matmul(p_s[:, i, :], st[:, i, :], kq[:, i, :], start=True, stop=True)
            pe.matmul(p_qk[:, :], K.ones[:, :], prod[:, :], start=True, stop=True).then_inc(E["read"], 1)
            pe.wait_ge(E["vnew"], 1)
            pe.transpose(p_t[:, 0, :], kn[:, :], K.ident[:, :])
            pe.transpose(p_t[:, 1, :], vn[:, :], K.ident[:, :]).then_inc(E["turned"], 1)
            pe.wait_ge(E["osq"], 1)
            pe.matmul(p_oss[:, :], K.ones[:, :], osq[:, :], start=True, stop=True).then_inc(E["oss"], 1)
            pe.wait_ge(E["apart"], 1)
            for i in range(R // 4):
                if i >= 2:
                    pe.wait_ge(s_sum, i - 1)
                pe.matmul(p_u[i % 2][:, :, :], kt[:, :], vm[:, i * 4:(i + 1) * 4, :], start=True, stop=True).then_inc(s_upd, 1)


def attend(nc, K, q_norm, outs):
    NK = SEQ
    with phase(nc, "att") as (c, stack):
        two = lambda name, shape, dt=F32: [c.sb(f"{name}{b}", shape, dt) for b in range(2)]
        qin, qg, iqin = two("qin", [P, QH, P]), two("qg", [P, QH, P]), two("iqin", [P, IH // 2, P])
        qsq = two("qsq", [P, QH, P])
        rq = c.sb("rq", [P, 2, QH])
        iw = c.sb("iw", [P, TILES, IH])
        r = [c.sb(f"r{i}", [P, 512]) for i in range(2)]
        sc = two("sc", [P, NK])
        above = c.sb("above", [P, NK], BF16)
        tie = c.sb("tie", [P, NK], BF16)
        hits = [above, tie]
        mask = two("mask", [P, NK], BF16)
        logit = two("logit", [P, QH, P + NK])
        pt = [c.sb(f"pt{i}", [P, 4, P]) for i in range(2)]
        ob, ot = two("ob", [P, QH, HD]), two("ot", [P, QH, P])
        gain = c.sb("gain", [P, 1])
        trial, other, miss = (c.sb(n, [P, 2], I32) for n in ("trial", "other", "miss"))
        count = c.sb("count", [P, 2])
        top = c.sb("top", [P, 2, QH])
        total = c.sb("total", [P, 2, QH])
        inv = c.sb("inv", [P, 2, QH])
        p_sc = [c.ps(f"sc{i}", [P, 512]) for i in range(2)]
        p_lg = [c.ps(f"lg{i}", [P, 512]) for i in range(2)]
        p_t = [c.ps(f"t{i}", [P, 4, P]) for i in range(2)]
        p_o = c.ps("o", [P, QH, HD])
        p_m = c.ps("m", [P, 512])
        S = {n: c.sem(n) for n in ("gain out zero sq qg ss mean rq sc relu sum added step lg lgc max exp turn ptc pv "
                                   "norm oturn otc").split()}
        s_q, s_iq = c.sems("q"), c.sems("iq")
        s_st = c.sems("st")
        block = open_block(nc, stack, c)
        per_turn = [2 + 4 + 3 * 31 + 2 * (6 + (G == 0)) + 2 + 2 for G in range(4)]
        before = lambda G: sum(4 * (g + 1) for g in range(G))

        def su(G, j, b, h=0, kc=0):
            return j * (16 * (G + 1)) + (IH * before(G) + b * 8 * (G + 1) + h * (G + 1) + kc)

        def lu(G, j, b, h=0, kc=0):
            return j * (8 * (G + 1)) + (QH * before(G) + b * 4 * (G + 1) + h * (G + 1) + kc)

        @block.sync
        def _(sp):
            credit(sp, c)
            sp.dma_start(gain[:, :], q_norm.rearrange("(p o) -> p o", o=1)).then_inc(S["gain"], 16)

            def load(i, b):
                sp.wait_ge(S["sq"], 4 + i * 2)
                sp.wait_ge(S["qg"], 4 + i * 2)
                sp.dma_start(qin[b][:, :, :], K.d_q[:, :, ds(i * 256 + b * P, P)].rearrange("m p n -> p m n")).then_inc(s_q[b], 16)
                sp.wait_ge(S["added"], 4 + i * 2)
                sp.dma_start(iqin[b][:, :, :], K.d_iq[:, :, ds(i * 256 + b * P, P)].rearrange("m p n -> p m n")).then_inc(s_iq[b], 16)

            def store(i, b):
                sp.wait_ge(S["otc"], 4 + i * 2 + b + 1)
                sp.dma_start(K.d_mix[GH:, :, ds(i * 256 + b * P, P)].rearrange("m p n -> p m n"), ot[b][:, :, :])\
                  .then_inc(s_st[b], 16)
            for b in range(2):
                load(0, b)
            with sp.Fori(0, NT // 2 - 1) as i:
                for b in range(2):
                    load(i + 1, b)
                for b in range(2):
                    store(i, b)
            for b in range(2):
                store(NT // 2 - 1, b)
            for b in range(2):
                sp.wait_ge(s_st[b], 4 + NT // 2 * 16)

        @block.tensor
        def _(pe):
            for G in range(4):
                with pe.Fori(0, 2) as j:
                    i = j + G * 2
                    for b in range(2):
                        pe.wait_ge(S["sq"], 4 + i * 2 + b + 1)
                        pe.wait_ge(S["mean"], 4 + i)
                        pe.wait_ge(S["otc"], 4 + i * 2)
                        for h in range(QH):
                            last = pe.matmul(p_m[:, b * QH + h:b * QH + h + 1], qsq[b][:, h, :], K.ones[:, 0:1],
                                             start=True, stop=True)
                    last.then_inc(S["ss"], 1)
                    for b in range(2):
                        pe.wait_ge(s_iq[b], 4 + i * 16 + 16)
                        for h in range(IH):
                            half = slice((h % 2) * ID, (h % 2 + 1) * ID)
                            for kc in range(G + 1):
                                pe.wait_ge(S["relu"], 4 + su(G, j, b, h, kc) - 1)
                                pe.matmul(p_sc[(h * (G + 1) + kc) % 2][:, :], iqin[b][half, h // 2, :],
                                          K.ikt[half, kc * 512:(kc + 1) * 512], start=True, stop=True).then_inc(S["sc"], 1)
                    for b in range(2):
                        pe.wait_ge(S["qg"], 4 + i * 2 + b + 1)
                        for h in range(QH):
                            for kc in range(G + 1):
                                pe.wait_ge(S["lgc"], 4 + lu(G, j, b, h, kc) - 1)
                                pe.matmul(p_lg[(h * (G + 1) + kc) % 2][:, :], qg[b][:, h, :],
                                          K.kt[:, h // GROUP, kc * 512:(kc + 1) * 512], start=True, stop=True).then_inc(S["lg"], 1)
                    for b in range(2):
                        def turn(u):
                            h, kc = divmod(u, G + 1)
                            pe.wait_ge(S["exp"], 4 + (i * 2 + b) * QH + h + 1)
                            pe.wait_ge(S["ptc"], 4 + lu(G, j, b, h, kc) - 1)
                            for k in range(4):
                                col = P + kc * 512 + k * P
                                last = pe.transpose(p_t[u % 2][:, k, :], logit[b][:, h, col:col + P], K.ident[:, :])
                            last.then_inc(S["turn"], 1)
                        U = QH * (G + 1)
                        pe.wait_ge(S["norm"], 4 + i * 2 + b)
                        turn(0)
                        for u in range(U):
                            h, kc = divmod(u, G + 1)
                            if u + 1 < U:
                                turn(u + 1)
                            pe.wait_ge(S["ptc"], 4 + lu(G, j, b, h, kc) + 1)
                            for k in range(4):
                                last = pe.matmul(p_o[:, h, :], pt[u % 2][:, k, :],
                                                 K.v[:, kc * 4 + k, (h // GROUP) * HD:(h // GROUP + 1) * HD],
                                                 start=(kc == 0 and k == 0), stop=(kc == G and k == 3))
                            last.then_inc(S["pv"], 1)
                        pe.wait_ge(S["norm"], 4 + i * 2 + b + 1)
                        pe.wait_ge(S["otc"], 4 + i * 2 + b)
                        for h in range(QH):
                            last = pe.transpose(p_m[:, h * P:(h + 1) * P], ob[b][:, h, :], K.ident[:, :])
                        last.then_inc(S["oturn"], 1)

        @block.scalar
        def _(act):
            act.wait_ge(S["gain"], 4 + 16)
            for G in range(4):
                with act.Fori(0, 2) as j:
                    i = j + G * 2
                    for b in range(2):
                        act.wait_ge(s_q[b], 4 + i * 16 + 16)
                        act.wait_ge(S["ss"], 4 + i)
                        act.activation(qsq[b][:, :, :], qin[b][:, :, :], ACT.Square).then_inc(S["sq"], 1)
                        act.wait_ge(S["norm"], 4 + i * 2)
                        act.activation(qg[b][:, :, :], qin[b][:, :, :], ACT.Copy, scale=gain[:, 0:1]).then_inc(S["qg"], 1)
                    act.wait_ge(S["mean"], 4 + i + 1)
                    act.activation(rq[:, :, :], rq[:, :, :], ACT.Sqrt).then_inc(S["rq"], 1)
                    for b in range(2):
                        for u in range(IH * (G + 1)):
                            n = su(G, j, b) + u
                            act.wait_ge(S["sc"], 4 + n + 1)
                            act.wait_ge(S["sum"], 4 + n - 1)
                            act.activation(r[u % 2][:, :], p_sc[u % 2][:, :], ACT.Relu).then_inc(S["relu"], 1)
                    for b in range(2):
                        act.wait_ge(S["max"], 4 + i * 2 + b + 1)
                        for h in range(QH):
                            row = logit[b][:, h, P:P + (G + 1) * 512]
                            act.activation(row, row, ACT.Exp, bias=top[:, b, h:h + 1], accum_out=total[:, b, h:h + 1])\
                               .then_inc(S["exp"], 1)
                        for u in range(QH * (G + 1)):
                            n = lu(G, j, b) + u
                            act.wait_ge(S["turn"], 4 + n + 1)
                            act.wait_ge(S["pv"], 4 + n - 1)
                            act.activation(pt[u % 2][:, :, :], p_t[u % 2][:, :, :], ACT.Copy).then_inc(S["ptc"], 1)
                        act.wait_ge(S["oturn"], 4 + i * 2 + b + 1)
                        act.wait_ge(s_st[b], 4 + i * 16)
                        act.activation(ot[b][:, :, :], p_m[:, :].rearrange("p (h n) -> p h n", h=QH), ACT.Copy)\
                           .then_inc(S["otc"], 1)

        @block.vector
        def _(dve):
            step = Steps(dve, S["step"])
            for b in range(2):
                dve.memset(logit[b][:, :, 0:P], 0.0)
            step.link(dve.tensor_scalar(iw[:, :, :], K.small[:, :, 2 * GH + ID:], INDEX_SCALE, None, ALU.mult))
            for G in range(4):
                nk = (G + 1) * 512
                with dve.Fori(0, 2) as j:
                    i = j + G * 2
                    step.enter(j, per_turn[G], 2)
                    dve.wait_ge(S["ss"], 4 + i + 1)
                    ss = p_m[:, 0:2 * QH].rearrange("p (b h) -> p b h", b=2)
                    step.link(dve.tensor_scalar(rq[:, :, :], ss, 1.0 / HD, EPS, ALU.mult, ALU.add))
                    dve.reciprocal(rq[:, :, :], rq[:, :, :]).then_inc(S["mean"], 1)
                    dve.wait_ge(S["rq"], 4 + i + 1)
                    step.link(dve.tensor_scalar(rq[:, :, :], rq[:, :, :], SCALE, None, ALU.mult))
                    for b in range(2):
                        for h in range(IH):
                            w = iw[:, ds(i * 2 + b, 1), h]
                            for kc in range(G + 1):
                                n, u = su(G, j, b, h, kc), h * (G + 1) + kc
                                part = sc[b][:, kc * 512:(kc + 1) * 512]
                                dve.wait_ge(S["relu"], 4 + n + 1)
                                if h == 0:
                                    dve.tensor_scalar(part, r[u % 2][:, :], w, None, ALU.mult).then_inc(S["sum"], 1)
                                else:
                                    dve.wait_ge(S["sum"], 4 + n - G)
                                    dve.scalar_tensor_tensor(out=part, in0=r[u % 2][:, :], scalar=w, in1=part,
                                                             op0=ALU.mult, op1=ALU.add).then_inc(S["sum"], 1)
                        dve.wait_ge(S["sum"], 4 + su(G, j, b + 1))
                        own = sc[b][:, G * 512:nk]
                        dve.tensor_tensor(own, own, K.below[:, ds((j * 2 + b) * -P + 384, 512)], ALU.min).then_inc(S["added"], 1)
                    dve.wait_ge(S["added"], 4 + i * 2 + 2)
                    for b in range(2):
                        last = dve.tensor_scalar(hits[b][:, 0:nk], sc[b][:, 0:nk], 0.0, None, ALU.is_ge, ALU.add,
                                                 accum_out=count[:, b:b + 1])
                    step.link(last)
                    step.link(dve.tensor_scalar(miss[:, :], count[:, :], float(NSEL), None, ALU.is_lt))
                    step.link(dve.tensor_scalar(trial[:, :], miss[:, :], 31, 31, ALU.logical_shift_left, ALU.arith_shift_right))
                    step.link(dve.tensor_scalar(trial[:, :], trial[:, :], 1 << 30, None, ALU.bitwise_xor))
                    for bit in range(30, -1, -1):
                        level = trial[:, :].bitcast(F32)
                        for b in range(2):
                            last = dve.tensor_scalar(hits[b][:, 0:nk], sc[b][:, 0:nk], level[:, b:b + 1], None, ALU.is_ge, ALU.add,
                                                     accum_out=count[:, b:b + 1])
                        if bit:
                            dve.tensor_scalar(other[:, :], trial[:, :], 1 << (bit - 1), None, ALU.bitwise_xor)
                        else:
                            dve.tensor_copy(other[:, :], trial[:, :])
                        step.link(last)
                        step.link(dve.tensor_scalar(miss[:, :], count[:, :], float(NSEL), None, ALU.is_lt))
                        step.link(dve.scalar_tensor_tensor(out=trial[:, :], in0=miss[:, :], scalar=bit, in1=other[:, :],
                                                           op0=ALU.logical_shift_left, op1=ALU.bitwise_xor))
                    for b in range(2):
                        s, m = sc[b][:, 0:nk], mask[b][:, 0:nk]
                        level = trial[:, b:b + 1].bitcast(F32)
                        order = logit[b][:, 0, P:P + nk]
                        dve.tensor_scalar(tie[:, 0:nk], s, level, None, ALU.is_equal)
                        step.link(dve.tensor_scalar(above[:, 0:nk], s, level, None, ALU.is_gt, ALU.add,
                                                    accum_out=count[:, b:b + 1]))
                        dve.wait_ge(S["pv"], 4 + lu(G, j, 0))
                        step.link(dve.tensor_scalar(count[:, b:b + 1], count[:, b:b + 1], -1.0, float(NSEL), ALU.mult, ALU.add))
                        step.link(dve.tensor_tensor_scan(order, tie[:, 0:nk], tie[:, 0:nk], 0.0, ALU.add, ALU.bypass))
                        step.link(dve.scalar_tensor_tensor(out=tie[:, 0:nk], in0=order, scalar=count[:, b:b + 1], in1=tie[:, 0:nk],
                                                           op0=ALU.is_le, op1=ALU.mult))
                        step.link(dve.tensor_tensor(m, above[:, 0:nk], tie[:, 0:nk], ALU.add))
                        if G == 0:
                            step.link(dve.scalar_tensor_tensor(out=m, in0=s, scalar=-BIG, in1=m, op0=ALU.is_gt, op1=ALU.mult))
                        step.link(dve.tensor_scalar(m, m, -1.0, -NEG, ALU.add, ALU.mult))
                    for b in range(2):
                        for h in range(QH):
                            for kc in range(G + 1):
                                n, u = lu(G, j, b, h, kc), h * (G + 1) + kc
                                dve.wait_ge(S["lg"], 4 + n + 1)
                                dve.scalar_tensor_tensor(out=logit[b][:, h, P + kc * 512:P + (kc + 1) * 512], in0=p_lg[u % 2][:, :],
                                                         scalar=rq[:, b, h:h + 1], in1=mask[b][:, kc * 512:(kc + 1) * 512],
                                                         op0=ALU.mult, op1=ALU.add).then_inc(S["lgc"], 1)
                        dve.wait_ge(S["lgc"], 4 + lu(G, j, b + 1))
                        near = logit[b][:, :, ds((i * 2 + b) * P, 256)]
                        step.link(dve.tensor_tensor(near, near, K.near[:, :, :], ALU.add))
                        dve.tensor_reduce(top[:, b, :], logit[b][:, :, P:P + nk], AX.X, ALU.max, negate=True).then_inc(S["max"], 1)
                    for b in range(2):
                        dve.wait_ge(S["exp"], 4 + (i * 2 + b + 1) * QH)
                        step.link(dve.reciprocal(inv[:, b, :], total[:, b, :]))
                        dve.wait_ge(S["pv"], 4 + lu(G, j, b + 1))
                        dve.tensor_tensor(ob[b][:, :, :], p_o[:, :, :], inv[:, b, :].unsqueeze(2).broadcast_to([P, QH, HD]), ALU.mult)\
                           .then_inc(S["norm"], 1)
                    step.leave()


PAIRS = DEC // 2
HEADCOLS = 2 * QH


def step_select(nc, K, idx_cache, page_table):
    with phase(nc, "pick") as (c, stack):
        pid = c.sb("pid", [P, PAIRS], I32)
        pages = [c.sb(f"pages{b}", [P, PAGE // 2, P]) for b in range(2)]
        iqs = c.sb("iqs", [P, IH // 2, 2, DEC])
        bd = c.sb("bd", [P, PAIRS, 2, 2, IH])
        turned = [c.sb(f"turned{b}", [P, 4, P]) for b in range(2)]
        wd, wsel = c.sb("wd", [DEC, DEC, IH]), c.sb("wsel", [P, PAIRS, 2, IH])
        wrow = c.sb("wrow", [P, DEC, IH])
        prod, rel = c.sb("prod", [ID, IH, DEC]), c.sb("rel", [P, DEC, IH])
        snew, sn = c.sb("snew", [P, DEC]), c.sb("sn", [P, PAIRS])
        part = [c.sb(f"part{b}", [P, 8, 2 * IH]) for b in range(2)]
        s, hit, tie, order = (c.sb(n, [P, PAIRS, PAGE]) for n in "s hit tie order".split())
        small = lambda n, dt=F32: c.sb(n, [P, PAIRS], dt)
        row, nhit, count, need, tierow, newtie = (small(n) for n in "row nhit count need tierow newtie".split())
        trial, other, miss = (small(n, I32) for n in "trial other miss".split())
        before2 = c.sb("before2", [P, P])
        p_t = [c.ps(f"t{b}", [P, 4, P]) for b in range(2)]
        p_x = [c.ps(f"x{b}", [P, 512]) for b in range(2)]
        p_w, p_c, p_n = c.ps("w", [P, 512]), c.ps("c", [P, 512]), c.ps("n", [P, 512])
        S = {n: c.sem(n) for n in "pid iq bd step turn copy score mul sum wd w rowcount total".split()}
        s_page = c.own_sems("page")
        block = open_block(nc, stack, c)
        cache = idx_cache.rearrange("n p d -> n (p d)")
        UNITS = PAGE // 8

        @block.sync
        def _(sp):
            credit(sp, c)
            table = page_table.rearrange("(i q) c -> q c i", q=2)
            for req in range(2):
                sp.dma_start(pid[req * NPAGE:(req + 1) * NPAGE, :], table[req], allow_slow_non_contiguous=True)\
                  .then_inc(S["pid"], 16)
            for k in range(2):
                for hp in range(2):
                    sp.dma_start(iqs[k * ID:(k + 1) * ID, :, hp, :],
                                 K.d_iq[:, hp * ID:(hp + 1) * ID, SEQ:TOK].rearrange("m d b -> d m b")).then_inc(S["iq"], 16)
            sp.wait_ge(S["iq"], 4 + 64)

        @block.gpsimd
        def _(pool):
            pool.wait_ge(S["pid"], 4 + 32)
            for i in range(PAIRS):
                if i >= 2:
                    pool.wait_ge(S["turn"], 4 + (i - 1) * UNITS)
                pool.indirect_dma_start(pages[i % 2][:, :, :].rearrange("p a b -> p (a b)"), None, cache,
                                        bass.IndirectOffsetOnAxis(ap=pid[:, i:i + 1].bitcast(U32), axis=0)).then_inc(s_page[i % 2], 16)

        @block.tensor
        def _(pe):
            pe.wait_ge(S["wd"], 4 + 1)
            pe.matmul(p_w[:, 0:DEC * IH], K.ones[0:DEC, :], wd[:, :, :].rearrange("r q h -> r (q h)"),
                      start=True, stop=True).then_inc(S["w"], 1)
            pe.wait_ge(S["wd"], 4 + 2)
            pe.matmul(p_n[:, 0:DEC * IH], K.ones[0:ID, :], prod[:, :, :].rearrange("d h r -> d (h r)"),
                      start=True, stop=True).then_inc(S["w"], 1)
            pe.wait_ge(S["bd"], 4 + 1)
            with pe.Fori(0, PAIRS // 2) as j:
                for b in range(2):
                    pe.wait_ge(s_page[b], j * 16 + 16)

                    def turn(u):
                        pe.wait_ge(S["copy"], 4 + (j * 2 + b) * UNITS + u - 1)
                        for k in range(4):
                            last = pe.transpose(p_t[u % 2][:, k, :], pages[b][:, u * 4 + k, :], K.ident[:, :])
                        last.then_inc(S["turn"], 1)
                    turn(0)
                    for u in range(UNITS):
                        n = (j * 2 + b) * UNITS + u
                        if u + 1 < UNITS:
                            turn(u + 1)
                        pe.wait_ge(S["copy"], 4 + n + 1)
                        pe.wait_ge(S["mul"], 4 + n - 1)
                        for k in range(4):
                            last = pe.matmul(p_x[u % 2][:, k * 32:(k + 1) * 32], turned[u % 2][:, k, :],
                                             bd[:, ds(j * 2 + b, 1), :, :, :].rearrange("p i k q h -> p (i k q h)"),
                                             start=True, stop=True)
                        last.then_inc(S["score"], 1)
            for m in range(32 + 1):
                pe.wait_ge(S["rowcount"], 4 + m + 1)
                pe.matmul(p_c[:, 0:PAIRS], K.halves[:, :], row[:, :], start=True, stop=True).then_inc(S["total"], 1)
            pe.wait_ge(S["rowcount"], 4 + 34)
            pe.matmul(p_c[:, 0:PAIRS], before2[:, :], tierow[:, :], start=True, stop=True)
            pe.matmul(p_c[:, PAIRS:2 * PAIRS], K.halves[:, :], tierow[:, :], start=True, stop=True).then_inc(S["total"], 1)

        @block.scalar
        def _(act):
            with act.Fori(0, PAIRS // 2) as j:
                for t in range(UNITS):
                    for b in range(2):
                        n = j * (2 * UNITS) + t * 2 + b
                        act.wait_ge(S["turn"], 4 + n + 1)
                        act.wait_ge(S["score"], 4 + n - 1)
                        act.activation(turned[b][:, :, :], p_t[b][:, :, :], ACT.Copy).then_inc(S["copy"], 1)

        @block.vector
        def _(dve):
            step = Steps(dve, S["step"])
            dve.tensor_copy(K.half[:, 0:1], K.upto[:, NPAGE - 1:NPAGE])
            step.link(dve.tensor_scalar(K.half[:, 1:2], K.upto[:, NPAGE - 1:NPAGE], -1.0, 1.0, ALU.mult, ALU.add))
            step.link(dve.tensor_copy(K.halves[:, :].rearrange("p (q c) -> p q c", q=2),
                                      K.half[:, :].unsqueeze(2).broadcast_to([P, 2, NPAGE])))
            dve.tensor_tensor(before2[:, :], K.halves[:, :], K.before[:, :], ALU.mult)
            step.link(dve.tensor_scalar(wd[:, :, :], K.small[0:DEC, NT, 2 * GH + ID:].unsqueeze(1).broadcast_to([DEC, DEC, IH]),
                                        INDEX_SCALE, None, ALU.mult))
            dve.tensor_tensor(wd[:, :, :], wd[:, :, :], K.ident[0:DEC, 0:DEC].unsqueeze(2).broadcast_to([DEC, DEC, IH]), ALU.mult)\
               .then_inc(S["wd"], 1)
            step.link(dve.memset(bd[:, :, :, :, :], 0.0))
            dve.wait_ge(S["iq"], 4 + 64)
            for k in range(2):
                part_of = slice(k * ID, (k + 1) * ID)
                for req in range(2):
                    last = dve.tensor_copy(bd[part_of, :, k, req, :],
                                           iqs[part_of, :, :, req::2].rearrange("p m q i -> p i (m q)"))
            last.then_inc(S["bd"], 1)
            dve.tensor_tensor(prod[:, :, :], iqs[0:ID, :, :, :].rearrange("p m q r -> p (m q) r"),
                              K.ikt[0:ID, SEQ:TOK].unsqueeze(1).broadcast_to([ID, IH, DEC]), ALU.mult).then_inc(S["wd"], 1)
            dve.wait_ge(S["w"], 4 + 2)
            step.link(dve.tensor_copy(wrow[:, :, :].rearrange("p r h -> p (r h)"), p_w[:, 0:DEC * IH]))
            dve.tensor_tensor(wsel[:, :, :, :].rearrange("p i q h -> p i (q h)"), wrow[:, :, :].rearrange("p (i q) h -> p i (q h)", q=2),
                              K.halves[:, 0:P:P // 16].unsqueeze(1).broadcast_to([P, PAIRS, 16]), ALU.mult)
            step.link(dve.scalar_tensor_tensor(out=rel[:, :, :], in0=p_n[:, 0:DEC * IH].rearrange("p (h r) -> p r h", h=IH), scalar=0.0,
                                               in1=wrow[:, :, :], op0=ALU.max, op1=ALU.mult))
            step.link(dve.tensor_reduce(snew[:, :], rel[:, :, :], AX.X, ALU.add))
            step.link(dve.tensor_tensor(snew[:, :].rearrange("p (i q) -> p i q", q=2), snew[:, :].rearrange("p (i q) -> p i q", q=2),
                                        K.half[:, :].unsqueeze(1).broadcast_to([P, PAIRS, 2]), ALU.mult))
            step.link(dve.tensor_reduce(sn[:, :], snew[:, :].rearrange("p (i q) -> p i q", q=2), AX.X, ALU.add))
            with dve.Fori(0, PAIRS // 2) as j:
                for i in range(2):
                    w = wsel[:, ds(j * 2 + i, 1), :, :].rearrange("p i q h -> p i (q h)").broadcast_to([P, 8, 2 * IH])
                    for t in range(UNITS // 2):
                        for b in range(2):
                            n = (j * 2 + i) * UNITS + t * 2 + b
                            dve.wait_ge(S["score"], 4 + n + 1)
                            dve.wait_ge(S["sum"], 4 + n - 1)
                            dve.scalar_tensor_tensor(out=part[b][:, :, :], in0=p_x[b][:, 0:128].rearrange("p (k w) -> p k w", k=8),
                                                     scalar=0.0, in1=w, op0=ALU.max, op1=ALU.mult).then_inc(S["mul"], 1)
                        for b in range(2):
                            n = (j * 2 + i) * UNITS + t * 2 + b
                            dve.wait_ge(S["mul"], 4 + n + 1)
                            dve.tensor_reduce(s[:, ds(j * 2 + i, 1), (t * 2 + b) * 8:(t * 2 + b + 1) * 8], part[b][:, :, :],
                                              AX.X, ALU.add).then_inc(S["sum"], 1)
            dve.wait_ge(S["sum"], 4 + PAIRS * UNITS)
            wide = [P, PAIRS, PAGE]

            def tally(level, m):
                dve.tensor_tensor(nhit[:, :], sn[:, :], level, ALU.is_ge)
                step.link(dve.tensor_tensor(hit[:, :, :], s[:, :, :], level.unsqueeze(2).broadcast_to(wide), ALU.is_ge))
                dve.tensor_reduce(row[:, :], hit[:, :, :], AX.X, ALU.add).then_inc(S["rowcount"], 1)
                dve.wait_ge(S["total"], 4 + m + 1)
                step.link(dve.tensor_tensor(count[:, :], p_c[:, 0:PAIRS], nhit[:, :], ALU.add))
            step.link(dve.memset(trial[:, :].bitcast(F32), 0.0))
            tally(trial[:, :].bitcast(F32), 0)
            step.link(dve.tensor_scalar(miss[:, :], count[:, :], float(NSEL), None, ALU.is_lt))
            step.link(dve.tensor_scalar(trial[:, :], miss[:, :], 31, 31, ALU.logical_shift_left, ALU.arith_shift_right))
            step.link(dve.tensor_scalar(trial[:, :], trial[:, :], 1 << 30, None, ALU.bitwise_xor))
            for bit in range(30, -1, -1):
                if bit:
                    dve.tensor_scalar(other[:, :], trial[:, :], 1 << (bit - 1), None, ALU.bitwise_xor)
                else:
                    dve.tensor_copy(other[:, :], trial[:, :])
                tally(trial[:, :].bitcast(F32), 31 - bit)
                step.link(dve.tensor_scalar(miss[:, :], count[:, :], float(NSEL), None, ALU.is_lt))
                step.link(dve.scalar_tensor_tensor(out=trial[:, :], in0=miss[:, :], scalar=bit, in1=other[:, :],
                                                   op0=ALU.logical_shift_left, op1=ALU.bitwise_xor))
            level = trial[:, :].bitcast(F32)
            dve.tensor_tensor(nhit[:, :], sn[:, :], level, ALU.is_gt)
            dve.tensor_tensor(newtie[:, :], sn[:, :], level, ALU.is_equal)
            dve.tensor_tensor(tie[:, :, :], s[:, :, :], level.unsqueeze(2).broadcast_to(wide), ALU.is_equal)
            step.link(dve.tensor_tensor(hit[:, :, :], s[:, :, :], level.unsqueeze(2).broadcast_to(wide), ALU.is_gt))
            dve.tensor_reduce(row[:, :], hit[:, :, :], AX.X, ALU.add).then_inc(S["rowcount"], 1)
            dve.tensor_reduce(tierow[:, :], tie[:, :, :], AX.X, ALU.add)
            for i in range(PAIRS):
                last = dve.tensor_tensor_scan(order[:, i, :], tie[:, i, :], tie[:, i, :], 0.0, ALU.add, ALU.bypass)
            dve.wait_ge(S["total"], 4 + 33)
            step.link(dve.tensor_tensor(count[:, :], p_c[:, 0:PAIRS], nhit[:, :], ALU.add))
            last = dve.tensor_scalar(need[:, :], count[:, :], -1.0, float(NSEL), ALU.mult, ALU.add)
            last.then_inc(S["rowcount"], 1)
            dve.wait_ge(S["rowcount"], 4 + 34)
            dve.wait_ge(S["total"], 4 + 34)
            step.link(dve.tensor_tensor(row[:, :], need[:, :], p_c[:, 0:PAIRS], ALU.subtract))
            step.link(dve.tensor_tensor(order[:, :, :], order[:, :, :], row[:, :].unsqueeze(2).broadcast_to(wide), ALU.is_le))
            step.link(dve.tensor_tensor(order[:, :, :], order[:, :, :], tie[:, :, :], ALU.mult))
            step.link(dve.tensor_tensor(K.taken[:, :, :], order[:, :, :], hit[:, :, :], ALU.add))
            step.link(dve.tensor_tensor(count[:, :], p_c[:, PAIRS:2 * PAIRS], need[:, :], ALU.is_lt))
            step.link(dve.tensor_tensor(count[:, :], count[:, :], newtie[:, :], ALU.mult))
            step.link(dve.tensor_tensor(K.new_taken[:, :], count[:, :], nhit[:, :], ALU.add))


def step_attend(nc, K, cache_k, cache_v, page_table, q_norm):
    KEYS, UNITS = 16, PAGE // 16
    with phase(nc, "satt") as (c, stack):
        pid = c.sb("pid", [P, PAIRS], I32)
        idx = c.sb("idx", [P, PAIRS, UNITS], I32)
        kp = [c.sb(f"k{b}", [P, KEYS, KVH * HD]) for b in range(2)]
        vp = [c.sb(f"v{b}", [P, KEYS, KVH * HD]) for b in range(2)]
        kt = [c.sb(f"kt{b}", [P, 4, P]) for b in range(2)]
        q, qsq, gain = c.sb("q", [P, QH, DEC]), c.sb("qsq", [P, QH, DEC]), c.sb("gain", [P, 1])
        inv = c.sb("inv", [P, QH, DEC])
        qs = c.sb("qs", [P, PAIRS, KVH, 2, GROUP])
        nprod, ln = c.sb("nprod", [P, PAIRS, HEADCOLS]), c.sb("ln", [P, PAIRS, HEADCOLS])
        edge, own_bias = c.sb("edge", [1, P]), c.sb("own_bias", [P, QH])
        away, nmask = c.sb("away", [P, 2]), c.sb("nmask", [P, PAIRS, 2])
        bias = c.sb("bias", [P, PAGE, HEADCOLS])
        lg = c.sb("lg", [P, PAIRS, PAGE, HEADCOLS])
        top, mx, tot = (c.sb(n, [P, PAIRS, HEADCOLS]) for n in "top mx tot".split())
        tall, dgm = c.sb("tall", [PAIRS * HEADCOLS, 1]), c.sb("dgm", [PAIRS * HEADCOLS, PAIRS * HEADCOLS])
        vnew = c.sb("vnew", [P, KVH, DEC])
        acc, out = c.sb("acc", [P, PAIRS, HEADCOLS]), c.sb("out", [P, QH, DEC])
        NC = PAIRS * HEADCOLS
        p_t = [c.ps(f"t{b}", [P, 4, P]) for b in range(2)]
        p_l = [c.ps(f"l{b}", [P, 512]) for b in range(2)]
        p_o = [c.ps(f"o{b}", [P, 512]) for b in range(2)]
        p_a, p_b = c.ps("a", [P, 512]), c.ps("b", [P, 512])
        S = {n: c.sem(n) for n in ("pid q sq ss gainq step idx edge bias newp newl turn copy used lgc maxed mturn diag "
                                   "mxb sub exp pv pvc sums tot out st").split()}
        s_k, s_v = c.own_sems("k"), c.own_sems("v")
        block = open_block(nc, stack, c)
        ks = cache_k.rearrange("l n (u k) g d -> (l n u) (k g d)", k=KEYS)
        vs = cache_v.rearrange("l n (u k) g d -> (l n u) (k g d)", k=KEYS)

        @block.sync
        def _(sp):
            credit(sp, c)
            table = page_table.rearrange("(i q) c -> q c i", q=2)
            for req in range(2):
                sp.dma_start(pid[req * NPAGE:(req + 1) * NPAGE, :], table[req], allow_slow_non_contiguous=True)\
                  .then_inc(S["pid"], 16)
            sp.dma_start(q[:, :, :], K.d_q[:, :, SEQ:TOK].rearrange("m p r -> p m r")).then_inc(S["q"], 16)
            sp.dma_start(gain[:, :], q_norm.rearrange("(p o) -> p o", o=1)).then_inc(S["q"], 16)
            sp.wait_ge(S["out"], 4 + 1)
            sp.dma_start(K.d_mix[GH:, :, SEQ:TOK].rearrange("m p r -> p m r"), out[:, :, :]).then_inc(S["st"], 16)
            sp.wait_ge(S["st"], 4 + 16)

        @block.gpsimd
        def _(pool):
            pool.wait_ge(S["idx"], 4 + 1)
            for src, buf, sem, done in ((ks, kp, s_k, "lgc"), (vs, vp, s_v, "pv")):
                for n in range(PAIRS * UNITS):
                    if n >= 2:
                        pool.wait_ge(S[done], 4 + n - 1)
                    pool.indirect_dma_start(buf[n % 2][:, :, :].rearrange("p k n -> p (k n)"), None, src,
                                            bass.IndirectOffsetOnAxis(ap=idx[:, n // UNITS, n % UNITS:n % UNITS + 1].bitcast(U32), axis=0))\
                        .then_inc(sem[n % 2], 16)

        @block.tensor
        def _(pe):
            pe.wait_ge(S["sq"], 4 + 1)
            pe.matmul(p_a[:, 0:NC], K.ones[:, :], qsq[:, :, :].rearrange("p h r -> p (h r)"), start=True, stop=True)\
              .then_inc(S["ss"], 1)
            pe.wait_ge(S["edge"], 4 + 1)
            pe.matmul(p_b[:, :], edge[:, :], K.near[0:1, :, 0:P], start=True, stop=True).then_inc(S["bias"], 1)
            pe.wait_ge(S["newp"], 4 + 1)
            pe.matmul(p_a[:, 0:NC], K.ones[:, :], nprod[:, :, :].rearrange("p i c -> p (i c)"), start=True, stop=True)
            pe.matmul(p_a[:, NC:NC + DEC], K.ones[:, :], nmask[:, :, :].rearrange("p i q -> p (i q)"), start=True, stop=True)
            for g in range(KVH):
                last = pe.transpose(p_a[:, 128 + g * 128:256 + g * 128], K.v[:, NT, g * HD:(g + 1) * HD], K.ident[:, :])
            last.then_inc(S["newl"], 1)
            for i in range(PAIRS):
                with pe.Fori(0, UNITS // 2) as t:
                    for b in range(2):
                        n = t * 2 + (i * UNITS + b)
                        pe.wait_ge(s_k[b], t * 16 + (i * (UNITS // 2) * 16 + 16))

                        def turn(u):
                            pe.wait_ge(S["copy"], 4 + n * 8 + u - 1)
                            for k in range(2):
                                for g in range(KVH):
                                    last = pe.transpose(p_t[u % 2][:, k * 2 + g, :], kp[b][:, u * 2 + k, g * HD:(g + 1) * HD],
                                                        K.ident[:, :])
                            last.then_inc(S["turn"], 1)
                        pe.wait_ge(S["lgc"], 4 + n - 1)
                        turn(0)
                        for u in range(8):
                            if u + 1 < 8:
                                turn(u + 1)
                            pe.wait_ge(S["copy"], 4 + n * 8 + u + 1)
                            for k in range(2):
                                for g in range(KVH):
                                    col = (u * 2 + k) * HEADCOLS + g * 4
                                    last = pe.matmul(p_l[b][:, col:col + 4], kt[u % 2][:, k * 2 + g, :],
                                                     qs[:, i, g, :, :].rearrange("p q h -> p (q h)"), start=True, stop=True)
                            last.then_inc(S["used"], 1)
            pe.wait_ge(S["maxed"], 4 + 1)
            pe.transpose(p_a[0:NC, 0:P], top[:, :, :].rearrange("p i c -> p (i c)"), K.ident[:, :]).then_inc(S["mturn"], 1)
            pe.wait_ge(S["diag"], 4 + 1)
            pe.matmul(p_b[:, 0:NC], K.ones[0:NC, :], dgm[:, :], start=True, stop=True).then_inc(S["mxb"], 1)
            pe.wait_ge(S["sums"], 4 + 1)
            pe.matmul(p_a[:, 0:NC], K.ones[:, :], tot[:, :, :].rearrange("p i c -> p (i c)"), start=True, stop=True)\
              .then_inc(S["tot"], 1)
            for i in range(PAIRS):
                with pe.Fori(0, UNITS // 2) as t:
                    for b in range(2):
                        n = t * 2 + (i * UNITS + b)
                        pe.wait_ge(s_v[b], t * 16 + (i * (UNITS // 2) * 16 + 16))
                        pe.wait_ge(S["pvc"], 4 + n - 1)
                        for g in range(KVH):
                            for k in range(KEYS):
                                last = pe.matmul(p_o[b][:, g * 4:(g + 1) * 4], vp[b][:, k, g * HD:(g + 1) * HD],
                                                 lg[:, i, ds(t * 32 + b * KEYS + k, 1), g * 4:(g + 1) * 4],
                                                 start=(k == 0), stop=(k == KEYS - 1))
                        last.then_inc(S["pv"], 1)

        @block.scalar
        def _(act):
            act.wait_ge(S["q"], 4 + 32)
            act.activation(qsq[:, :, :], q[:, :, :], ACT.Square).then_inc(S["sq"], 1)
            act.wait_ge(S["gainq"], 4 + 1)
            act.activation(inv[:, :, :], inv[:, :, :], ACT.Sqrt).then_inc(S["gainq"], 1)
            for i in range(PAIRS):
                with act.Fori(0, UNITS // 2) as t:
                    for b in range(2):
                        for u in range(8):
                            n = t * 16 + (i * UNITS * 8 + b * 8 + u)
                            act.wait_ge(S["turn"], 4 + n + 1)
                            act.wait_ge(S["used"], 4 + n - 1)
                            act.activation(kt[u % 2][:, :, :], p_t[u % 2][:, :, :], ACT.Copy).then_inc(S["copy"], 1)
            act.wait_ge(S["sub"], 4 + 1)
            act.activation(lg[:, :, :, :], lg[:, :, :, :], ACT.Exp)
            act.activation(ln[:, :, :], ln[:, :, :], ACT.Exp).then_inc(S["exp"], 1)

        @block.vector
        def _(dve):
            step = Steps(dve, S["step"])
            dve.wait_ge(S["pid"], 4 + 32)
            step.link(dve.tensor_scalar(pid[:, :], pid[:, :], 3, None, ALU.logical_shift_left))
            for u in range(UNITS):
                last = dve.tensor_scalar(idx[:, :, u], pid[:, :], u, None, ALU.bitwise_or)
            last.then_inc(S["idx"], 1)
            dve.tensor_tensor(own_bias[:, :], K.rb[:, 0, :], K.rb[:, BUCKETS - 1, :], ALU.subtract)
            step.link(dve.memset(edge[:, :], 0.0))
            dve.memset(edge[:, NPAGE - 1:P:NPAGE], 1.0).then_inc(S["edge"], 1)
            dve.wait_ge(S["ss"], 4 + 1)
            flat = inv[:, :, :].rearrange("p h r -> p (h r)")
            step.link(dve.tensor_scalar(flat, p_a[:, 0:NC], 1.0 / HD, EPS, ALU.mult, ALU.add))
            dve.reciprocal(flat, flat).then_inc(S["gainq"], 1)
            dve.wait_ge(S["gainq"], 4 + 2)
            step.link(dve.scalar_tensor_tensor(out=q[:, :, :], in0=q[:, :, :], scalar=gain[:, 0:1], in1=inv[:, :, :],
                                               op0=ALU.mult, op1=ALU.mult))
            for g in range(KVH):
                for hh in range(GROUP):
                    last = dve.tensor_scalar(qs[:, :, g, :, hh], q[:, g * GROUP + hh, :].rearrange("p (i r) -> p i r", r=2),
                                             SCALE, None, ALU.mult)
            step.link(last)
            for g in range(KVH):
                for hh in range(GROUP):
                    dve.tensor_tensor(nprod[:, :, :].rearrange("p i (g r h) -> p i g r h", g=KVH, r=2)[:, :, g, :, hh], qs[:, :, g, :, hh],
                                      K.kt[:, g, SEQ:TOK].rearrange("p (i r) -> p i r", r=2), ALU.mult)
            dve.tensor_tensor(nmask[:, :, :], K.new_taken[:, :].unsqueeze(2).broadcast_to([P, PAIRS, 2]),
                              K.ident[:, 0:P:NPAGE].unsqueeze(1).broadcast_to([P, PAIRS, 2]), ALU.mult).then_inc(S["newp"], 1)
            step.link(dve.tensor_scalar(away[:, :], K.half[:, :], -1.0, -NEG, ALU.add, ALU.mult))
            dve.wait_ge(S["bias"], 4 + 1)
            for g in range(KVH):
                for hh in range(GROUP):
                    h = g * GROUP + hh
                    for r in range(2):
                        last = dve.tensor_scalar(bias[:, :, g * 4 + r * 2 + hh], p_b[:, h * P:(h + 1) * P], away[:, r:r + 1],
                                                 None, ALU.add)
            step.link(last)
            dve.wait_ge(S["newl"], 4 + 1)
            cols = ln[:, :, :].rearrange("p i (g r h) -> p i g r h", g=KVH, r=2)
            step.link(dve.tensor_scalar(nmask[:, :, :].rearrange("p i q -> p (i q)"), p_a[:, NC:NC + DEC], -1.0, -NEG, ALU.add, ALU.mult))
            new = p_a[:, 0:NC].rearrange("p (i g r h) -> p i g r h", g=KVH, r=2, h=GROUP)
            for g in range(KVH):
                for hh in range(GROUP):
                    h = g * GROUP + hh
                    last = dve.scalar_tensor_tensor(out=cols[:, :, g, :, hh], in0=new[:, :, g, :, hh], scalar=own_bias[:, h:h + 1],
                                                    in1=nmask[:, :, :], op0=ALU.add, op1=ALU.add)
            dve.tensor_copy(vnew[:, :, :], p_a[:, P:3 * P].rearrange("p (g n) -> p g n", g=KVH)[:, :, 0:DEC])
            step.link(last)
            for i in range(PAIRS):
                with dve.Fori(0, UNITS // 2) as t:
                    for b in range(2):
                        n = t * 2 + (i * UNITS + b)
                        dve.wait_ge(S["used"], 4 + n * 8 + 8)
                        at = ds(t * 32 + b * KEYS, KEYS)
                        dve.tensor_tensor(lg[:, i, at, :], p_l[b][:, 0:KEYS * HEADCOLS].rearrange("p (k c) -> p k c", k=KEYS),
                                          bias[:, at, :], ALU.add).then_inc(S["lgc"], 1)
            dve.wait_ge(S["lgc"], 4 + PAIRS * UNITS)
            taken = K.taken[:, :, :].rearrange("p i k -> p (i k)")
            step.link(dve.tensor_scalar(taken, taken, -1.0, -NEG, ALU.add, ALU.mult))
            rows = lg[:, :, :, :].rearrange("p i k c -> p (i k) c")
            step.link(dve.tensor_tensor(rows, rows, taken.unsqueeze(2).broadcast_to([P, PAIRS * PAGE, HEADCOLS]), ALU.add))
            step.link(dve.tensor_reduce(top[:, :, :], lg[:, :, :, :].rearrange("p i k c -> p i c k"), AX.X, ALU.max))
            dve.tensor_tensor(top[:, :, :], top[:, :, :], ln[:, :, :], ALU.max).then_inc(S["maxed"], 1)
            dve.wait_ge(S["mturn"], 4 + 1)
            step.link(dve.tensor_reduce(tall[:, :], p_a[0:NC, 0:P], AX.X, ALU.max))
            dve.tensor_scalar(dgm[:, :], K.ident[0:NC, 0:NC], tall[:, 0:1], None, ALU.mult).then_inc(S["diag"], 1)
            dve.wait_ge(S["mxb"], 4 + 1)
            step.link(dve.tensor_copy(mx[:, :, :].rearrange("p i c -> p (i c)"), p_b[:, 0:NC]))
            dve.tensor_tensor(ln[:, :, :], ln[:, :, :], mx[:, :, :], ALU.subtract)
            for i in range(PAIRS):
                last = dve.tensor_tensor(lg[:, i, :, :], lg[:, i, :, :], mx[:, i, :].unsqueeze(1).broadcast_to([P, PAGE, HEADCOLS]),
                                         ALU.subtract)
            last.then_inc(S["sub"], 1)
            dve.wait_ge(S["exp"], 4 + 1)
            dve.tensor_reduce(tot[:, :, :], lg[:, :, :, :].rearrange("p i k c -> p i c k"), AX.X, ALU.add).then_inc(S["sums"], 1)
            own = acc[:, :, :].rearrange("p i (g r h) -> p i g r h", g=KVH, r=2)
            for g in range(KVH):
                for hh in range(GROUP):
                    last = dve.tensor_tensor(own[:, :, g, :, hh], cols[:, :, g, :, hh], vnew[:, g, :].rearrange("p (i r) -> p i r", r=2), ALU.mult)
            step.link(last)
            for i in range(PAIRS):
                with dve.Fori(0, UNITS // 2) as t:
                    for b in range(2):
                        n = t * 2 + (i * UNITS + b)
                        dve.wait_ge(S["pv"], 4 + n + 1)
                        dve.wait_ge(S["pvc"], 4 + n)
                        dve.tensor_tensor(acc[:, i, :], acc[:, i, :], p_o[b][:, 0:HEADCOLS], ALU.add).then_inc(S["pvc"], 1)
            dve.wait_ge(S["pvc"], 4 + PAIRS * UNITS)
            dve.wait_ge(S["tot"], 4 + 1)
            step.link(dve.tensor_tensor(tot[:, :, :].rearrange("p i c -> p (i c)"), p_a[:, 0:NC], ln[:, :, :].rearrange("p i c -> p (i c)"), ALU.add))
            step.link(dve.reciprocal(tot[:, :, :], tot[:, :, :]))
            share = tot[:, :, :].rearrange("p i (g r h) -> p i g r h", g=KVH, r=2)
            for g in range(KVH):
                for hh in range(GROUP):
                    last = dve.tensor_tensor(out[:, g * GROUP + hh, :].rearrange("p (i r) -> p i r", r=2), own[:, :, g, :, hh],
                                             share[:, :, g, :, hh], ALU.mult)
            last.then_inc(S["out"], 1)


def mix(nc, K, x_prompt, x_sample, w_out, norm_ffn):
    with phase(nc, "mix") as (c, stack):
        two = lambda name, shape, dt=F32: [c.sb(f"{name}{b}", shape, dt) for b in range(2)]
        w = c.sb("w", [P, KD, D])
        m, x, xn = two("m", [P, KD, P]), two("x", [P, D]), two("xn", [P, D])
        junk = c.sb("junk", [P, D])
        stat = two("stat", [P, 4])
        gain = c.sb("gain", [P, KD])
        p_y = [c.ps(f"y{b}", [P, 2, 512]) for b in range(2)]
        p_t = [c.ps(f"t{b}", [P, KD, P]) for b in range(2)]
        s_w = c.sem("w")
        s_m, s_x, s_mm, s_x2, s_sum, s_mean, s_root, s_inv, s_norm, s_turn, s_ht, s_st = (
            c.sems(n) for n in "m x mm x2 sum mean root inv norm turn ht st".split())
        block = open_block(nc, stack, c)
        LAST = NT // 2

        @block.sync
        def _(sp):
            credit(sp, c)
            sp.dma_start(gain[:, :], norm_ffn.rearrange("(k p) -> p k", p=P), allow_slow_non_contiguous=True)\
              .then_inc(s_w, 16)

            def load(j, b, n=P):
                rows = ds(j * 256 + b * P, P) if n == P else slice(SEQ, TOK)
                sp.wait_ge(s_mm[b], 4 + j)
                sp.dma_start(m[b][:, :, 0:n], K.d_mix[:, :, rows].rearrange("k p n -> p k n")).then_inc(s_m[b], 16)
                sp.wait_ge(s_norm[b], 4 + j)
                sp.wait_ge(s_st[b], 4 + j * 16)
                sp.dma_start(x[b][0:n, :], x_prompt[rows, :] if n == P else x_sample).then_inc(s_x[b], 16)

            def store(j, b, n=P):
                rows = ds(j * 256 + b * P, P) if n == P else slice(SEQ, TOK)
                sp.wait_ge(s_x2[b], 4 + j + 1)
                sp.dma_start(K.d_x2[rows, :], x[b][0:n, :]).then_inc(s_st[b], 16)
            load(0, 0)
            load(0, 1)
            with sp.Fori(0, LAST - 1) as j:
                for b in range(2):
                    store(j, b)
                    load(j + 1, b)
            store(LAST - 1, 0)
            load(LAST, 0, DEC)
            store(LAST - 1, 1)
            store(LAST, 0, DEC)
            sp.wait_ge(s_st[0], 4 + (LAST + 1) * 16)
            sp.wait_ge(s_st[1], 4 + LAST * 16)

        @block.tensor
        def _(pe):
            def multiply(j, b):
                pe.wait_ge(s_m[b], 4 + j * 16 + 16)
                pe.wait_ge(s_x2[b], 4 + j)
                for k in range(KD):
                    for half in range(2):
                        last = pe.matmul(p_y[b][:, half, :], m[b][:, k, :], w[:, k, half * 512:(half + 1) * 512],
                                         start=(k == 0), stop=(k == KD - 1))
                last.then_inc(s_mm[b], 1)

            def turn(j, b):
                pe.wait_ge(s_norm[b], 4 + j + 1)
                pe.wait_ge(s_ht[b], 4 + j)
                for k in range(KD):
                    last = pe.transpose(p_t[b][:, k, :], xn[b][:, k * P:(k + 1) * P], K.ident[:, :])
                last.then_inc(s_turn[b], 1)
            pe.wait_ge(s_w, 4 + 32)
            multiply(0, 0)
            with pe.Fori(0, LAST) as j:
                multiply(j, 1)
                turn(j, 0)
                multiply(j + 1, 0)
                turn(j, 1)
            turn(LAST, 0)

        @block.scalar
        def _(act):
            act.dma_start(w[:, :, :], w_out.rearrange("(k p) n -> p k n", p=P)).then_inc(s_w, 16)

            def stats(j, b):
                act.wait_ge(s_x2[b], 4 + j + 1)
                act.activation(junk[:, :], x[b][:, :], ACT.Square, accum_out=stat[b][:, 0:1]).then_inc(s_sum[b], 1)
                act.wait_ge(s_mean[b], 4 + j + 1)
                act.activation(stat[b][:, 2:3], stat[b][:, 1:2], ACT.Sqrt).then_inc(s_root[b], 1)
            with act.Fori(0, LAST) as j:
                stats(j, 0)
                stats(j, 1)
            stats(LAST, 0)

        @block.vector
        def _(dve):
            dve.wait_ge(s_w, 4 + 32)

            def norm(j, b):
                dve.wait_ge(s_x[b], 4 + j * 16 + 16)
                dve.wait_ge(s_mm[b], 4 + j + 1)
                dve.tensor_tensor(x[b][:, :], p_y[b][:, :, :].rearrange("p a n -> p (a n)"), x[b][:, :], ALU.add)\
                   .then_inc(s_x2[b], 1)
                dve.wait_ge(s_sum[b], 4 + j + 1)
                dve.tensor_scalar(stat[b][:, 1:2], stat[b][:, 0:1], 1.0 / D, EPS, ALU.mult, ALU.add).then_inc(s_mean[b], 1)
                dve.wait_ge(s_root[b], 4 + j + 1)
                dve.reciprocal(stat[b][:, 3:4], stat[b][:, 2:3]).then_inc(s_inv[b], 1)
                dve.wait_ge(s_inv[b], 4 + j + 1)
                dve.wait_ge(s_turn[b], 4 + j)
                dve.tensor_scalar(xn[b][:, :], x[b][:, :], stat[b][:, 3:4], None, ALU.mult).then_inc(s_norm[b], 1)

            def scale(j, b):
                dve.wait_ge(s_turn[b], 4 + j + 1)
                dve.tensor_tensor(K.ht[:, :, ds(j * 256 + b * P, P)], p_t[b][:, :, :],
                                  gain[:, :].unsqueeze(2).broadcast_to([P, KD, P]), ALU.mult).then_inc(s_ht[b], 1)
            norm(0, 0)
            with dve.Fori(0, LAST) as j:
                norm(j, 1)
                scale(j, 0)
                norm(j + 1, 0)
                scale(j, 1)
            scale(LAST, 0)


def ffn_up(nc, K, w_up, conv_w, conv_b, conv_state, outs):
    PAST = DEC * 2
    with phase(nc, "up") as (c, stack):
        two = lambda name, shape, dt=F32: [c.sb(f"{name}{b}", shape, dt) for b in range(2)]
        w = two("w", [P, 2, KD, P])
        pre = [c.sb(f"pre{s}", [P, 2 + SEQ]) for s in range(2)]
        new = c.sb("new", [P, 2, 2 + DEC])
        acc = [c.sb(f"acc{s}", [P, TOK]) for s in range(2)]
        res = two("res", [P, TOK])
        past = two("past", [P, 2, P])
        rows = c.sb("rows", [2 * (2 + DEC), FF])
        slab = c.sb("slab", [P, 4, P])
        taps = c.sb("taps", [P, 4, 2, NF])
        p_g = [c.ps(f"g{g}", [P, 512]) for g in range(4)]
        p_s = c.ps("s", [P, 2, DEC])
        p_past = c.ps("past", [P, 2, P])
        p_rows = c.ps("rows", [2 * (2 + DEC), P])
        p_taps = c.ps("taps", [P, 4, P])
        S = {n: c.sem(n) for n in ("slab zero tturn taps mm smm used free sfree new hist back rows conv step silu res state").split()}
        s_w, s_past, s_st = c.sems("w"), c.sems("past"), c.sems("st")
        wv = w_up.rearrange("(k p) n -> p k n", p=P)
        block = open_block(nc, stack, c)

        @block.sync
        def _(sp):
            credit(sp, c)
            sp.wait_ge(S["zero"], 4 + 4)
            for i in range(3):
                sp.dma_start(slab[0:2 * NF, i, :], conv_w[i, :].rearrange("(m p) -> m p", p=P)).then_inc(S["slab"], 16)
            sp.dma_start(slab[0:2 * NF, 3, :], conv_b.rearrange("(m p) -> m p", p=P)).then_inc(S["slab"], 16)
            with sp.Fori(0, NF // 2) as j:
                for b in range(2):
                    sp.wait_ge(S["used"], 4 + (j * 2 + b) - 1)
                    sp.wait_ge(S["hist"], 4 + (j * 2 + b) - 1)
                    for s in range(2):
                        cols = ds(j * 256 + b * P + s * FF, P)
                        sp.dma_start(w[b][:, s, :, :], wv[:, :, cols]).then_inc(s_w[b], 16)
                        sp.dma_start(past[b][0:PAST, s, :], conv_state[:, cols]).then_inc(s_past[b], 16)
            sp.wait_ge(S["rows"], 4 + NF)
            for s in range(2):
                o, cols = s * (2 + DEC), slice(s * FF, (s + 1) * FF)
                sp.dma_start(outs["p_fconv"][:, cols], rows[o:o + 2, :]).then_inc(S["state"], 16)
                sp.dma_start(outs["s_fconv"][:, 1, cols], rows[o + 2:o + 2 + DEC, :]).then_inc(S["state"], 16)
            sp.dma_start(outs["s_fconv"][:, 0, :], conv_state.rearrange("(b j) n -> b j n", j=2)[:, 1, :])\
              .then_inc(S["state"], 16)
            sp.wait_ge(S["state"], 4 + 80)

        @block.tensor
        def _(pe):
            pe.wait_ge(S["slab"], 4 + 64)
            for i in range(4):
                last = pe.transpose(p_taps[:, i, :], slab[:, i, :], K.ident[:, :])
            last.then_inc(S["tturn"], 1)
            with pe.Fori(0, NF // 2) as j:
                for b in range(2):
                    n = j * 2 + b
                    pe.wait_ge(s_w[b], 4 + j * 32 + 32)
                    for s in range(2):
                        for g in range(GROUPS):
                            pe.wait_ge(S["free"], 4 + n * 8 + s * 4 + g - 3)
                            for k in range(KD):
                                last = pe.matmul(p_g[g][:, :], w[b][:, s, k, :], K.ht[:, k, g * 512:(g + 1) * 512],
                                                 start=(k == 0), stop=(k == KD - 1))
                            last.then_inc(S["mm"], 1)
                    pe.wait_ge(S["sfree"], 4 + n)
                    for s in range(2):
                        for k in range(KD):
                            last = pe.matmul(p_s[:, s, :], w[b][:, s, k, :], K.ht[:, k, SEQ:TOK],
                                             start=(k == 0), stop=(k == KD - 1))
                    last.then_inc(S["used"], 1)
                    pe.wait_ge(s_past[b], 4 + j * 32 + 32)
                    pe.wait_ge(S["conv"], 4 + n)
                    for s in range(2):
                        last = pe.transpose(p_past[:, s, :], past[b][:, s, :], K.ident[:, :])
                    last.then_inc(S["hist"], 1)
                    pe.wait_ge(S["new"], 4 + n + 1)
                    pe.wait_ge(S["rows"], 4 + n)
                    pe.transpose(p_rows[:, :], new[:, :, :].rearrange("p s r -> p (s r)"), K.ident[:, :]).then_inc(S["back"], 1)

        @block.scalar
        def _(act):
            act.wait_ge(S["zero"], 4 + 4)

            def copies(n):
                act.wait_ge(S["conv"], 4 + n)
                for s in range(2):
                    for g in range(GROUPS):
                        act.wait_ge(S["mm"], 4 + n * 8 + s * 4 + g + 1)
                        act.activation(pre[s][:, 2 + g * 512:2 + (g + 1) * 512], p_g[g][:, :], ACT.Copy).then_inc(S["free"], 1)
                act.wait_ge(S["used"], 4 + n + 1)
                act.wait_ge(S["back"], 4 + n)
                act.activation(new[:, :, 2:], p_s[:, :, :], ACT.Copy).then_inc(S["sfree"], 1)
                act.wait_ge(S["free"], 4 + n * 8 + 8)
                act.activation(new[:, 0, 0:2], pre[0][:, SEQ:], ACT.Copy)
                act.activation(new[:, 1, 0:2], pre[1][:, SEQ:], ACT.Copy).then_inc(S["new"], 1)

            def finish(n, b, j):
                act.wait_ge(S["conv"], 4 + n + 1)
                act.activation(acc[0][:, :], acc[0][:, :], ACT.Silu).then_inc(S["silu"], 1)
                act.wait_ge(S["back"], 4 + n + 1)
                act.activation(rows[:, ds(n * P, P)], p_rows[:, :], ACT.Copy).then_inc(S["rows"], 1)
                act.wait_ge(S["res"], 4 + n + 1)
                act.dma_start(K.d_act[ds(n, 1), :, :].rearrange("o p n -> (o p) n"), res[b][:, :]).then_inc(s_st[b], 16)
            with act.Fori(0, NF // 2) as j:
                for b in range(2):
                    copies(j * 2 + b)
                    finish(j * 2 + b, b, j)
            for b in range(2):
                act.wait_ge(s_st[b], 4 + NF // 2 * 16)

        @block.vector
        def _(dve):
            for s in range(2):
                dve.memset(pre[s][:, 0:2], 0.0)
            dve.memset(slab[:, :, :], 0.0).then_inc(S["zero"], 2)
            for b in range(2):
                dve.memset(past[b][:, :, :], 0.0).then_inc(S["zero"], 1)
            dve.wait_ge(S["tturn"], 4 + 1)
            dve.tensor_copy(taps[:, :, :, :].rearrange("p i s m -> p i (s m)"), p_taps[:, :, 0:2 * NF]).then_inc(S["taps"], 1)
            dve.wait_ge(S["taps"], 4 + 1)
            step = Steps(dve, S["step"])
            with dve.Fori(0, NF // 2) as j:
                step.enter(j, 4, NF // 2)
                for b in range(2):
                    n = j * 2 + b
                    tap = [[taps[:, i, s, ds(n, 1)] for i in range(4)] for s in range(2)]
                    a = [acc[s][:, 0:SEQ] for s in range(2)]
                    t = [acc[s][:, SEQ:] for s in range(2)]
                    dve.wait_ge(S["new"], 4 + n + 1)
                    dve.wait_ge(S["hist"], 4 + n + 1)
                    dve.wait_ge(S["res"], 4 + n)
                    for s in range(2):
                        dve.tensor_scalar(a[s], pre[s][:, 0:SEQ], tap[s][0], tap[s][3], ALU.mult, ALU.add)
                        last = dve.tensor_scalar(t[s], p_past[:, s, 0:PAST:2], tap[s][0], tap[s][3], ALU.mult, ALU.add)
                    step.link(last)
                    for s in range(2):
                        dve.scalar_tensor_tensor(out=a[s], in0=pre[s][:, 1:SEQ + 1], scalar=tap[s][1], in1=a[s],
                                                 op0=ALU.mult, op1=ALU.add)
                        last = dve.scalar_tensor_tensor(out=t[s], in0=p_past[:, s, 1:PAST:2], scalar=tap[s][1], in1=t[s],
                                                        op0=ALU.mult, op1=ALU.add)
                    step.link(last)
                    for s in range(2):
                        dve.scalar_tensor_tensor(out=a[s], in0=pre[s][:, 2:], scalar=tap[s][2], in1=a[s],
                                                 op0=ALU.mult, op1=ALU.add)
                        last = dve.scalar_tensor_tensor(out=t[s], in0=new[:, s, 2:], scalar=tap[s][2], in1=t[s],
                                                        op0=ALU.mult, op1=ALU.add)
                    last.then_inc(S["conv"], 1)
                    dve.wait_ge(S["silu"], 4 + n + 1)
                    dve.wait_ge(s_st[b], 4 + j * 16)
                    dve.tensor_tensor(res[b][:, :], acc[0][:, :], acc[1][:, :], ALU.mult).then_inc(S["res"], 1)
                step.leave()


def ffn_down(nc, K, w_down, outs):
    with phase(nc, "down") as (c, stack):
        two = lambda name, shape, dt=F32: [c.sb(f"{name}{b}", shape, dt) for b in range(2)]
        w = c.sb("w", [P, NF, D])
        a, x = two("a", [P, NF, P]), two("x", [P, D])
        p_y = [c.ps(f"y{b}", [P, 2, 512]) for b in range(2)]
        s_w = c.sems("w", 2)
        s_a, s_x, s_mm, s_y, s_st = (c.sems(n) for n in "a x mm y st".split())
        block = open_block(nc, stack, c)
        LAST = NT // 2

        @block.sync
        def _(sp):
            credit(sp, c)

            def load(j, b, n=P):
                rows = ds(j * 256 + b * P, P) if n == P else slice(SEQ, TOK)
                sp.wait_ge(s_mm[b], 4 + j)
                sp.dma_start(a[b][:, :, 0:n], K.d_act[:, :, rows].rearrange("f p n -> p f n")).then_inc(s_a[b], 16)
                sp.wait_ge(s_st[b], 4 + j * 16)
                sp.dma_start(x[b][0:n, :], K.d_x2[rows, :]).then_inc(s_x[b], 16)

            def store(j, b, n=P):
                sp.wait_ge(s_y[b], 4 + j + 1)
                dst = outs["y_prompt"][ds(j * 256 + b * P, P), :] if n == P else outs["y_sample"]
                sp.dma_start(dst, x[b][0:n, :]).then_inc(s_st[b], 16)
            load(0, 0)
            load(0, 1)
            with sp.Fori(0, LAST - 1) as j:
                for b in range(2):
                    store(j, b)
                    load(j + 1, b)
            store(LAST - 1, 0)
            load(LAST, 0, DEC)
            store(LAST - 1, 1)
            store(LAST, 0, DEC)
            sp.wait_ge(s_st[0], 4 + (LAST + 1) * 16)
            sp.wait_ge(s_st[1], 4 + LAST * 16)

        @block.scalar
        def _(act):
            rows = w_down.rearrange("(f p) n -> p f n", p=P)
            half = NF // 2
            for i in range(2):
                act.dma_start(w[:, i * half:(i + 1) * half, :], rows[:, i * half:(i + 1) * half, :]).then_inc(s_w[i], 16)

        @block.tensor
        def _(pe):
            def multiply(j, b, m=P, first=False):
                pe.wait_ge(s_a[b], 4 + j * 16 + 16)
                pe.wait_ge(s_y[b], 4 + j)
                for f in range(NF):
                    if first and f % (NF // 2) == 0:
                        pe.wait_ge(s_w[f // (NF // 2)], 4 + 16)
                    for half in range(2):
                        last = pe.matmul(p_y[b][0:m, half, :], a[b][:, f, 0:m], w[:, f, half * 512:(half + 1) * 512],
                                         start=(f == 0), stop=(f == NF - 1))
                last.then_inc(s_mm[b], 1)
            multiply(0, 0, first=True)
            with pe.Fori(0, LAST) as j:
                multiply(j, 1)
                multiply(j + 1, 0)

        @block.vector
        def _(dve):
            def add(j, b):
                dve.wait_ge(s_x[b], 4 + j * 16 + 16)
                dve.wait_ge(s_mm[b], 4 + j + 1)
                dve.tensor_tensor(x[b][:, :], p_y[b][:, :, :].rearrange("p a n -> p (a n)"), x[b][:, :], ALU.add)\
                   .then_inc(s_y[b], 1)
            with dve.Fori(0, LAST) as j:
                add(j, 0)
                add(j, 1)
            add(LAST, 0)


def build(nc, ins, outs):
    K = Held()

    def scratch(name, shape):
        return nc.dram_tensor(f"scratch_{name}", shape, F32, kind="Internal").ap()
    K.d_qkv = scratch("qkv", (CONVW, P, TOK))
    K.d_z = scratch("z", (GH, P, TOK))
    K.d_q = scratch("q", (QH, P, TOK))
    K.d_iq = scratch("iq", (IH // 2, P, TOK))
    K.d_mix = scratch("mix", (KD, P, TOK))
    K.d_x2 = scratch("x2", (TOK, D))
    K.d_act = scratch("act", (NF, P, TOK))
    with ExitStack() as held:
        def keep(name, shape, dt=F32, stack=held):
            return stack.enter_context(nc.sbuf_tensor(name, shape, dt))
        K.ident, K.ones = keep("ident", [P, P]), keep("ones", [P, P])
        K.upto, K.before, K.after = keep("upto", [P, P]), keep("before", [P, P]), keep("after", [P, P])
        K.below = keep("below", [P, 896])
        K.rb = keep("rb", [P, BUCKETS, QH])
        K.near = keep("near", [P, QH, 256])
        constants(nc, K, ins["rel_bias"])
        with ExitStack() as mixer:
            K.knew = keep("knew", [P, KVH * HD], F32, mixer)
            K.v = keep("v", [P, TILES, KVH * HD], F32, mixer)
            K.small = keep("small", [P, TILES, SMALL], F32, mixer)
            K.kt = keep("kt", [P, KVH, COLS], F32, mixer)
            K.ikt = keep("ikt", [P, COLS], F32, mixer)
            with ExitStack() as hidden:
                K.ht = keep("ht", [P, KD, COLS], F32, hidden)
                K.k = keep("k", [P, TILES, KVH * HD], F32, hidden)
                w_in = ins["w_in"].rearrange("l k n -> (l k) n")
                project(nc, K, ins["x_prompt"].rearrange("b t d -> (b t) d"), ins["x_sample"].rearrange("b t d -> (b t) d"),
                        ins["norm_mix"].rearrange("l d -> (l d)"), w_in)
                keys(nc, K, ins["k_norm"].rearrange("l d -> (l d)"), outs)
                channels(nc, K, w_in, ins["gdn_conv_w"].rearrange("l j n -> (l j) n"),
                         ins["state_gdn_conv"].rearrange("l b j n -> (l b j) n"), None, outs)
            with ExitStack() as rule:
                per_token = lambda name: keep(name, [P, TILES, GH], F32, rule)
                K.g, K.beta, K.decay_sum = per_token("g"), per_token("beta"), per_token("gc")
                K.kdec, K.bexp, K.glast = per_token("kdec"), per_token("bexp"), per_token("glast")
                K.join, K.join_t = keep("join", [P, LEVELS, P], F32, rule), keep("join_t", [P, LEVELS, P], F32, rule)
                K.state = keep("state", [P, GH, HD], F32, rule)
                gates(nc, K, ins["gdn_a_log"], ins["gdn_dt_bias"])
                delta(nc, K, ins["gdn_out_norm"].rearrange("l d -> (l d)"), outs)
                delta_step(nc, K, ins["state_gdn"].rearrange("l b h k v -> (l b) h k v"),
                           ins["gdn_out_norm"].rearrange("l d -> (l d)"), dict(outs, s_gdn=outs["s_gdn"].rearrange("(b h) k v -> b h k v", h=GH)))
            with ExitStack() as step:
                K.taken, K.new_taken = keep("taken", [P, PAIRS, PAGE], F32, step), keep("new_taken", [P, PAIRS], F32, step)
                K.half, K.halves = keep("half", [P, 2], F32, step), keep("halves", [P, P], F32, step)
                step_select(nc, K, ins["cache_idx_k"].rearrange("l n p d -> (l n) p d"), ins["page_table"])
                step_attend(nc, K, ins["cache_k"], ins["cache_v"], ins["page_table"], ins["q_norm"].rearrange("l d -> (l d)"))
            attend(nc, K, ins["q_norm"].rearrange("l d -> (l d)"), outs)
        with ExitStack() as hidden:
            K.ht = keep("ht2", [P, KD, COLS], F32, hidden)
            mix(nc, K, ins["x_prompt"].rearrange("b t d -> (b t) d"), ins["x_sample"].rearrange("b t d -> (b t) d"),
                ins["w_out"].rearrange("l k n -> (l k) n"), ins["norm_ffn"].rearrange("l d -> (l d)"))
            ffn_up(nc, K, ins["w_up"].rearrange("l k n -> (l k) n"), ins["ffn_conv_w"].rearrange("l j n -> (l j) n"),
                   ins["ffn_conv_b"].rearrange("l n -> (l n)"), ins["state_ffn_conv"].rearrange("l b j n -> (l b j) n"), outs)
        ffn_down(nc, K, ins["w_down"].rearrange("l f n -> (l f) n"), outs)


class Held:
    pass


_OUTS = [("y_prompt", (1, SEQ, D)), ("y_sample", (DEC, 1, D)),
         ("p_k", (1, 1, SEQ, KVH, HD)), ("p_v", (1, 1, SEQ, KVH, HD)), ("p_idx", (1, 1, SEQ, ID)),
         ("p_gdn", (1, 1, GH, HD, HD)), ("p_gconv", (1, 1, 3, CONV_CH)), ("p_fconv", (1, 1, 2, 2 * FF)),
         ("s_k", (1, DEC, 1, KVH, HD)), ("s_v", (1, DEC, 1, KVH, HD)), ("s_idx", (1, DEC, 1, ID)),
         ("s_gdn", (1, DEC, GH, HD, HD)), ("s_gconv", (1, DEC, 3, CONV_CH)), ("s_fconv", (1, DEC, 2, 2 * FF))]
_FLAT = {"y_prompt": "a t d -> (a t) d", "y_sample": "b t d -> (b t) d",
         "p_k": "l b t g d -> (l b t) (g d)", "p_v": "l b t g d -> (l b t) (g d)", "p_idx": "l b t d -> (l b t) d",
         "p_gdn": "l b h k v -> (l b h) k v", "p_gconv": "l b j n -> (l b j) n", "p_fconv": "l b j n -> (l b j) n",
         "s_k": "l b t g d -> (l b t) (g d)", "s_v": "l b t g d -> (l b t) (g d)", "s_idx": "l b t d -> (l b t) d",
         "s_gdn": "l b h k v -> (l b h) k v", "s_gconv": "l b j n -> (l b) j n", "s_fconv": "l b j n -> (l b) j n"}
_INS = ["x_prompt", "x_sample", "cache_k", "cache_v", "cache_idx_k", "state_gdn", "state_gdn_conv",
        "state_ffn_conv", "page_table", "rel_bias", "norm_mix", "w_in", "gdn_conv_w", "gdn_a_log", "gdn_dt_bias",
        "gdn_out_norm", "q_norm", "k_norm", "w_out", "norm_ffn", "w_up", "ffn_conv_w", "ffn_conv_b", "w_down"]


def kernel(**inputs):
    import concourse.bacc as bacc
    from concourse.bass_utils import run_bass_kernel_spmd

    nc = bacc.Bacc("TRN2", target_bir_lowering=False, num_devices=1)
    arrays, ins, outs = {}, {}, {}
    for name in _INS:
        a = np.ascontiguousarray(inputs[name])
        arrays[f"in_{name}"] = a
        ins[name] = nc.dram_tensor(f"in_{name}", a.shape, mybir.dt.from_np(a.dtype), kind="ExternalInput").ap()
    for name, shape in _OUTS:
        outs[name] = nc.dram_tensor(f"out_{name}", shape, F32, kind="ExternalOutput").ap().rearrange(_FLAT[name])
    build(nc, ins, outs)
    r = run_bass_kernel_spmd(nc, [arrays], core_ids=[0])
    return tuple(r.results[0][f"out_{name}"] for name, _ in _OUTS)
```

```python
from contextlib import ExitStack, contextmanager
import math

import numpy as np

import concourse.bass as bass
from concourse import mybir

F32 = mybir.dt.float32
F32R = mybir.dt.float32r
BF16 = mybir.dt.bfloat16
I32 = mybir.dt.int32
U32 = mybir.dt.uint32
ALU = mybir.AluOpType
ACT = mybir.ActivationFunctionType
AX = mybir.AxisListType
ds = bass.ds

P = 128
SEQ, DEC, D = 2048, 8, 1024
KD = D // P
NT = SEQ // P
TILES = NT + 1
COLS = TILES * P
TOK = SEQ + DEC
HD = 128
GH = 4
QH, KVH = 4, 2
GROUP = QH // KVH
IH, ID = 8, 64
CONV_CH = 3 * GH * HD
C_Z = CONV_CH
C_AB = C_Z + GH * HD
C_Q = C_AB + 2 * GH
C_K = C_Q + QH * HD
C_V = C_K + KVH * HD
C_IQ = C_V + KVH * HD
C_IK = C_IQ + IH * ID
C_IW = C_IK + ID
D_IN = C_IW + IH
SMALL = 2 * GH + ID + IH
GROUPS = SEQ // 512
FF = 2816
NF = FF // P
CONVW = CONV_CH // P
NSEL = 256
PAST, PAGE = 8192, 128
NPAGE = PAST // PAGE
KCOL = NPAGE + 1
NPOOL = DEC * NPAGE * 5 // 4
EPS = 1e-6
BIG = 3.4028234663852886e38
NEG = -1.0e30
INDEX_SCALE = (IH * ID) ** -0.5
SCALE = HD ** -0.5
BUCKETS = 32


def bucket_starts():
    n = np.arange(1, 256)
    half = BUCKETS // 2
    large = half + (np.log(np.maximum(n, 1).astype(np.float32) / np.float32(half)) / np.float32(math.log(128 / half))
                    * np.float32(BUCKETS - half)).astype(np.int32)
    bucket = np.where(n < half, n, np.minimum(large, BUCKETS - 1))
    return [0] + [int(n[np.argmax(bucket >= b)]) for b in range(1, BUCKETS)]


class Steps:

    def __init__(self, eng, sem):
        self.eng, self.sem, self.n, self.base, self.per = eng, sem, 0, 0, None
        self.total = 0

    def link(self, ins):
        self.n += 1
        ins.then_inc(self.sem, 1)
        self.eng.wait_ge(self.sem, 4 + self.base + self.n)

    def enter(self, i, per, count):
        self.start = self.total + self.n
        self.base, self.n, self.per, self.count = self.start + i * per, 0, per, count

    def leave(self):
        assert self.n == self.per, f"{self.n} steps in a turn, not {self.per}"
        self.total = self.base = self.start + self.per * self.count
        self.total, self.n = self.start + self.per * self.count, 0
        self.base = self.total


class Ctx:

    def __init__(self, nc, stack, name):
        self.nc, self.stack, self.name, self.all = nc, stack, name, []
        self.own = []

    def sb(self, name, shape, dt=F32):
        return self.stack.enter_context(self.nc.sbuf_tensor(f"{self.name}_{name}", shape, dt))

    def ps(self, name, shape, dt=F32):
        return self.stack.enter_context(self.nc.psum_tensor(f"{self.name}_p_{name}", shape, dt))

    def sem(self, name):
        s = self.stack.enter_context(self.nc.semaphore(f"{self.name}_{name}"))
        self.all.append(s)
        return s

    def own_sems(self, name, n=2):
        self.own += [self.stack.enter_context(self.nc.semaphore(f"{self.name}_{name}{i}")) for i in range(n)]
        return self.own[-n:]

    def sems(self, name, n=2):
        return [self.sem(f"{name}{i}") for i in range(n)]


@contextmanager
def phase(nc, name):
    with ExitStack() as stack:
        yield Ctx(nc, stack, name), stack


def credit(sp, c):
    for s in c.all:
        sp.sem_inc(s, 4)


def open_block(nc, stack, c):
    def clear():
        for s in c.all:
            nc.sync.sem_clear(s)
        for s in c.own:
            nc.gpsimd.sem_clear(s)
    stack.callback(clear)
    return stack.enter_context(nc.Block())


def constants(nc, K, rel_bias):
    with phase(nc, "const") as (c, stack):
        s_base = c.sem("base")
        s_load = c.sem("load")
        s_rel = c.sem("rel")
        block = open_block(nc, stack, c)

        @block.gpsimd
        def _(pool):
            pool.memset(K.ident[:, :], 0.0).then_inc(s_base, 1)
            pool.memset(K.ones[:, :], 1.0).then_inc(s_base, 1)
            pool.memset(K.below[:, :], BIG).then_inc(s_base, 1)
            pool.wait_ge(s_base, 4 + 3)
            pool.affine_select(out=K.ident[:, :], in_=K.ident[:, :], compare_op=ALU.not_equal, fill=1.0,
                               base=0, pattern=[[-1, P]], channel_multiplier=1)
            pool.affine_select(out=K.upto[:, :], in_=K.ones[:, :], compare_op=ALU.is_ge, fill=0.0,
                               base=0, pattern=[[1, P]], channel_multiplier=-1)
            pool.affine_select(out=K.before[:, :], in_=K.ones[:, :], compare_op=ALU.is_gt, fill=0.0,
                               base=0, pattern=[[1, P]], channel_multiplier=-1)
            pool.affine_select(out=K.after[:, :], in_=K.ones[:, :], compare_op=ALU.is_gt, fill=0.0,
                               base=0, pattern=[[-1, P]], channel_multiplier=1)
            pool.affine_select(out=K.below[:, :], in_=K.below[:, :], compare_op=ALU.is_ge, fill=-BIG,
                               base=384, pattern=[[-1, 896]], channel_multiplier=1).then_inc(s_rel, 1)
            pool.drain()

        @block.sync
        def _(sp):
            credit(sp, c)
            sp.dma_start(K.rb[:, :, :], rel_bias.rearrange("(o b) h -> o b h", o=1).broadcast_to([P, BUCKETS, QH]))\
              .then_inc(s_load, 16)
            sp.wait_ge(s_load, 4 + 16)


def near_bias(dve, step, K, span, ge, diff):
    starts = bucket_starts()
    dve.tensor_tensor(diff[:, 1:, :], K.rb[:, 1:, :], K.rb[:, :-1, :], ALU.subtract)
    dve.tensor_tensor(diff[:, 0, :], K.rb[:, 0, :], K.rb[:, BUCKETS - 1, :], ALU.subtract)
    step.link(dve.tensor_scalar(ge[:, :], span, -1.0e9, None, ALU.is_ge))
    for h in range(QH):
        last = dve.tensor_scalar(K.near[:, h, :], ge[:, :], diff[:, 0, h:h + 1], None, ALU.mult)
    step.link(last)
    for b in range(1, BUCKETS):
        step.link(dve.tensor_scalar(ge[:, :], span, float(starts[b]), None, ALU.is_ge))
        for h in range(QH):
            last = dve.scalar_tensor_tensor(out=K.near[:, h, :], in0=ge[:, :], scalar=diff[:, b, h:h + 1],
                                            in1=K.near[:, h, :], op0=ALU.mult, op1=ALU.add)
        step.link(last)


def project(nc, K, x_prompt, x_sample, norm_mix, w_in):
    with phase(nc, "proj") as (c, stack):
        x = [c.sb(f"x{b}", [P, D]) for b in range(2)]
        junk = c.sb("junk", [P, D])
        stat = [c.sb(f"stat{b}", [P, 4]) for b in range(2)]
        ht = [c.sb(f"ht{b}", [P, KD, P]) for b in range(2)]
        gain = c.sb("gain", [P, KD])
        w_kv = c.sb("w_kv", [P, KD, 2 * KVH * HD])
        w_small = c.sb("w_small", [P, KD, SMALL])
        p_t = [c.ps(f"t{b}", [P, KD, P]) for b in range(2)]
        p_kv = [c.ps(f"kv{b}", [P, 512]) for b in range(2)]
        p_sm = [c.ps(f"sm{b}", [P, 512]) for b in range(2)]
        s_w = c.sem("w")
        s_load = c.sems("load")
        s_sum = c.sems("sum")
        s_mean = c.sems("mean")
        s_root = c.sems("root")
        s_inv = c.sems("inv")
        s_norm = c.sems("norm")
        s_turn = c.sems("turn")
        s_ht = c.sems("ht")
        s_kept = c.sems("kept")
        s_mm = c.sems("mm")
        s_out = c.sems("out")
        rows = w_in.rearrange("(k p) n -> p k n", p=P)
        block = open_block(nc, stack, c)

        def turns(eng, body):
            with eng.Fori(0, NT // 2) as j:
                for b in range(2):
                    body(j, b, j * 256 + b * P, j * 2 + b)
            body(NT // 2, 0, SEQ, NT)

        @block.sync
        def _(sp):
            credit(sp, c)
            sp.dma_start(gain[:, :], norm_mix.rearrange("(k p) -> p k", p=P), allow_slow_non_contiguous=True)\
              .then_inc(s_w, 16)

            def load(j, b, col, t):
                sp.wait_ge(s_turn[b], 4 + j)
                if t is NT or isinstance(t, int):
                    sp.dma_start(x[b][0:DEC, :], x_sample).then_inc(s_load[b], 16)
                else:
                    sp.dma_start(x[b][:, :], x_prompt[ds(col, P), :]).then_inc(s_load[b], 16)
            turns(sp, load)

        @block.gpsimd
        def _(pool):
            def keep(j, b, col, t):
                pool.wait_ge(s_ht[b], 4 + j + 1)
                pool.tensor_copy(K.ht[:, :, ds(col, P)], ht[b][:, :, :]).then_inc(s_kept[b], 1)
            turns(pool, keep)

        @block.scalar
        def _(act):
            act.dma_start(w_kv[:, :, :], rows[:, :, C_K:C_IQ]).then_inc(s_w, 16)
            act.dma_start(w_small[:, :, 0:2 * GH], rows[:, :, C_AB:C_Q]).then_inc(s_w, 16)
            act.dma_start(w_small[:, :, 2 * GH:], rows[:, :, C_IK:D_IN]).then_inc(s_w, 16)

            def stats(j, b, col, t):
                act.wait_ge(s_load[b], 4 + j * 16 + 16)
                act.activation(junk[:, :], x[b][:, :], ACT.Square, accum_out=stat[b][:, 0:1]).then_inc(s_sum[b], 1)
                act.wait_ge(s_mean[b], 4 + j + 1)
                act.activation(stat[b][:, 2:3], stat[b][:, 1:2], ACT.Sqrt).then_inc(s_root[b], 1)

            def copy_out(j, b, col, t):
                act.wait_ge(s_mm[b], 4 + j + 1)
                act.activation(K.k[:, t, :] if isinstance(t, int) else K.k[:, ds(t, 1), :], p_kv[b][:, 0:KVH * HD], ACT.Copy)
                act.activation(K.v[:, t, :] if isinstance(t, int) else K.v[:, ds(t, 1), :], p_kv[b][:, KVH * HD:], ACT.Copy)
                act.activation(K.small[:, t, :] if isinstance(t, int) else K.small[:, ds(t, 1), :], p_sm[b][:, 0:SMALL], ACT.Copy)\
                   .then_inc(s_out[b], 1)
            stats(0, 0, 0, 0)
            with act.Fori(0, NT // 2) as j:
                stats(j, 1, 0, 0)
                copy_out(j, 0, 0, j * 2)
                stats(j + 1, 0, 0, 0)
                copy_out(j, 1, 0, j * 2 + 1)
            copy_out(NT // 2, 0, 0, NT)

        @block.vector
        def _(dve):
            dve.wait_ge(s_w, 4 + 64)

            def norm(j, b, col, t):
                dve.wait_ge(s_sum[b], 4 + j + 1)
                dve.tensor_scalar(stat[b][:, 1:2], stat[b][:, 0:1], 1.0 / D, EPS, ALU.mult, ALU.add).then_inc(s_mean[b], 1)
                dve.wait_ge(s_root[b], 4 + j + 1)
                dve.reciprocal(stat[b][:, 3:4], stat[b][:, 2:3]).then_inc(s_inv[b], 1)
                dve.wait_ge(s_inv[b], 4 + j + 1)
                dve.tensor_scalar(x[b][:, :], x[b][:, :], stat[b][:, 3:4], None, ALU.mult).then_inc(s_norm[b], 1)

            def scale(j, b, col, t):
                dve.wait_ge(s_turn[b], 4 + j + 1)
                dve.wait_ge(s_kept[b], 4 + j)
                dve.wait_ge(s_mm[b], 4 + j)
                dve.tensor_tensor(ht[b][:, :, :], p_t[b][:, :, :],
                                  gain[:, :].unsqueeze(2).broadcast_to([P, KD, P]), ALU.mult).then_inc(s_ht[b], 1)
            norm(0, 0, 0, 0)
            with dve.Fori(0, NT // 2) as j:
                norm(j, 1, 0, 0)
                scale(j, 0, 0, 0)
                norm(j + 1, 0, 0, 0)
                scale(j, 1, 0, 0)
            scale(NT // 2, 0, 0, 0)

        @block.tensor
        def _(pe):
            pe.wait_ge(s_w, 4 + 64)

            def turn(j, b):
                pe.wait_ge(s_norm[b], 4 + j + 1)
                pe.wait_ge(s_ht[b], 4 + j)
                for k in range(KD):
                    last = pe.transpose(p_t[b][:, k, :], x[b][:, k * P:(k + 1) * P], K.ident[:, :])
                last.then_inc(s_turn[b], 1)

            def multiply(j, b):
                pe.wait_ge(s_ht[b], 4 + j + 1)
                pe.wait_ge(s_out[b], 4 + j)
                for k in range(KD):
                    pe.matmul(p_kv[b][:, :], ht[b][:, k, :], w_kv[:, k, :], start=(k == 0), stop=(k == KD - 1))
                for k in range(KD):
                    last = pe.matmul(p_sm[b][:, 0:SMALL], ht[b][:, k, :], w_small[:, k, :],
                                     start=(k == 0), stop=(k == KD - 1))
                last.then_inc(s_mm[b], 1)
            turn(0, 0)
            with pe.Fori(0, NT // 2) as j:
                turn(j, 1)
                multiply(j, 0)
                turn(j + 1, 0)
                multiply(j, 1)
            multiply(NT // 2, 0)


def keys(nc, K, k_norm, outs):
    with phase(nc, "keys") as (c, stack):
        sq = c.sb("sq", [P, TILES * KVH, HD])
        stat = c.sb("stat", [P, 4, TILES * KVH])
        gain = c.sb("gain", [P, HD])
        st = [c.sb(f"st{b}", [P, 3, P]) for b in range(2)]
        p_t = [c.ps(f"t{b}", [P, 4, P]) for b in range(2)]
        s_w, s_step, s_mean, s_root, s_normed, s_store = (c.sem(n) for n in
                                                          ("w", "step", "mean", "root", "normed", "store"))
        s_st, s_turn, s_out = c.sems("st"), c.sems("turn"), c.sems("out")
        kk = K.k[:, :, :].rearrange("p t (g d) -> p (t g) d", g=KVH)
        block = open_block(nc, stack, c)

        @block.sync
        def _(sp):
            credit(sp, c)
            sp.dma_start(gain[:, :], k_norm.rearrange("(o d) -> o d", o=1).broadcast_to([P, HD])).then_inc(s_w, 16)
            small = K.small[:, :, 2 * GH:2 * GH + ID]
            sp.dma_start(outs["p_idx"].rearrange("(t p) c -> p t c", p=P), small[:, 0:NT, :]).then_inc(s_store, 16)
            sp.dma_start(outs["s_idx"], K.small[0:DEC, NT, 2 * GH:2 * GH + ID]).then_inc(s_store, 16)
            sp.dma_start(outs["p_v"].rearrange("(t p) c -> p t c", p=P), K.v[:, 0:NT, :]).then_inc(s_store, 16)
            sp.dma_start(outs["s_v"], K.v[0:DEC, NT, :]).then_inc(s_store, 16)
            sp.wait_ge(s_normed, 4 + 1)
            sp.dma_start(outs["p_k"].rearrange("(t p) c -> p t c", p=P), K.k[:, 0:NT, :]).then_inc(s_store, 16)
            sp.dma_start(outs["s_k"], K.k[0:DEC, NT, :]).then_inc(s_store, 16)
            sp.wait_ge(s_store, 4 + 96)

        @block.vector
        def _(dve):
            step = Steps(dve, s_step)
            step.link(dve.tensor_tensor(sq[:, :, :], kk, kk, ALU.mult))
            step.link(dve.tensor_reduce(stat[:, 0, :], sq[:, :, :], AX.X, ALU.add))
            dve.tensor_scalar(stat[:, 1, :], stat[:, 0, :], 1.0 / HD, EPS, ALU.mult, ALU.add).then_inc(s_mean, 1)
            dve.wait_ge(s_root, 4 + 1)
            step.link(dve.reciprocal(stat[:, 3, :], stat[:, 2, :]))
            step.link(dve.tensor_tensor(kk, kk, stat[:, 3, :].unsqueeze(2).broadcast_to([P, TILES * KVH, HD]), ALU.mult))
            dve.wait_ge(s_w, 4 + 16)
            dve.tensor_tensor(kk, kk, gain[:, :].unsqueeze(1).broadcast_to([P, TILES * KVH, HD]), ALU.mult)\
               .then_inc(s_normed, 1)

            dve.wait_ge(s_normed, 4 + 1)
            dve.tensor_copy(K.knew[:, :], K.k[:, NT, :])

            def out(j, b, col):
                dve.wait_ge(s_turn[b], 4 + j + 1)
                dve.tensor_copy(K.kt[:, :, ds(col, P)], p_t[b][:, 0:KVH, :])
                dve.tensor_copy(K.ikt[:, ds(col, P)], p_t[b][:, KVH, :]).then_inc(s_out[b], 1)
            with dve.Fori(0, NT // 2) as j:
                out(j, 0, j * 256)
                out(j, 1, j * 256 + P)
            out(NT // 2, 0, SEQ)

        @block.scalar
        def _(act):
            act.wait_ge(s_mean, 4 + 1)
            act.activation(stat[:, 2, :], stat[:, 1, :], ACT.Sqrt).then_inc(s_root, 1)

        @block.gpsimd
        def _(pool):
            pool.wait_ge(s_normed, 4 + 1)

            def stage(j, b, t):
                pool.wait_ge(s_turn[b], 4 + j)
                pool.tensor_copy(st[b][:, 0:KVH, :], K.k[:, ds(t, 1), :].rearrange("p o (g d) -> p (o g) d", g=KVH))
                for half in range(2):
                    last = pool.tensor_copy(st[b][:, KVH, half * ID:(half + 1) * ID],
                                            K.small[:, ds(t, 1), 2 * GH:2 * GH + ID])
                last.then_inc(s_st[b], 1)
            with pool.Fori(0, NT // 2) as j:
                stage(j, 0, j * 2)
                stage(j, 1, j * 2 + 1)
            stage(NT // 2, 0, NT)

        @block.tensor
        def _(pe):
            def turn(j, b):
                pe.wait_ge(s_st[b], 4 + j + 1)
                pe.wait_ge(s_out[b], 4 + j)
                for g in range(3):
                    last = pe.transpose(p_t[b][:, g, :], st[b][:, g, :], K.ident[:, :])
                last.then_inc(s_turn[b], 1)
            with pe.Fori(0, NT // 2) as j:
                turn(j, 0)
                turn(j, 1)
            turn(NT // 2, 0)


def channels(nc, K, w_in, conv_w, conv_state, q_norm, outs):
    with phase(nc, "chan") as (c, stack):
        w = [c.sb(f"w{b}", [P, KD, P]) for b in range(2)]
        pre = [c.sb(f"pre{b}", [P, 3 + SEQ]) for b in range(2)]
        new = [c.sb(f"new{b}", [P, 3 + DEC]) for b in range(2)]
        acc = [c.sb(f"acc{b}", [P, TOK]) for b in range(2)]
        res = [c.sb(f"res{b}", [P, TOK]) for b in range(2)]
        past = [c.sb(f"past{b}", [P, P]) for b in range(2)]
        taps = c.sb("taps", [P, 4, CONVW])
        rows = c.sb("rows", [3 + DEC, CONV_CH])
        p_g = [c.ps(f"g{g}", [P, 512]) for g in range(GROUPS)]
        p_s = c.ps("s", [P, 512])
        p_past = c.ps("past", [P, P])
        p_rows = c.ps("rows", [3 + DEC, P])
        s_taps, s_zero, s_step, s_state, s_span = (c.sem(n) for n in ("taps", "zero", "step", "state", "span"))
        s_w = c.sems("w")
        s_past = c.sems("past")
        s_mm = c.sem("mm")
        s_free = c.sems("free", GROUPS)
        s_used = c.sems("used")
        s_sfree = c.sem("sfree")
        s_pre = c.sems("pre")
        s_acc = c.sems("acc")
        s_res = c.sems("res")
        s_st = c.sems("st")
        s_hist = c.sem("hist")
        s_back = c.sem("back")
        s_rows = c.sem("rows")
        wv = w_in.rearrange("(k p) n -> p k n", p=P)
        parts = [(0, CONVW, K.d_qkv, "conv"), (C_Z, 4, K.d_z, "silu"), (C_Q, 4, K.d_q, "copy"), (C_IQ, 4, K.d_iq, "copy")]
        block = open_block(nc, stack, c)

        def each(eng, body):
            n2 = 0
            for first, n, scratch, kind in parts:
                with eng.Fori(0, n // 2) as j:
                    for b in range(2):
                        body(j + n2, b, j * 256 + first + b * P, scratch, kind, j * 2 + b)
                n2 += n // 2

        @block.sync
        def _(sp):
            credit(sp, c)
            for i in range(4):
                sp.dma_start(taps[:, i, :], conv_w[i, :].rearrange("(m p) -> p m", p=P), allow_slow_non_contiguous=True)\
                  .then_inc(s_taps, 16)

            def load(j, b, col, scratch, kind, m):
                sp.wait_ge(s_used[b], 4 + j)
                sp.dma_start(w[b][:, :, :], wv[:, :, ds(col, P)]).then_inc(s_w[b], 16)
                if kind == "conv":
                    sp.wait_ge(s_hist, 4 + j * 2)
                    sp.dma_start(past[b][0:DEC * 3, :], conv_state[:, ds(col, P)]).then_inc(s_past[b], 16)
            sp.wait_ge(s_zero, 4 + 4)
            each(sp, load)
            sp.wait_ge(s_rows, 4 + CONVW)
            sp.dma_start(outs["p_gconv"], rows[0:3, :]).then_inc(s_state, 16)
            sp.dma_start(outs["s_gconv"][:, 2, :], rows[3:3 + DEC, :]).then_inc(s_state, 16)
            sp.dma_start(outs["s_gconv"][:, 0:2, :], conv_state.rearrange("(b j) n -> b j n", j=3)[:, 1:3, :])\
              .then_inc(s_state, 16)
            sp.wait_ge(s_state, 4 + 48)

        @block.tensor
        def _(pe):
            def multiply(j, b, col, scratch, kind, m):
                chunk = j * 2 + b
                pe.wait_ge(s_w[b], 4 + j * 16 + 16)
                for g in range(GROUPS):
                    pe.wait_ge(s_free[g], 4 + chunk)
                    for k in range(KD):
                        last = pe.matmul(p_g[g][:, :], w[b][:, k, :], K.ht[:, k, g * 512:(g + 1) * 512],
                                         start=(k == 0), stop=(k == KD - 1))
                    last.then_inc(s_mm, 1)
                pe.wait_ge(s_sfree, 4 + chunk)
                for k in range(KD):
                    last = pe.matmul(p_s[:, 0:DEC], w[b][:, k, :], K.ht[:, k, SEQ:SEQ + DEC],
                                     start=(k == 0), stop=(k == KD - 1))
                last.then_inc(s_used[b], 1)
                if kind == "conv":
                    pe.wait_ge(s_past[b], 4 + j * 16 + 16)
                    pe.wait_ge(s_step, 4 + chunk * 7)
                    pe.transpose(p_past[:, :], past[b][:, :], K.ident[:, :]).then_inc(s_hist, 1)
                    pe.wait_ge(s_pre[b], 4 + j + 1)
                    pe.wait_ge(s_rows, 4 + chunk)
                    pe.transpose(p_rows[:, :], new[b][:, :], K.ident[:, :]).then_inc(s_back, 1)
            each(pe, multiply)

        @block.scalar
        def _(act):
            def store(j, b, scratch, m, ready, n):
                act.wait_ge(ready, 4 + n)
                act.dma_start(scratch[ds(m, 1), :, :].rearrange("o p n -> (o p) n"), res[b][:, :])\
                   .then_inc(s_st[b], 16)

            def copies(j, b, col, kind):
                chunk = j * 2 + b
                if kind == "conv":
                    act.wait_ge(s_acc[b], 4 + j)
                else:
                    act.wait_ge(s_st[b], 4 + j * 16)
                dst = pre[b][:, 3:] if kind == "conv" else res[b]
                f = ACT.Silu if kind == "silu" else ACT.Copy
                for g in range(GROUPS):
                    act.wait_ge(s_mm, 4 + chunk * 4 + g + 1)
                    act.activation(dst[:, g * 512:(g + 1) * 512], p_g[g][:, :], f).then_inc(s_free[g], 1)
                act.wait_ge(s_used[b], 4 + j + 1)
                if kind == "conv":
                    act.activation(new[b][:, 3:], p_s[:, 0:DEC], ACT.Copy).then_inc(s_sfree, 1)
                    act.wait_ge(s_free[GROUPS - 1], 4 + chunk + 1)
                    act.activation(new[b][:, 0:3], pre[b][:, SEQ:], ACT.Copy).then_inc(s_pre[b], 1)
                    act.wait_ge(s_back, 4 + chunk + 1)
                    act.activation(rows[:, ds(col, P)], p_rows[:, :], ACT.Copy).then_inc(s_rows, 1)
                else:
                    act.activation(res[b][:, SEQ:], p_s[:, 0:DEC], f).then_inc(s_sfree, 1)

            def silu(j, b):
                act.wait_ge(s_acc[b], 4 + j + 1)
                act.wait_ge(s_st[b], 4 + j * 16)
                act.activation(res[b][:, :], acc[b][:, :], ACT.Silu).then_inc(s_res[b], 1)
            n2 = 0
            for _, n, scratch, kind in parts:
                if kind == "conv":
                    copies(0, 0, 0, kind)
                    with act.Fori(0, n // 2 - 1) as j:
                        copies(j, 1, j * 256 + P, kind)
                        silu(j, 0)
                        store(j, 0, K.d_qkv, j * 2, s_res[0], j + 1)
                        copies(j + 1, 0, j * 256 + 256, kind)
                        silu(j, 1)
                        store(j, 1, K.d_qkv, j * 2 + 1, s_res[1], j + 1)
                    last = n // 2 - 1
                    copies(last, 1, last * 256 + P, kind)
                    silu(last, 0)
                    silu(last, 1)
                    store(last, 1, K.d_qkv, n - 1, s_res[1], last + 1)
                    store(last, 0, K.d_qkv, n - 2, s_res[0], last + 1)
                else:
                    with act.Fori(0, n // 2) as j:
                        for b in range(2):
                            copies(j + n2, b, 0, kind)
                            store(j, b, scratch, j * 2 + b, s_sfree, (j + n2) * 2 + b + 1)
                n2 += n // 2
            for b in range(2):
                act.wait_ge(s_st[b], 4 + n2 * 16)

        @block.gpsimd
        def _(pool):
            for b in range(2):
                pool.wait_ge(s_res[b], 4 + CONVW // 2)
            pool.iota(acc[0][:, 256:512], pattern=[[-1, 256]], base=P, channel_multiplier=1,
                      allow_small_or_imprecise_dtypes=True).then_inc(s_span, 1)

        @block.vector
        def _(dve):
            for b in range(2):
                dve.memset(pre[b][:, 0:3], 0.0).then_inc(s_zero, 1)
                dve.memset(past[b][:, :], 0.0).then_inc(s_zero, 1)
            dve.wait_ge(s_zero, 4 + 4)
            dve.wait_ge(s_taps, 4 + 64)
            step = Steps(dve, s_step)
            with dve.Fori(0, CONVW // 2) as j:
                step.enter(j, 14, CONVW // 2)
                for b in range(2):
                    chunk = j * 2 + b
                    tap = [taps[:, i, ds(chunk, 1)] for i in range(4)]
                    dve.wait_ge(s_pre[b], 4 + j + 1)
                    dve.wait_ge(s_res[b], 4 + j)
                    a = acc[b][:, 0:SEQ]
                    step.link(dve.tensor_scalar(a, pre[b][:, 0:SEQ], tap[0], None, ALU.mult))
                    for i in range(1, 4):
                        step.link(dve.scalar_tensor_tensor(out=a, in0=pre[b][:, i:SEQ + i], scalar=tap[i], in1=a,
                                                           op0=ALU.mult, op1=ALU.add))
                    old = p_past[:, 0:DEC * 3].rearrange("p (b j) -> p b j", j=3)
                    a = acc[b][:, SEQ:]
                    dve.wait_ge(s_hist, 4 + chunk + 1)
                    step.link(dve.tensor_scalar(a, old[:, :, 0], tap[0], None, ALU.mult))
                    for i in range(1, 3):
                        step.link(dve.scalar_tensor_tensor(out=a, in0=old[:, :, i], scalar=tap[i], in1=a,
                                                           op0=ALU.mult, op1=ALU.add))
                    dve.scalar_tensor_tensor(out=a, in0=new[b][:, 3:], scalar=tap[3], in1=a,
                                             op0=ALU.mult, op1=ALU.add).then_inc(s_acc[b], 1)
                step.leave()
            for b in range(2):
                dve.wait_ge(s_res[b], 4 + CONVW // 2)
            dve.wait_ge(s_span, 4 + 1)
            near_bias(dve, step, K, acc[0][:, 256:512], acc[0][:, 0:256], acc[1][:, 0:BUCKETS * QH].rearrange("p (b h) -> p b h", h=QH))


LEVELS = 7


def gates(nc, K, a_log, dt_bias):
    with phase(nc, "gate") as (c, stack):
        x = c.sb("x", [P, TILES, GH])
        pos = c.sb("pos", [P, TILES, GH])
        e = c.sb("e", [P, TILES, GH])
        bias = c.sb("bias", [P, 2, GH])
        rowi, coli = c.sb("rowi", [P, P], I32), c.sb("coli", [P, P], I32)
        both, shifted = c.sb("both", [P, P], I32), c.sb("shifted", [P, P], I32)
        p_cum, p_all = c.ps("cum", [P, TILES * GH]), c.ps("all", [P, TILES * GH])
        s_load, s_step, s_abs, s_exp, s_one, s_ln, s_g, s_cum, s_cum_exp, s_iota, s_sig, s_alog, s_diff = (
            c.sem(n) for n in ("load", "step", "abs", "exp", "one", "ln", "g", "cum", "cum_exp", "iota", "sig", "alog", "diff"))
        a, b = K.small[:, :, 0:GH], K.small[:, :, GH:2 * GH]
        flat = lambda t: t[:, :, :].rearrange("p t h -> p (t h)")
        block = open_block(nc, stack, c)

        @block.sync
        def _(sp):
            credit(sp, c)
            sp.dma_start(bias[:, 0, :], dt_bias.broadcast_to([P, GH])).then_inc(s_load, 16)
            sp.dma_start(bias[:, 1, :], a_log.broadcast_to([P, GH])).then_inc(s_load, 16)

        @block.gpsimd
        def _(pool):
            pool.iota(rowi[:, :], pattern=[[0, P]], base=0, channel_multiplier=1)
            pool.iota(coli[:, :], pattern=[[1, P]], base=0, channel_multiplier=0).then_inc(s_iota, 1)

        @block.vector
        def _(dve):
            step = Steps(dve, s_step)
            dve.wait_ge(s_load, 4 + 32)
            step.link(dve.tensor_tensor(x[:, :, :], a, bias[:, 0, :].unsqueeze(1).broadcast_to([P, TILES, GH]), ALU.add))
            step.link(dve.tensor_scalar(pos[:, :, :], x[:, :, :], 0.0, None, ALU.max))
            dve.scalar_tensor_tensor(out=x[:, :, :], in0=pos[:, :, :], scalar=-2.0, in1=x[:, :, :],
                                     op0=ALU.mult, op1=ALU.add).then_inc(s_abs, 1)
            dve.wait_ge(s_exp, 4 + 1)
            dve.tensor_scalar(e[:, :, :], e[:, :, :], 1.0, None, ALU.add).then_inc(s_one, 1)
            dve.wait_ge(s_ln, 4 + 1)
            step.link(dve.tensor_tensor(x[:, :, :], pos[:, :, :], e[:, :, :], ALU.add))
            dve.wait_ge(s_alog, 4 + 1)
            dve.scalar_tensor_tensor(out=K.g[:, :, :], in0=x[:, :, :], scalar=-1.0,
                                     in1=bias[:, 1, :].unsqueeze(1).broadcast_to([P, TILES, GH]),
                                     op0=ALU.mult, op1=ALU.mult).then_inc(s_g, 1)
            dve.wait_ge(s_sig, 4 + 1)
            step.link(dve.tensor_scalar(K.beta[:, :, :], K.beta[:, :, :], 1.0, None, ALU.add))
            step.link(dve.reciprocal(K.beta[:, :, :], K.beta[:, :, :]))
            dve.wait_ge(s_cum, 4 + 1)
            step.link(dve.tensor_copy(flat(K.decay_sum), p_cum[:, :]))
            step.link(dve.tensor_copy(flat(K.glast), p_all[:, :]))
            dve.tensor_tensor(flat(K.kdec), flat(K.glast), flat(K.decay_sum), ALU.subtract).then_inc(s_diff, 1)
            dve.wait_ge(s_cum_exp, 4 + 3)
            step.link(dve.tensor_tensor(K.bexp[:, :, :], K.bexp[:, :, :], K.beta[:, :, :], ALU.mult))
            dve.wait_ge(s_iota, 4 + 1)
            step.link(dve.tensor_tensor(both[:, :], rowi[:, :], coli[:, :], ALU.bitwise_xor))
            for l in range(LEVELS):
                step.link(dve.tensor_scalar(shifted[:, :], both[:, :], l, None, ALU.logical_shift_right))
                for m, half in ((K.join, K.after), (K.join_t, K.before)):
                    last = dve.scalar_tensor_tensor(out=m[:, l, :], in0=shifted[:, :], scalar=1.0, in1=half[:, :],
                                                    op0=ALU.is_equal, op1=ALU.mult)
                step.link(last)

        @block.scalar
        def _(act):
            act.wait_ge(s_load, 4 + 32)
            act.activation(bias[:, 1, :], bias[:, 1, :], ACT.Exp).then_inc(s_alog, 1)
            act.activation(K.beta[:, :, :], b, ACT.Exp, scale=-1.0).then_inc(s_sig, 1)
            act.wait_ge(s_abs, 4 + 1)
            act.activation(e[:, :, :], x[:, :, :], ACT.Exp).then_inc(s_exp, 1)
            act.wait_ge(s_one, 4 + 1)
            act.activation(e[:, :, :], e[:, :, :], ACT.Ln).then_inc(s_ln, 1)
            act.wait_ge(s_diff, 4 + 1)
            act.activation(flat(K.bexp), flat(K.decay_sum), ACT.Exp).then_inc(s_cum_exp, 1)
            act.activation(flat(K.glast), flat(K.glast), ACT.Exp).then_inc(s_cum_exp, 1)
            act.activation(K.kdec[:, :, :], K.kdec[:, :, :], ACT.Exp).then_inc(s_cum_exp, 1)

        @block.tensor
        def _(pe):
            pe.wait_ge(s_g, 4 + 1)
            pe.matmul(p_cum[:, :], K.upto[:, :], flat(K.g), start=True, stop=True)
            pe.matmul(p_all[:, :], K.ones[:, :], flat(K.g), start=True, stop=True).then_inc(s_cum, 1)


def delta(nc, K, out_gain, outs):
    N = NT
    with phase(nc, "delta") as (c, stack):
        two = lambda name, shape: [c.sb(f"{name}{b}", shape) for b in range(2)]
        HW = [P, GH, P]
        raw = two("raw", [P, 3 * GH, P])
        z = two("z", HW)
        tmp = two("tmp", [P, 2 * GH, P])
        kq = two("kq", [P, GH, 2, P])
        qd = two("qd", HW)
        kw, kd, vb = two("kw", HW), two("kd", HW), two("vb", HW)
        gb = two("gb", HW)
        er = two("er", HW)
        et, el = two("et", HW), two("el", HW)
        am, at = two("am", HW), two("at", HW)
        qk = two("qk", HW)
        x, xt = two("x", HW), two("xt", HW)
        atm = two("atm", HW)
        y = two("y", HW)
        wt, vn = two("wt", HW), two("vn", HW)
        osb, orr = two("osb", HW), two("orr", HW)
        gain = c.sb("gain", [P, 1])
        bank = [[c.ps(f"bank{b}{i}", [P, GH, P]) for i in range(4)] for b in range(2)]
        names = ("gain zero qkv z gb sq ss inv rs norm turn tok row er dif dec eda gram attn sys syst first mask ycopy "
                 "yv prod upd wt wtc vnew vnc o oread kv state osq oss oinv ors ogain res").split()
        S = {n: c.sem(n) for n in names}
        s_ld, s_st, s_step = c.sems("ld"), c.sems("st"), c.sem("step")
        flat = lambda t: t[:, :, :].rearrange("p a b -> p (a b)")
        wide = lambda m: m.unsqueeze(1).broadcast_to(HW)
        block = open_block(nc, stack, c)

        def turns(eng, *bodies):
            with eng.Fori(0, N // 2) as j:
                for body in bodies:
                    for b in range(2):
                        body(j, b, j * 2 + b)

        @block.sync
        def _(sp):
            credit(sp, c)
            sp.dma_start(gain[:, :], out_gain.rearrange("(p o) -> p o", o=1)).then_inc(S["gain"], 16)

            def load(j, b, n):
                sp.wait_ge(S["tok"], 4 + n - 1)
                sp.dma_start(raw[b][:, :, :], K.d_qkv[:, :, ds(n * P, P)].rearrange("m p n -> p m n")).then_inc(s_ld[b], 16)
                sp.wait_ge(S["res"], 4 + n - 1)
                sp.dma_start(z[b][:, :, :], K.d_z[:, :, ds(n * P, P)].rearrange("m p n -> p m n")).then_inc(s_ld[b], 16)

            def store(j, b, n):
                sp.wait_ge(S["res"], 4 + n + 1)
                sp.dma_start(K.d_mix[0:GH, :, ds(n * P, P)].rearrange("m p n -> p m n"), orr[b][:, :, :]).then_inc(s_st[b], 16)
            turns(sp, load, store)
            sp.wait_ge(S["state"], 4 + N)
            sp.dma_start(outs["p_gdn"].rearrange("h k v -> k h v"), K.state[:, :, :]).then_inc(S["gain"], 16)
            sp.wait_ge(S["gain"], 4 + 32)
            for b in range(2):
                sp.wait_ge(s_st[b], 4 + N // 2 * 16)

        @block.tensor
        def _(pe):
            def norms(j, b, n):
                pe.wait_ge(S["sq"], 4 + n + 1)
                pe.wait_ge(S["state"], 4 + n - 1)
                for i in range(2):
                    last = pe.matmul(bank[b][i][:, :, :], K.ones[:, :], tmp[b][:, i * GH:(i + 1) * GH, :],
                                     start=True, stop=True)
                last.then_inc(S["ss"], 1)

            def rows(j, b, n):
                pe.wait_ge(S["gb"], 4 + n + 1)
                pe.wait_ge(S["vnc"], 4 + n - 1)
                for h in range(GH):
                    last = pe.matmul(bank[b][2][:, h, :], gb[b][:, h, :], K.upto[:, :], start=True, stop=True)
                last.then_inc(S["row"], 1)

            def turn(j, b, n):
                pe.wait_ge(S["norm"], 4 + n + 1)
                for h in range(GH):
                    pe.transpose(bank[b][0][:, h, :], kq[b][:, h, 0, :], K.ident[:, :])
                for h in range(GH):
                    last = pe.transpose(bank[b][1][:, h, :], raw[b][:, 2 * GH + h, :], K.ident[:, :])
                last.then_inc(S["turn"], 1)

            def gram(j, b, n):
                pe.wait_ge(S["dif"], 4 + n + 1)
                pe.wait_ge(S["er"], 4 + n + 1)
                pe.wait_ge(S["oinv"], 4 + n - 1)
                for h in range(GH):
                    last = pe.matmul(bank[b][2 + h // 2][:, (h % 2) * 2:(h % 2) * 2 + 2, :], kq[b][:, h, 0, :],
                                     kq[b][:, h, :, :], start=True, stop=True)
                last.then_inc(S["gram"], 1)

            def system(j, b, n):
                pe.wait_ge(S["sys"], 4 + n + 1)
                pe.wait_ge(S["tok"], 4 + n + 1)
                for h in range(GH):
                    last = pe.transpose(bank[b][0][:, h, :], am[b][:, h, :], K.ident[:, :])
                last.then_inc(S["syst"], 1)

            with pe.Fori(0, N // 2) as j:
                for body in (norms, rows, turn, gram, system):
                    for b in range(2):
                        body(j, b, j * 2 + b)
                for l in range(1, LEVELS):
                    for b in range(2):
                        m = j * 2 * (LEVELS - 1) + (l - 1) * 2 + b
                        pe.wait_ge(S["mask"], 4 + m + 1)
                        if l == 1:
                            pe.wait_ge(S["first"], 4 + j * 2 + b + 1)
                        else:
                            pe.wait_ge(S["upd"], 4 + m - 1)
                        for h in range(GH):
                            last = pe.matmul(bank[b][1][:, h, :], atm[b][:, h, :], x[b][:, h, :], start=True, stop=True)
                        last.then_inc(S["yv"], 1)
                    for b in range(2):
                        m = j * 2 * (LEVELS - 1) + (l - 1) * 2 + b
                        pe.wait_ge(S["ycopy"], 4 + m + 1)
                        for h in range(GH):
                            pe.matmul(bank[b][0][:, h, :], xt[b][:, h, :], y[b][:, h, :], start=True, stop=True)
                        for h in range(GH):
                            last = pe.matmul(bank[b][2][:, h, :], y[b][:, h, :], xt[b][:, h, :], start=True, stop=True)
                        last.then_inc(S["prod"], 1)
                for b in range(2):
                    m = j * 2 * (LEVELS - 1) + (LEVELS - 2) * 2 + b
                    pe.wait_ge(S["upd"], 4 + m + 1)
                    for h in range(GH):
                        last = pe.matmul(bank[b][3][:, h, :], kw[b][:, h, :], xt[b][:, h, :], start=True, stop=True)
                    last.then_inc(S["wt"], 1)
                for b in range(2):
                    n = j * 2 + b
                    pe.wait_ge(S["wtc"], 4 + n + 1)
                    pe.wait_ge(S["state"], 4 + n)
                    for h in range(GH):
                        pe.matmul(bank[b][1][:, h, :], xt[b][:, h, :], vb[b][:, h, :], start=True, stop=False)
                        last = pe.matmul(bank[b][1][:, h, :], wt[b][:, h, :], K.state[:, h, :], start=False, stop=True)
                    last.then_inc(S["vnew"], 1)
                    pe.wait_ge(S["vnc"], 4 + n + 1)
                    pe.wait_ge(S["eda"], 4 + n + 1)
                    for h in range(GH):
                        last = pe.matmul(bank[b][0][:, h, :], kd[b][:, h, :], vn[b][:, h, :], start=True, stop=True)
                    last.then_inc(S["kv"], 1)
                    for h in range(GH):
                        pe.matmul(bank[b][2][:, h, :], K.state[:, h, :], qd[b][:, h, :], start=True, stop=False)
                        last = pe.matmul(bank[b][2][:, h, :], vn[b][:, h, :], qk[b][:, h, :], start=False, stop=True)
                    last.then_inc(S["o"], 1)
                for b in range(2):
                    n = j * 2 + b
                    pe.wait_ge(S["osq"], 4 + n + 1)
                    pe.matmul(bank[b][3][:, :, :], K.ones[:, :], tmp[b][:, 0:GH, :], start=True, stop=True)\
                      .then_inc(S["oss"], 1)

        @block.scalar
        def _(act):
            with act.Fori(0, N // 2) as j:
                for b in range(2):
                    n = j * 2 + b
                    act.wait_ge(s_ld[b], 4 + j * 32 + 32)
                    act.wait_ge(S["ogain"], 4 + n - 1)
                    act.activation(tmp[b][:, :, :], raw[b][:, 0:2 * GH, :], ACT.Square).then_inc(S["sq"], 1)
                for b in range(2):
                    act.wait_ge(S["inv"], 4 + j * 2 + b + 1)
                    act.activation(tmp[b][:, :, :], tmp[b][:, :, :], ACT.Sqrt).then_inc(S["rs"], 1)
                for b in range(2):
                    act.wait_ge(S["row"], 4 + j * 2 + b + 1)
                    act.activation(er[b][:, :, :], bank[b][2][:, :, :], ACT.Exp).then_inc(S["er"], 1)
                for b in range(2):
                    act.wait_ge(S["dif"], 4 + j * 2 + b + 1)
                    act.activation(et[b][:, :, :], et[b][:, :, :], ACT.Exp)
                    act.activation(el[b][:, :, :], el[b][:, :, :], ACT.Exp, scale=-1.0).then_inc(S["dec"], 1)
                for l in range(1, LEVELS):
                    for b in range(2):
                        m = j * 2 * (LEVELS - 1) + (l - 1) * 2 + b
                        act.wait_ge(S["yv"], 4 + m + 1)
                        act.activation(y[b][:, :, :], bank[b][1][:, :, :], ACT.Copy).then_inc(S["ycopy"], 1)
                for b in range(2):
                    act.wait_ge(S["wt"], 4 + j * 2 + b + 1)
                    act.activation(wt[b][:, :, :], bank[b][3][:, :, :], ACT.Copy, scale=-1.0).then_inc(S["wtc"], 1)
                for b in range(2):
                    n = j * 2 + b
                    act.wait_ge(S["vnew"], 4 + n + 1)
                    act.activation(vn[b][:, :, :], bank[b][1][:, :, :], ACT.Copy).then_inc(S["vnc"], 1)
                    act.wait_ge(S["o"], 4 + n + 1)
                    act.activation(tmp[b][:, 0:GH, :], bank[b][2][:, :, :], ACT.Square)
                    act.activation(osb[b][:, :, :], bank[b][2][:, :, :], ACT.Copy).then_inc(S["osq"], 1)
                for b in range(2):
                    act.wait_ge(S["oinv"], 4 + j * 2 + b + 1)
                    act.activation(tmp[b][:, GH:, :], tmp[b][:, GH:, :], ACT.Sqrt).then_inc(S["ors"], 1)

        @block.gpsimd
        def _(pool):
            pool.memset(K.state[:, :, :], 0.0).then_inc(S["zero"], 1)
            with pool.Fori(0, N // 2) as j:
                for b in range(2):
                    n = j * 2 + b
                    pool.wait_ge(S["row"], 4 + n - 1)
                    pool.tensor_copy(gb[b][:, :, :], K.g[:, ds(n, 1), :].rearrange("p o h -> p (o h)").unsqueeze(2).broadcast_to(HW))\
                        .then_inc(S["gb"], 1)
                for b in range(2):
                    n = j * 2 + b
                    pool.wait_ge(S["er"], 4 + n + 1)
                    pool.wait_ge(S["norm"], 4 + n + 1)
                    pool.wait_ge(S["o"], 4 + n - 1)
                    pool.tensor_tensor(qd[b][:, :, :], kq[b][:, :, 1, :], er[b][:, :, :], ALU.mult)
                    pool.wait_ge(S["dec"], 4 + n + 1)
                    pool.tensor_tensor(et[b][:, :, :], et[b][:, :, :], wide(K.upto[:, :]), ALU.mult)
                    pool.tensor_tensor(el[b][:, :, :], el[b][:, :, :], wide(K.after[:, :]), ALU.mult).then_inc(S["eda"], 1)
                for l in range(1, LEVELS):
                    for b in range(2):
                        n = j * 2 + b
                        m = j * 2 * (LEVELS - 1) + (l - 1) * 2 + b
                        pool.wait_ge(S["first"], 4 + n + 1)
                        if l > 1:
                            pool.wait_ge(S["yv"], 4 + m - 1)
                        pool.tensor_tensor(atm[b][:, :, :], at[b][:, :, :], wide(K.join_t[:, l, :]), ALU.mult)\
                            .then_inc(S["mask"], 1)
                for b in range(2):
                    n = j * 2 + b
                    pool.wait_ge(S["ogain"], 4 + n + 1)
                    pool.wait_ge(s_ld[b], 4 + j * 32 + 32)
                    pool.tensor_tensor(orr[b][:, :, :], orr[b][:, :, :], z[b][:, :, :], ALU.mult).then_inc(S["res"], 1)

        @block.vector
        def _(dve):
            dve.wait_ge(S["gain"], 4 + 16)
            dve.wait_ge(S["zero"], 4 + 1)
            step = Steps(dve, s_step)
            with dve.Fori(0, N // 2) as j:
                step.enter(j, 8, N // 2)
                for b in range(2):
                    n = j * 2 + b
                    dve.wait_ge(S["ss"], 4 + n + 1)
                    for i in range(2):
                        last = dve.tensor_scalar(tmp[b][:, i * GH:(i + 1) * GH, :], bank[b][i][:, :, :], EPS, None, ALU.add)
                    step.link(last)
                    dve.reciprocal(tmp[b][:, :, :], tmp[b][:, :, :]).then_inc(S["inv"], 1)
                for b in range(2):
                    n = j * 2 + b
                    dve.wait_ge(S["er"], 4 + n + 1)
                    for h in range(GH):
                        gc = K.decay_sum[:, ds(n, 1), h]
                        dve.tensor_scalar(et[b][:, h, :], bank[b][2][:, h, :], gc, 0.0, ALU.subtract, ALU.min)
                        last = dve.tensor_scalar(el[b][:, h, :], bank[b][2][:, h, :], gc, 0.0, ALU.subtract, ALU.max)
                    last.then_inc(S["dif"], 1)
                for b in range(2):
                    n = j * 2 + b
                    dve.wait_ge(S["rs"], 4 + n + 1)
                    dve.tensor_tensor(kq[b][:, :, 0, :], raw[b][:, GH:2 * GH, :], tmp[b][:, GH:, :], ALU.mult)
                    dve.scalar_tensor_tensor(out=kq[b][:, :, 1, :], in0=raw[b][:, 0:GH, :], scalar=HD ** -0.5,
                                             in1=tmp[b][:, 0:GH, :], op0=ALU.mult, op1=ALU.mult).then_inc(S["norm"], 1)
                for b in range(2):
                    n = j * 2 + b
                    col = lambda t: t[:, ds(n, 1), :].rearrange("p o h -> p (o h)").unsqueeze(2).broadcast_to(HW)
                    dve.wait_ge(S["turn"], 4 + n + 1)
                    dve.tensor_tensor(kw[b][:, :, :], bank[b][0][:, :, :], col(K.bexp), ALU.mult)
                    dve.tensor_tensor(kd[b][:, :, :], bank[b][0][:, :, :], col(K.kdec), ALU.mult)
                    dve.tensor_tensor(vb[b][:, :, :], bank[b][1][:, :, :], col(K.beta), ALU.mult).then_inc(S["tok"], 1)
                for b in range(2):
                    n = j * 2 + b
                    dve.wait_ge(S["gram"], 4 + n + 1)
                    dve.wait_ge(S["eda"], 4 + n + 1)
                    for h in range(GH):
                        bk, o = bank[b][2 + h // 2], (h % 2) * 2
                        dve.tensor_tensor(qk[b][:, h, :], bk[:, o + 1, :], et[b][:, h, :], ALU.mult)
                        last = dve.scalar_tensor_tensor(out=am[b][:, h, :], in0=bk[:, o, :], scalar=K.beta[:, ds(n, 1), h],
                                                        in1=el[b][:, h, :], op0=ALU.mult, op1=ALU.mult)
                    last.then_inc(S["sys"], 1)
                for b in range(2):
                    n = j * 2 + b
                    dve.wait_ge(S["sys"], 4 + n + 1)
                    step.link(dve.tensor_tensor(x[b][:, :, :], am[b][:, :, :], wide(K.join[:, 0, :]), ALU.mult))
                    dve.tensor_tensor(x[b][:, :, :], wide(K.ident[:, :]), x[b][:, :, :], ALU.subtract)
                    dve.wait_ge(S["syst"], 4 + n + 1)
                    step.link(dve.tensor_copy(at[b][:, :, :], bank[b][0][:, :, :]))
                    dve.tensor_tensor(xt[b][:, :, :], at[b][:, :, :], wide(K.join_t[:, 0, :]), ALU.mult).then_inc(S["attn"], 1)
                    dve.wait_ge(S["attn"], 4 + n + 1)
                    dve.tensor_tensor(xt[b][:, :, :], wide(K.ident[:, :]), xt[b][:, :, :], ALU.subtract).then_inc(S["first"], 1)
                for l in range(1, LEVELS):
                    for b in range(2):
                        m = j * 2 * (LEVELS - 1) + (l - 1) * 2 + b
                        dve.wait_ge(S["prod"], 4 + m + 1)
                        dve.tensor_tensor(x[b][:, :, :], x[b][:, :, :], bank[b][0][:, :, :], ALU.subtract)
                        dve.tensor_tensor(xt[b][:, :, :], xt[b][:, :, :], bank[b][2][:, :, :], ALU.subtract).then_inc(S["upd"], 1)
                for b in range(2):
                    n = j * 2 + b
                    dve.wait_ge(S["o"], 4 + n + 1)
                    for h in range(GH):
                        last = dve.scalar_tensor_tensor(out=K.state[:, h, :], in0=K.state[:, h, :], scalar=K.glast[:, ds(n, 1), h],
                                                        in1=bank[b][0][:, h, :], op0=ALU.mult, op1=ALU.add)
                    last.then_inc(S["state"], 1)
                for b in range(2):
                    n = j * 2 + b
                    dve.wait_ge(S["oss"], 4 + n + 1)
                    step.link(dve.tensor_scalar(tmp[b][:, GH:, :], bank[b][3][:, :, :], 1.0 / HD, EPS, ALU.mult, ALU.add))
                    dve.reciprocal(tmp[b][:, GH:, :], tmp[b][:, GH:, :]).then_inc(S["oinv"], 1)
                for b in range(2):
                    n = j * 2 + b
                    dve.wait_ge(S["ors"], 4 + n + 1)
                    dve.wait_ge(s_st[b], 4 + j * 16)
                    dve.scalar_tensor_tensor(out=orr[b][:, :, :], in0=osb[b][:, :, :], scalar=gain[:, 0:1],
                                             in1=tmp[b][:, GH:, :], op0=ALU.mult, op1=ALU.mult).then_inc(S["ogain"], 1)
                step.leave()


class Events(dict):

    def __init__(self, c):
        super().__init__()
        self.c = c

    def __missing__(self, name):
        self[name] = self.c.sem(name)
        return self[name]


class Chain:

    def __init__(self, eng, sem):
        self.eng, self.sem, self.n = eng, sem, 0

    def __call__(self, ins):
        self.n += 1
        ins.then_inc(self.sem, 1)
        self.eng.wait_ge(self.sem, self.n)


def delta_step(nc, K, state_in, out_gain, outs):
    R = GH * DEC
    with phase(nc, "dstep") as (c, stack):
        raw, z = c.sb("raw", [P, 3 * GH, DEC]), c.sb("z", [P, GH, DEC])
        st = c.sb("st", [P, R, HD])
        sq = c.sb("sq", [P, 2 * GH, DEC])
        dg = c.sb("dg", [DEC, 2, GH, DEC])
        eg, beta = c.sb("eg", [P, R]), c.sb("beta", [P, R])
        kn, kq = c.sb("kn", [P, R]), c.sb("kq", [P, R, 2])
        qn, prod, vn = c.sb("qn", [P, R]), c.sb("prod", [P, R]), c.sb("vn", [P, R])
        tmp, o, osq, inv = c.sb("tmp", [P, R]), c.sb("o", [P, R]), c.sb("osq", [P, R]), c.sb("inv", [P, R])
        kt, vt = c.sb("kt", [R, P]), c.sb("vt", [R, P])
        vm = c.sb("vm", [R, R, HD])
        gain = c.sb("gain", [P, 1])
        p_ss, p_g, p_s = c.ps("ss", [P, 2 * R]), c.ps("g", [P, 2 * R]), c.ps("s", [P, R, 2])
        p_qk, p_t, p_oss = c.ps("qk", [P, R]), c.ps("t", [R, 2, P]), c.ps("oss", [P, R])
        p_u = [c.ps(f"u{i}", [P, 4, HD]) for i in range(2)]
        E = Events(c)
        s_upd = c.sem("upd")
        s_sum = c.sem("usum")
        flat = lambda t: t[:, :, :].rearrange("p h r -> p (h r)")
        block = open_block(nc, stack, c)

        @block.sync
        def _(sp):
            sp.dma_start(raw[:, :, :], K.d_qkv[:, :, SEQ:TOK].rearrange("m p r -> p m r")).then_inc(E["load"], 16)
            sp.dma_start(z[:, :, :], K.d_z[:, :, SEQ:TOK].rearrange("m p r -> p m r")).then_inc(E["load"], 16)
            sp.dma_start(gain[:, :], out_gain.rearrange("(p o) -> p o", o=1)).then_inc(E["load"], 16)
            for h in range(GH):
                sp.dma_start(st[:, h * DEC:(h + 1) * DEC, :], state_in[:, h, :, :].rearrange("b k v -> k b v"))\
                  .then_inc(E["state"], 16)
            sp.wait_ge(s_sum, R // 4)
            for h in range(GH):
                sp.dma_start(outs["s_gdn"][:, h, :, :].rearrange("b k v -> k b v"), st[:, h * DEC:(h + 1) * DEC, :])\
                  .then_inc(E["stored"], 16)
            sp.wait_ge(E["mixed"], 1)
            sp.dma_start(K.d_mix[0:GH, :, SEQ:TOK].rearrange("m p r -> p m r"), o[:, :].rearrange("p (h r) -> p h r", h=GH))\
              .then_inc(E["stored"], 16)
            sp.wait_ge(E["stored"], 80)

        @block.vector
        def _(dve):
            step = Chain(dve, E["dve"])
            for i, src in enumerate((K.g, K.beta)):
                last = dve.tensor_tensor(dg[:, i, :, :], src[0:DEC, NT, :].unsqueeze(2).broadcast_to([DEC, GH, DEC]),
                                         K.ident[0:DEC, 0:DEC].unsqueeze(1).broadcast_to([DEC, GH, DEC]), ALU.mult)
            last.then_inc(E["diagonal"], 1)
            dve.wait_ge(E["ss"], 1)
            step(dve.tensor_scalar(flat(sq), p_ss[:, :], EPS, None, ALU.add))
            dve.reciprocal(flat(sq), flat(sq)).then_inc(E["inv"], 1)
            dve.wait_ge(E["eg"], 1)
            step(dve.tensor_copy(beta[:, :], p_g[:, R:]))
            dve.wait_ge(E["rs"], 1)
            step(dve.tensor_tensor(kn[:, :], raw[:, GH:2 * GH, :].rearrange("p h r -> p (h r)"), flat(sq)[:, R:], ALU.mult))
            step(dve.scalar_tensor_tensor(out=qn[:, :], in0=raw[:, 0:GH, :].rearrange("p h r -> p (h r)"), scalar=HD ** -0.5,
                                          in1=flat(sq)[:, 0:R], op0=ALU.mult, op1=ALU.mult))
            dve.tensor_tensor(kq[:, :, 0], kn[:, :], eg[:, :], ALU.mult)
            dve.tensor_tensor(kq[:, :, 1], qn[:, :], eg[:, :], ALU.mult)
            dve.tensor_tensor(prod[:, :], qn[:, :], kn[:, :], ALU.mult).then_inc(E["columns"], 1)
            dve.wait_ge(E["read"], 1)
            step(dve.tensor_tensor(tmp[:, :], raw[:, 2 * GH:, :].rearrange("p h r -> p (h r)"), p_s[:, :, 0], ALU.subtract))
            dve.tensor_tensor(vn[:, :], tmp[:, :], beta[:, :], ALU.mult).then_inc(E["vnew"], 1)
            dve.wait_ge(E["vnew"], 1)
            step(dve.tensor_tensor(tmp[:, :], p_qk[:, :], vn[:, :], ALU.mult))
            step(dve.tensor_tensor(o[:, :], p_s[:, :, 1], tmp[:, :], ALU.add))
            dve.tensor_tensor(osq[:, :], o[:, :], o[:, :], ALU.mult).then_inc(E["osq"], 1)
            dve.wait_ge(E["turned"], 1)
            dve.tensor_copy(kt[:, :], p_t[:, 0, :])
            step(dve.tensor_copy(vt[:, :], p_t[:, 1, :]))
            dve.tensor_tensor(vm[:, :, :], vt[:, :].unsqueeze(1).broadcast_to([R, R, HD]),
                              K.ident[0:R, 0:R].unsqueeze(2).broadcast_to([R, R, HD]), ALU.mult).then_inc(E["apart"], 1)
            dve.wait_ge(E["state"], 64)
            dve.wait_ge(E["read"], 1)
            step(dve.tensor_tensor(st[:, :, :], st[:, :, :], eg[:, :].unsqueeze(2).broadcast_to([P, R, HD]), ALU.mult))
            for i in range(R // 4):
                dve.wait_ge(s_upd, i + 1)
                part = st[:, i * 4:(i + 1) * 4, :]
                dve.tensor_tensor(part, part, p_u[i % 2][:, :, :], ALU.add).then_inc(s_sum, 1)
            dve.wait_ge(E["oss"], 1)
            step(dve.tensor_scalar(inv[:, :], p_oss[:, :], 1.0 / HD, EPS, ALU.mult, ALU.add))
            dve.reciprocal(inv[:, :], inv[:, :]).then_inc(E["oinv"], 1)
            dve.wait_ge(E["ors"], 1)
            step(dve.scalar_tensor_tensor(out=o[:, :], in0=o[:, :], scalar=gain[:, 0:1], in1=inv[:, :], op0=ALU.mult, op1=ALU.mult))
            dve.tensor_tensor(o[:, :], o[:, :], flat(z), ALU.mult).then_inc(E["mixed"], 1)

        @block.scalar
        def _(act):
            act.wait_ge(E["load"], 48)
            act.activation(sq[:, :, :], raw[:, 0:2 * GH, :], ACT.Square).then_inc(E["sq"], 1)
            act.wait_ge(E["gates"], 1)
            act.activation(eg[:, :], p_g[:, 0:R], ACT.Exp).then_inc(E["eg"], 1)
            act.wait_ge(E["inv"], 1)
            act.activation(sq[:, :, :], sq[:, :, :], ACT.Sqrt).then_inc(E["rs"], 1)
            act.wait_ge(E["oinv"], 1)
            act.activation(inv[:, :], inv[:, :], ACT.Sqrt).then_inc(E["ors"], 1)

        @block.tensor
        def _(pe):
            pe.wait_ge(E["diagonal"], 1)
            pe.matmul(p_g[:, :], K.ones[0:DEC, :], dg[:, :, :, :].rearrange("r i h s -> r (i h s)"), start=True, stop=True)\
              .then_inc(E["gates"], 1)
            pe.wait_ge(E["sq"], 1)
            pe.matmul(p_ss[:, :], K.ones[:, :], flat(sq), start=True, stop=True).then_inc(E["ss"], 1)
            pe.wait_ge(E["columns"], 1)
            pe.wait_ge(E["state"], 64)
            for i in range(R):
                pe.matmul(p_s[:, i, :], st[:, i, :], kq[:, i, :], start=True, stop=True)
            pe.matmul(p_qk[:, :], K.ones[:, :], prod[:, :], start=True, stop=True).then_inc(E["read"], 1)
            pe.wait_ge(E["vnew"], 1)
            pe.transpose(p_t[:, 0, :], kn[:, :], K.ident[:, :])
            pe.transpose(p_t[:, 1, :], vn[:, :], K.ident[:, :]).then_inc(E["turned"], 1)
            pe.wait_ge(E["osq"], 1)
            pe.matmul(p_oss[:, :], K.ones[:, :], osq[:, :], start=True, stop=True).then_inc(E["oss"], 1)
            pe.wait_ge(E["apart"], 1)
            for i in range(R // 4):
                if i >= 2:
                    pe.wait_ge(s_sum, i - 1)
                pe.matmul(p_u[i % 2][:, :, :], kt[:, :], vm[:, i * 4:(i + 1) * 4, :], start=True, stop=True).then_inc(s_upd, 1)


def attend(nc, K, q_norm, outs):
    NK = SEQ
    with phase(nc, "att") as (c, stack):
        two = lambda name, shape, dt=F32: [c.sb(f"{name}{b}", shape, dt) for b in range(2)]
        qin, qg, iqin = two("qin", [P, QH, P]), two("qg", [P, QH, P]), two("iqin", [P, IH // 2, P])
        qsq = two("qsq", [P, QH, P])
        rq = c.sb("rq", [P, 2, QH])
        iw = c.sb("iw", [P, TILES, IH])
        r = [c.sb(f"r{i}", [P, 512]) for i in range(2)]
        sc = two("sc", [P, NK])
        above = c.sb("above", [P, NK], BF16)
        tie = c.sb("tie", [P, NK], BF16)
        hits = [above, tie]
        mask = two("mask", [P, NK], BF16)
        logit = two("logit", [P, QH, P + NK])
        pt = [c.sb(f"pt{i}", [P, 4, P]) for i in range(2)]
        ob, ot = two("ob", [P, QH, HD]), two("ot", [P, QH, P])
        gain = c.sb("gain", [P, 1])
        trial, other, miss = (c.sb(n, [P, 2], I32) for n in ("trial", "other", "miss"))
        count = c.sb("count", [P, 2])
        signs = c.sb("signs", [P, 1])
        next_up, normal = c.sb("next_up", [P, 1]), c.sb("normal", [P, 1])
        flip = c.sb("flip", [P, 1], I32)
        top = c.sb("top", [P, 2, QH])
        total = c.sb("total", [P, 2, QH])
        inv = c.sb("inv", [P, 2, QH])
        p_sc = [c.ps(f"sc{i}", [P, 512]) for i in range(2)]
        p_lg = [c.ps(f"lg{i}", [P, 512]) for i in range(2)]
        p_t = [c.ps(f"t{i}", [P, 4, P]) for i in range(2)]
        p_o = c.ps("o", [P, QH, HD])
        p_m = c.ps("m", [P, 512])
        S = {n: c.sem(n) for n in ("gain out zero sq qg ss mean rq sc relu sum added step lg lgc max exp turn ptc pv "
                                   "norm oturn otc tried signs").split()}
        s_q, s_iq = c.sems("q"), c.sems("iq")
        s_st = c.sems("st")
        block = open_block(nc, stack, c)
        per_turn = [2 + 3 + 2 * 31 + 11 + 2 * (6 + (G == 0)) + 2 + 2 for G in range(4)]
        before = lambda G: sum(4 * (g + 1) for g in range(G))

        def su(G, j, b, h=0, kc=0):
            return j * (16 * (G + 1)) + (IH * before(G) + b * 8 * (G + 1) + h * (G + 1) + kc)

        def lu(G, j, b, h=0, kc=0):
            return j * (8 * (G + 1)) + (QH * before(G) + b * 4 * (G + 1) + h * (G + 1) + kc)

        @block.sync
        def _(sp):
            credit(sp, c)
            sp.dma_start(gain[:, :], q_norm.rearrange("(p o) -> p o", o=1)).then_inc(S["gain"], 16)

            def load(i, b):
                sp.wait_ge(S["sq"], 4 + i * 2)
                sp.wait_ge(S["qg"], 4 + i * 2)
                sp.dma_start(qin[b][:, :, :], K.d_q[:, :, ds(i * 256 + b * P, P)].rearrange("m p n -> p m n")).then_inc(s_q[b], 16)
                sp.wait_ge(S["added"], 4 + i * 2)
                sp.dma_start(iqin[b][:, :, :], K.d_iq[:, :, ds(i * 256 + b * P, P)].rearrange("m p n -> p m n")).then_inc(s_iq[b], 16)

            def store(i, b):
                sp.wait_ge(S["otc"], 4 + i * 2 + b + 1)
                sp.dma_start(K.d_mix[GH:, :, ds(i * 256 + b * P, P)].rearrange("m p n -> p m n"), ot[b][:, :, :])\
                  .then_inc(s_st[b], 16)
            for b in range(2):
                load(0, b)
            with sp.Fori(0, NT // 2 - 1) as i:
                for b in range(2):
                    load(i + 1, b)
                for b in range(2):
                    store(i, b)
            for b in range(2):
                store(NT // 2 - 1, b)
            for b in range(2):
                sp.wait_ge(s_st[b], 4 + NT // 2 * 16)

        @block.tensor
        def _(pe):
            for G in range(4):
                with pe.Fori(0, 2) as j:
                    i = j + G * 2
                    for b in range(2):
                        pe.wait_ge(S["sq"], 4 + i * 2 + b + 1)
                        pe.wait_ge(S["mean"], 4 + i)
                        pe.wait_ge(S["otc"], 4 + i * 2)
                        for h in range(QH):
                            last = pe.matmul(p_m[:, b * QH + h:b * QH + h + 1], qsq[b][:, h, :], K.ones[:, 0:1],
                                             start=True, stop=True)
                    last.then_inc(S["ss"], 1)
                    for b in range(2):
                        pe.wait_ge(s_iq[b], 4 + i * 16 + 16)
                        for h in range(IH):
                            half = slice((h % 2) * ID, (h % 2 + 1) * ID)
                            for kc in range(G + 1):
                                pe.wait_ge(S["relu"], 4 + su(G, j, b, h, kc) - 1)
                                pe.matmul(p_sc[(h * (G + 1) + kc) % 2][:, :], iqin[b][half, h // 2, :],
                                          K.ikt[half, kc * 512:(kc + 1) * 512], start=True, stop=True).then_inc(S["sc"], 1)
                    for b in range(2):
                        pe.wait_ge(S["qg"], 4 + i * 2 + b + 1)
                        for h in range(QH):
                            for kc in range(G + 1):
                                pe.wait_ge(S["lgc"], 4 + lu(G, j, b, h, kc) - 1)
                                pe.matmul(p_lg[(h * (G + 1) + kc) % 2][:, :], qg[b][:, h, :],
                                          K.kt[:, h // GROUP, kc * 512:(kc + 1) * 512], start=True, stop=True).then_inc(S["lg"], 1)
                    for b in range(2):
                        def turn(u):
                            h, kc = divmod(u, G + 1)
                            pe.wait_ge(S["exp"], 4 + (i * 2 + b) * QH + h + 1)
                            pe.wait_ge(S["ptc"], 4 + lu(G, j, b, h, kc) - 1)
                            for k in range(4):
                                col = P + kc * 512 + k * P
                                last = pe.transpose(p_t[u % 2][:, k, :], logit[b][:, h, col:col + P], K.ident[:, :])
                            last.then_inc(S["turn"], 1)
                        U = QH * (G + 1)
                        pe.wait_ge(S["norm"], 4 + i * 2 + b)
                        turn(0)
                        for u in range(U):
                            h, kc = divmod(u, G + 1)
                            if u + 1 < U:
                                turn(u + 1)
                            pe.wait_ge(S["ptc"], 4 + lu(G, j, b, h, kc) + 1)
                            for k in range(4):
                                last = pe.matmul(p_o[:, h, :], pt[u % 2][:, k, :],
                                                 K.v[:, kc * 4 + k, (h // GROUP) * HD:(h // GROUP + 1) * HD],
                                                 start=(kc == 0 and k == 0), stop=(kc == G and k == 3))
                            last.then_inc(S["pv"], 1)
                        pe.wait_ge(S["norm"], 4 + i * 2 + b + 1)
                        pe.wait_ge(S["otc"], 4 + i * 2 + b)
                        for h in range(QH):
                            last = pe.transpose(p_m[:, h * P:(h + 1) * P], ob[b][:, h, :], K.ident[:, :])
                        last.then_inc(S["oturn"], 1)

        @block.scalar
        def _(act):
            act.wait_ge(S["gain"], 4 + 16)
            for G in range(4):
                with act.Fori(0, 2) as j:
                    i = j + G * 2
                    for b in range(2):
                        act.wait_ge(s_q[b], 4 + i * 16 + 16)
                        act.wait_ge(S["ss"], 4 + i)
                        act.activation(qsq[b][:, :, :], qin[b][:, :, :], ACT.Square).then_inc(S["sq"], 1)
                        act.wait_ge(S["norm"], 4 + i * 2)
                        act.activation(qg[b][:, :, :], qin[b][:, :, :], ACT.Copy, scale=gain[:, 0:1]).then_inc(S["qg"], 1)
                    act.wait_ge(S["mean"], 4 + i + 1)
                    act.activation(rq[:, :, :], rq[:, :, :], ACT.Sqrt).then_inc(S["rq"], 1)
                    for b in range(2):
                        for u in range(IH * (G + 1)):
                            n = su(G, j, b) + u
                            act.wait_ge(S["sc"], 4 + n + 1)
                            act.wait_ge(S["sum"], 4 + n - 1)
                            act.activation(r[u % 2][:, :], p_sc[u % 2][:, :], ACT.Relu).then_inc(S["relu"], 1)
                    for m in range(31):
                        act.wait_ge(S["tried"], 4 + i * 32 + m + 1)
                        act.activation(tie[:, 0:(G + 1) * 512], sc[1][:, 0:(G + 1) * 512], ACT.Sign, scale=-1.0,
                                       bias=trial[:, 1:2].bitcast(F32), accum_out=signs[:, :]).then_inc(S["signs"], 1)
                    for b in range(2):
                        act.wait_ge(S["max"], 4 + i * 2 + b + 1)
                        for h in range(QH):
                            row = logit[b][:, h, P:P + (G + 1) * 512]
                            act.activation(row, row, ACT.Exp, bias=top[:, b, h:h + 1], accum_out=total[:, b, h:h + 1])\
                               .then_inc(S["exp"], 1)
                        for u in range(QH * (G + 1)):
                            n = lu(G, j, b) + u
                            act.wait_ge(S["turn"], 4 + n + 1)
                            act.wait_ge(S["pv"], 4 + n - 1)
                            act.activation(pt[u % 2][:, :, :], p_t[u % 2][:, :, :], ACT.Copy).then_inc(S["ptc"], 1)
                        act.wait_ge(S["oturn"], 4 + i * 2 + b + 1)
                        act.wait_ge(s_st[b], 4 + i * 16)
                        act.activation(ot[b][:, :, :], p_m[:, :].rearrange("p (h n) -> p h n", h=QH), ACT.Copy)\
                           .then_inc(S["otc"], 1)

        @block.vector
        def _(dve):
            step = Steps(dve, S["step"])
            for b in range(2):
                dve.memset(logit[b][:, :, 0:P], 0.0)
            step.link(dve.tensor_scalar(iw[:, :, :], K.small[:, :, 2 * GH + ID:], INDEX_SCALE, None, ALU.mult))
            for G in range(4):
                nk = (G + 1) * 512
                with dve.Fori(0, 2) as j:
                    i = j + G * 2
                    step.enter(j, per_turn[G], 2)
                    dve.wait_ge(S["ss"], 4 + i + 1)
                    ss = p_m[:, 0:2 * QH].rearrange("p (b h) -> p b h", b=2)
                    step.link(dve.tensor_scalar(rq[:, :, :], ss, 1.0 / HD, EPS, ALU.mult, ALU.add))
                    dve.reciprocal(rq[:, :, :], rq[:, :, :]).then_inc(S["mean"], 1)
                    dve.wait_ge(S["rq"], 4 + i + 1)
                    step.link(dve.tensor_scalar(rq[:, :, :], rq[:, :, :], SCALE, None, ALU.mult))
                    for b in range(2):
                        for h in range(IH):
                            w = iw[:, ds(i * 2 + b, 1), h]
                            for kc in range(G + 1):
                                n, u = su(G, j, b, h, kc), h * (G + 1) + kc
                                part = sc[b][:, kc * 512:(kc + 1) * 512]
                                dve.wait_ge(S["relu"], 4 + n + 1)
                                if h == 0:
                                    dve.tensor_scalar(part, r[u % 2][:, :], w, None, ALU.mult).then_inc(S["sum"], 1)
                                else:
                                    dve.wait_ge(S["sum"], 4 + n - G)
                                    dve.scalar_tensor_tensor(out=part, in0=r[u % 2][:, :], scalar=w, in1=part,
                                                             op0=ALU.mult, op1=ALU.add).then_inc(S["sum"], 1)
                        dve.wait_ge(S["sum"], 4 + su(G, j, b + 1))
                        own = sc[b][:, G * 512:nk]
                        dve.tensor_tensor(own, own, K.below[:, ds((j * 2 + b) * -P + 384, 512)], ALU.min).then_inc(S["added"], 1)
                    dve.wait_ge(S["added"], 4 + i * 2 + 2)
                    for b in range(2):
                        last = dve.tensor_scalar(hits[b][:, 0:nk], sc[b][:, 0:nk], 0.0, None, ALU.is_ge, ALU.add,
                                                 accum_out=count[:, b:b + 1])
                    step.link(last)
                    step.link(dve.tensor_scalar(miss[:, :], count[:, :], float(NSEL), None, ALU.is_lt))
                    step.link(dve.tensor_scalar(trial[:, :], miss[:, :], 31, 31, ALU.logical_shift_left, ALU.arith_shift_right))
                    dve.tensor_scalar(trial[:, :], trial[:, :], 1 << 30, None, ALU.bitwise_xor).then_inc(S["tried"], 1)
                    dve.wait_ge(S["tried"], 4 + i * 32 + 1)
                    for bit in range(30, -1, -1):
                        level = trial[:, :].bitcast(F32)
                        last = dve.tensor_scalar(above[:, 0:nk], sc[0][:, 0:nk], level[:, 0:1], None, ALU.is_ge, ALU.add,
                                                 accum_out=count[:, 0:1])
                        if bit:
                            dve.tensor_scalar(other[:, :], trial[:, :], 1 << (bit - 1), None, ALU.bitwise_xor)
                        else:
                            dve.tensor_copy(other[:, :], trial[:, :])
                        step.link(last)
                        dve.tensor_scalar(miss[:, 0:1], count[:, 0:1], float(NSEL), None, ALU.is_lt)
                        dve.wait_ge(S["signs"], 4 + i * 31 + (30 - bit) + 1)
                        step.link(dve.tensor_scalar(miss[:, 1:2], signs[:, :], float(nk - 2 * NSEL), None, ALU.is_gt))
                        dve.scalar_tensor_tensor(out=trial[:, :], in0=miss[:, :], scalar=bit, in1=other[:, :],
                                                 op0=ALU.logical_shift_left, op1=ALU.bitwise_xor).then_inc(S["tried"], 1)
                        dve.wait_ge(S["tried"], 4 + i * 32 + (30 - bit) + 2)
                    level, below_s = trial[:, 1:2].bitcast(F32), logit[1][:, 0, P:P + nk]
                    dve.wait_ge(S["pv"], 4 + lu(G, j, 0))
                    step.link(dve.tensor_scalar(flip[:, :], trial[:, 1:2], 0x7F800000, None, ALU.bitwise_and))
                    step.link(dve.tensor_scalar(normal[:, :], flip[:, :].bitcast(F32), 0.0, None, ALU.is_gt))
                    step.link(dve.tensor_tensor(level, level, normal[:, :], ALU.mult))
                    step.link(dve.tensor_scalar(above[:, 0:nk], sc[1][:, 0:nk], level, None, ALU.is_gt, ALU.add, accum_out=signs[:, :]))
                    step.link(dve.tensor_scalar(below_s, sc[1][:, 0:nk], level, BIG, ALU.is_le, ALU.mult))
                    step.link(dve.scalar_tensor_tensor(out=below_s, in0=sc[1][:, 0:nk], scalar=-1.0e38, in1=below_s,
                                                       op0=ALU.max, op1=ALU.add))
                    step.link(dve.tensor_reduce(next_up[:, :], below_s, AX.X, ALU.min))
                    step.link(dve.tensor_scalar(flip[:, :], signs[:, :], float(NSEL), None, ALU.is_ge))
                    step.link(dve.tensor_scalar(flip[:, :], flip[:, :], 31, 31, ALU.logical_shift_left, ALU.arith_shift_right))
                    step.link(dve.tensor_tensor(next_up[:, :].bitcast(I32), next_up[:, :].bitcast(I32), trial[:, 1:2], ALU.bitwise_xor))
                    step.link(dve.scalar_tensor_tensor(out=trial[:, 1:2], in0=next_up[:, :].bitcast(I32), scalar=flip[:, 0:1], in1=trial[:, 1:2],
                                                       op0=ALU.bitwise_and, op1=ALU.bitwise_xor))
                    for b in range(2):
                        s, m = sc[b][:, 0:nk], mask[b][:, 0:nk]
                        level = trial[:, b:b + 1].bitcast(F32)
                        order = logit[b][:, 0, P:P + nk]
                        dve.tensor_scalar(tie[:, 0:nk], s, level, None, ALU.is_equal)
                        step.link(dve.tensor_scalar(above[:, 0:nk], s, level, None, ALU.is_gt, ALU.add,
                                                    accum_out=count[:, b:b + 1]))
                        dve.wait_ge(S["pv"], 4 + lu(G, j, 0))
                        step.link(dve.tensor_scalar(count[:, b:b + 1], count[:, b:b + 1], -1.0, float(NSEL), ALU.mult, ALU.add))
                        step.link(dve.tensor_tensor_scan(order, tie[:, 0:nk], tie[:, 0:nk], 0.0, ALU.add, ALU.bypass))
                        step.link(dve.scalar_tensor_tensor(out=tie[:, 0:nk], in0=order, scalar=count[:, b:b + 1], in1=tie[:, 0:nk],
                                                           op0=ALU.is_le, op1=ALU.mult))
                        step.link(dve.tensor_tensor(m, above[:, 0:nk], tie[:, 0:nk], ALU.add))
                        if G == 0:
                            step.link(dve.scalar_tensor_tensor(out=m, in0=s, scalar=-BIG, in1=m, op0=ALU.is_gt, op1=ALU.mult))
                        step.link(dve.tensor_scalar(m, m, -1.0, -NEG, ALU.add, ALU.mult))
                    for b in range(2):
                        for h in range(QH):
                            for kc in range(G + 1):
                                n, u = lu(G, j, b, h, kc), h * (G + 1) + kc
                                dve.wait_ge(S["lg"], 4 + n + 1)
                                dve.scalar_tensor_tensor(out=logit[b][:, h, P + kc * 512:P + (kc + 1) * 512], in0=p_lg[u % 2][:, :],
                                                         scalar=rq[:, b, h:h + 1], in1=mask[b][:, kc * 512:(kc + 1) * 512],
                                                         op0=ALU.mult, op1=ALU.add).then_inc(S["lgc"], 1)
                        dve.wait_ge(S["lgc"], 4 + lu(G, j, b + 1))
                        near = logit[b][:, :, ds((i * 2 + b) * P, 256)]
                        step.link(dve.tensor_tensor(near, near, K.near[:, :, :], ALU.add))
                        dve.tensor_reduce(top[:, b, :], logit[b][:, :, P:P + nk], AX.X, ALU.max, negate=True).then_inc(S["max"], 1)
                    for b in range(2):
                        dve.wait_ge(S["exp"], 4 + (i * 2 + b + 1) * QH)
                        step.link(dve.reciprocal(inv[:, b, :], total[:, b, :]))
                        dve.wait_ge(S["pv"], 4 + lu(G, j, b + 1))
                        dve.tensor_tensor(ob[b][:, :, :], p_o[:, :, :], inv[:, b, :].unsqueeze(2).broadcast_to([P, QH, HD]), ALU.mult)\
                           .then_inc(S["norm"], 1)
                    step.leave()


PAIRS = DEC // 2
SIDE = 16
QUARTERS = 4


def step_select(nc, K, idx_cache, page_table):
    with phase(nc, "pick") as (c, stack):
        pid = c.sb("pid", [P, PAIRS], I32)
        pages = [c.sb(f"pages{b}", [P, PAGE // 2, P]) for b in range(2)]
        iqs = c.sb("iqs", [P, IH // 2, 2, DEC])
        bd = c.sb("bd", [P, PAIRS, 2, 2, IH])
        turned = [c.sb(f"turned{b}", [P, 4, P]) for b in range(2)]
        wd, wsel = c.sb("wd", [DEC, DEC, IH]), c.sb("wsel", [P, PAIRS, 2, IH])
        wrow = c.sb("wrow", [P, DEC, IH])
        prod, rel = c.sb("prod", [ID, IH, DEC]), c.sb("rel", [P, DEC, IH])
        snew, sn = c.sb("snew", [P, DEC]), c.sb("sn", [P, PAIRS])
        part = [c.sb(f"part{b}", [P, 8, 2 * IH]) for b in range(2)]
        s, hit, tie, order = (c.sb(n, [P, PAIRS, PAGE]) for n in "s hit tie order".split())
        small = lambda n, dt=F32: c.sb(n, [P, PAIRS], dt)
        row, nhit, count, need, tierow, newtie = (small(n) for n in "row nhit count need tierow newtie".split())
        trial, other, miss = (small(n, I32) for n in "trial other miss".split())
        p_t = [c.ps(f"t{b}", [P, 4, P]) for b in range(2)]
        p_x = [c.ps(f"x{b}", [P, 512]) for b in range(2)]
        p_w, p_c, p_n = c.ps("w", [P, 512]), c.ps("c", [P, 512]), c.ps("n", [P, 512])
        S = {n: c.sem(n) for n in "pid iq bd step turn copy score mul sum wd w rowcount total".split()}
        s_page = c.own_sems("page")
        block = open_block(nc, stack, c)
        cache = idx_cache.rearrange("n p d -> n (p d)")
        UNITS = PAGE // 8

        @block.sync
        def _(sp):
            credit(sp, c)
            table = page_table.rearrange("(i q) c -> q c i", q=2)
            for req in range(2):
                sp.dma_start(pid[req * NPAGE:(req + 1) * NPAGE, :], table[req], allow_slow_non_contiguous=True)\
                  .then_inc(S["pid"], 16)
            for k in range(2):
                for hp in range(2):
                    sp.dma_start(iqs[k * ID:(k + 1) * ID, :, hp, :],
                                 K.d_iq[:, hp * ID:(hp + 1) * ID, SEQ:TOK].rearrange("m d b -> d m b")).then_inc(S["iq"], 16)
            sp.wait_ge(S["iq"], 4 + 64)

        @block.gpsimd
        def _(pool):
            pool.wait_ge(S["pid"], 4 + 32)
            for i in range(PAIRS):
                if i >= 2:
                    pool.wait_ge(S["turn"], 4 + (i - 1) * UNITS)
                pool.indirect_dma_start(pages[i % 2][:, :, :].rearrange("p a b -> p (a b)"), None, cache,
                                        bass.IndirectOffsetOnAxis(ap=pid[:, i:i + 1].bitcast(U32), axis=0)).then_inc(s_page[i % 2], 16)

        @block.tensor
        def _(pe):
            pe.wait_ge(S["wd"], 4 + 1)
            pe.matmul(p_w[:, 0:DEC * IH], K.ones[0:DEC, :], wd[:, :, :].rearrange("r q h -> r (q h)"),
                      start=True, stop=True).then_inc(S["w"], 1)
            pe.wait_ge(S["wd"], 4 + 2)
            pe.matmul(p_n[:, 0:DEC * IH], K.ones[0:ID, :], prod[:, :, :].rearrange("d h r -> d (h r)"),
                      start=True, stop=True).then_inc(S["w"], 1)
            pe.wait_ge(S["bd"], 4 + 1)
            with pe.Fori(0, PAIRS // 2) as j:
                for b in range(2):
                    pe.wait_ge(s_page[b], j * 16 + 16)

                    def turn(u):
                        pe.wait_ge(S["copy"], 4 + (j * 2 + b) * UNITS + u - 1)
                        for k in range(4):
                            last = pe.transpose(p_t[u % 2][:, k, :], pages[b][:, u * 4 + k, :], K.ident[:, :])
                        last.then_inc(S["turn"], 1)
                    turn(0)
                    for u in range(UNITS):
                        n = (j * 2 + b) * UNITS + u
                        if u + 1 < UNITS:
                            turn(u + 1)
                        pe.wait_ge(S["copy"], 4 + n + 1)
                        pe.wait_ge(S["mul"], 4 + n - 1)
                        for k in range(4):
                            last = pe.matmul(p_x[u % 2][:, k * 32:(k + 1) * 32], turned[u % 2][:, k, :],
                                             bd[:, ds(j * 2 + b, 1), :, :, :].rearrange("p i k q h -> p (i k q h)"),
                                             start=True, stop=True)
                        last.then_inc(S["score"], 1)
            for m in range(32 + 1):
                pe.wait_ge(S["rowcount"], 4 + m + 1)
                pe.matmul(p_c[:, 0:PAIRS], K.halves[:, :], row[:, :], start=True, stop=True).then_inc(S["total"], 1)
            pe.wait_ge(S["rowcount"], 4 + 34)
            pe.matmul(p_c[:, 0:PAIRS], K.page_before[:, :], tierow[:, :], start=True, stop=True)
            pe.matmul(p_c[:, PAIRS:2 * PAIRS], K.halves[:, :], tierow[:, :], start=True, stop=True).then_inc(S["total"], 1)

        @block.scalar
        def _(act):
            with act.Fori(0, PAIRS // 2) as j:
                for t in range(UNITS):
                    for b in range(2):
                        n = j * (2 * UNITS) + t * 2 + b
                        act.wait_ge(S["turn"], 4 + n + 1)
                        act.wait_ge(S["score"], 4 + n - 1)
                        act.activation(turned[b][:, :, :], p_t[b][:, :, :], ACT.Copy).then_inc(S["copy"], 1)

        @block.vector
        def _(dve):
            step = Steps(dve, S["step"])
            dve.tensor_copy(K.half[:, 0:1], K.upto[:, NPAGE - 1:NPAGE])
            step.link(dve.tensor_scalar(K.half[:, 1:2], K.upto[:, NPAGE - 1:NPAGE], -1.0, 1.0, ALU.mult, ALU.add))
            step.link(dve.tensor_copy(K.halves[:, :].rearrange("p (q c) -> p q c", q=2),
                                      K.half[:, :].unsqueeze(2).broadcast_to([P, 2, NPAGE])))
            dve.tensor_tensor(K.page_before[:, :], K.halves[:, :], K.before[:, :], ALU.mult)
            step.link(dve.tensor_scalar(wd[:, :, :], K.small[0:DEC, NT, 2 * GH + ID:].unsqueeze(1).broadcast_to([DEC, DEC, IH]),
                                        INDEX_SCALE, None, ALU.mult))
            dve.tensor_tensor(wd[:, :, :], wd[:, :, :], K.ident[0:DEC, 0:DEC].unsqueeze(2).broadcast_to([DEC, DEC, IH]), ALU.mult)\
               .then_inc(S["wd"], 1)
            step.link(dve.memset(bd[:, :, :, :, :], 0.0))
            dve.wait_ge(S["iq"], 4 + 64)
            for k in range(2):
                part_of = slice(k * ID, (k + 1) * ID)
                for req in range(2):
                    last = dve.tensor_copy(bd[part_of, :, k, req, :],
                                           iqs[part_of, :, :, req::2].rearrange("p m q i -> p i (m q)"))
            last.then_inc(S["bd"], 1)
            dve.tensor_tensor(prod[:, :, :], iqs[0:ID, :, :, :].rearrange("p m q r -> p (m q) r"),
                              K.ikt[0:ID, SEQ:TOK].unsqueeze(1).broadcast_to([ID, IH, DEC]), ALU.mult).then_inc(S["wd"], 1)
            dve.wait_ge(S["w"], 4 + 2)
            step.link(dve.tensor_copy(wrow[:, :, :].rearrange("p r h -> p (r h)"), p_w[:, 0:DEC * IH]))
            dve.tensor_tensor(wsel[:, :, :, :].rearrange("p i q h -> p i (q h)"), wrow[:, :, :].rearrange("p (i q) h -> p i (q h)", q=2),
                              K.halves[:, 0:P:P // 16].unsqueeze(1).broadcast_to([P, PAIRS, 16]), ALU.mult)
            step.link(dve.scalar_tensor_tensor(out=rel[:, :, :], in0=p_n[:, 0:DEC * IH].rearrange("p (h r) -> p r h", h=IH), scalar=0.0,
                                               in1=wrow[:, :, :], op0=ALU.max, op1=ALU.mult))
            step.link(dve.tensor_reduce(snew[:, :], rel[:, :, :], AX.X, ALU.add))
            step.link(dve.tensor_tensor(snew[:, :].rearrange("p (i q) -> p i q", q=2), snew[:, :].rearrange("p (i q) -> p i q", q=2),
                                        K.half[:, :].unsqueeze(1).broadcast_to([P, PAIRS, 2]), ALU.mult))
            step.link(dve.tensor_reduce(sn[:, :], snew[:, :].rearrange("p (i q) -> p i q", q=2), AX.X, ALU.add))
            with dve.Fori(0, PAIRS // 2) as j:
                for i in range(2):
                    w = wsel[:, ds(j * 2 + i, 1), :, :].rearrange("p i q h -> p i (q h)").broadcast_to([P, 8, 2 * IH])
                    for t in range(UNITS // 2):
                        for b in range(2):
                            n = (j * 2 + i) * UNITS + t * 2 + b
                            dve.wait_ge(S["score"], 4 + n + 1)
                            dve.wait_ge(S["sum"], 4 + n - 1)
                            dve.scalar_tensor_tensor(out=part[b][:, :, :], in0=p_x[b][:, 0:128].rearrange("p (k w) -> p k w", k=8),
                                                     scalar=0.0, in1=w, op0=ALU.max, op1=ALU.mult).then_inc(S["mul"], 1)
                        for b in range(2):
                            n = (j * 2 + i) * UNITS + t * 2 + b
                            dve.wait_ge(S["mul"], 4 + n + 1)
                            dve.tensor_reduce(s[:, ds(j * 2 + i, 1), (t * 2 + b) * 8:(t * 2 + b + 1) * 8], part[b][:, :, :],
                                              AX.X, ALU.add).then_inc(S["sum"], 1)
            dve.wait_ge(S["sum"], 4 + PAIRS * UNITS)
            wide = [P, PAIRS, PAGE]

            def tally(level, m):
                dve.tensor_tensor(nhit[:, :], sn[:, :], level, ALU.is_ge)
                step.link(dve.tensor_tensor(hit[:, :, :], s[:, :, :], level.unsqueeze(2).broadcast_to(wide), ALU.is_ge))
                dve.tensor_reduce(row[:, :], hit[:, :, :], AX.X, ALU.add).then_inc(S["rowcount"], 1)
                dve.wait_ge(S["total"], 4 + m + 1)
                step.link(dve.tensor_tensor(count[:, :], p_c[:, 0:PAIRS], nhit[:, :], ALU.add))
            step.link(dve.memset(trial[:, :].bitcast(F32), 0.0))
            tally(trial[:, :].bitcast(F32), 0)
            step.link(dve.tensor_scalar(miss[:, :], count[:, :], float(NSEL), None, ALU.is_lt))
            step.link(dve.tensor_scalar(trial[:, :], miss[:, :], 31, 31, ALU.logical_shift_left, ALU.arith_shift_right))
            step.link(dve.tensor_scalar(trial[:, :], trial[:, :], 1 << 30, None, ALU.bitwise_xor))
            for bit in range(30, -1, -1):
                if bit:
                    dve.tensor_scalar(other[:, :], trial[:, :], 1 << (bit - 1), None, ALU.bitwise_xor)
                else:
                    dve.tensor_copy(other[:, :], trial[:, :])
                tally(trial[:, :].bitcast(F32), 31 - bit)
                step.link(dve.tensor_scalar(miss[:, :], count[:, :], float(NSEL), None, ALU.is_lt))
                step.link(dve.scalar_tensor_tensor(out=trial[:, :], in0=miss[:, :], scalar=bit, in1=other[:, :],
                                                   op0=ALU.logical_shift_left, op1=ALU.bitwise_xor))
            level = trial[:, :].bitcast(F32)
            dve.tensor_tensor(nhit[:, :], sn[:, :], level, ALU.is_gt)
            dve.tensor_tensor(newtie[:, :], sn[:, :], level, ALU.is_equal)
            dve.tensor_tensor(tie[:, :, :], s[:, :, :], level.unsqueeze(2).broadcast_to(wide), ALU.is_equal)
            step.link(dve.tensor_tensor(hit[:, :, :], s[:, :, :], level.unsqueeze(2).broadcast_to(wide), ALU.is_gt))
            dve.tensor_reduce(row[:, :], hit[:, :, :], AX.X, ALU.add).then_inc(S["rowcount"], 1)
            dve.tensor_reduce(tierow[:, :], tie[:, :, :], AX.X, ALU.add)
            for i in range(PAIRS):
                last = dve.tensor_tensor_scan(order[:, i, :], tie[:, i, :], tie[:, i, :], 0.0, ALU.add, ALU.bypass)
            dve.wait_ge(S["total"], 4 + 33)
            step.link(dve.tensor_tensor(count[:, :], p_c[:, 0:PAIRS], nhit[:, :], ALU.add))
            last = dve.tensor_scalar(need[:, :], count[:, :], -1.0, float(NSEL), ALU.mult, ALU.add)
            last.then_inc(S["rowcount"], 1)
            dve.wait_ge(S["rowcount"], 4 + 34)
            dve.wait_ge(S["total"], 4 + 34)
            step.link(dve.tensor_tensor(row[:, :], need[:, :], p_c[:, 0:PAIRS], ALU.subtract))
            step.link(dve.tensor_tensor(order[:, :, :], order[:, :, :], row[:, :].unsqueeze(2).broadcast_to(wide), ALU.is_le))
            step.link(dve.tensor_tensor(order[:, :, :], order[:, :, :], tie[:, :, :], ALU.mult))
            step.link(dve.tensor_tensor(K.taken[:, :, :], order[:, :, :], hit[:, :, :], ALU.add))
            step.link(dve.tensor_tensor(count[:, :], p_c[:, PAIRS:2 * PAIRS], need[:, :], ALU.is_lt))
            step.link(dve.tensor_tensor(count[:, :], count[:, :], newtie[:, :], ALU.mult))
            step.link(dve.tensor_tensor(K.new_taken[:, :], count[:, :], nhit[:, :], ALU.add))


def step_slots(nc, K, page_table):
    VALS = 4
    with phase(nc, "slot") as (c, stack):
        pid, part = c.sb("pid", [P, PAIRS], I32), c.sb("part", [P, 2, PAIRS], I32)
        side = c.sb("side", [P, SIDE])
        nextkey = c.sb("nextkey", [P, PAGE])
        page = c.sb("page", [P, 1])
        rank = c.sb("rank", [P, PAIRS, PAGE])
        ranki, ab = c.sb("ranki", [P, PAIRS, PAGE], I32), c.sb("ab", [P, 2, PAIRS, PAGE], I32)
        a, b_ = c.sb("a", [P, PAIRS, PAGE]), c.sb("b", [P, PAIRS, PAGE])
        row, offset = c.sb("row", [P, PAIRS]), c.sb("offset", [P, PAIRS])
        val = c.sb("val", [P, PAIRS, VALS - 1])
        hot = [c.sb(f"hot{b}", [P, PAGE, SIDE], BF16) for b in range(2)]
        left = [c.sb(f"left{b}", [P, PAGE, 2, SIDE], BF16) for b in range(2)]
        right = [c.sb(f"right{b}", [P, PAGE, VALS, SIDE], BF16) for b in range(2)]
        boxes = c.sb("boxes", [2 * SIDE, VALS, PAIRS, SIDE])
        spread = c.sb("spread", [2 * SIDE, QUARTERS, P])
        own = c.sb("own", [P, SIDE])
        picked = c.sb("picked", [P, QUARTERS, VALS * PAIRS, SIDE])
        got = c.sb("got", [P, QUARTERS, VALS, PAIRS])
        at = c.sb("at", [P, QUARTERS, PAIRS])
        p_r, p_box = c.ps("r", [P, 512]), c.ps("box", [2 * SIDE, PAIRS, P])
        p_s = c.ps("s", [P, QUARTERS, VALS * PAIRS * SIDE])
        S = {n: c.sem(n) for n in "pid iota cut spread step rows before boxed box boxes spreadmm".split()}
        s_left, s_right = c.sems("left"), c.sems("right")
        block = open_block(nc, stack, c)

        @block.sync
        def _(sp):
            credit(sp, c)
            table = page_table.rearrange("(i q) c -> q c i", q=2)
            for req in range(2):
                sp.dma_start(pid[req * NPAGE:(req + 1) * NPAGE, :], table[req], allow_slow_non_contiguous=True)\
                  .then_inc(S["pid"], 16)
            sp.wait_ge(S["pid"], 4 + 32)

        @block.gpsimd
        def _(pool):
            pool.iota(side[:, :], pattern=[[1, SIDE]], base=0, channel_multiplier=0, allow_small_or_imprecise_dtypes=True)
            pool.iota(nextkey[:, :], pattern=[[1, PAGE]], base=1, channel_multiplier=0, allow_small_or_imprecise_dtypes=True)
            pool.iota(page[:, :], pattern=[[0, 1]], base=0, channel_multiplier=1, allow_small_or_imprecise_dtypes=True)\
                .then_inc(S["iota"], 1)
            pool.memset(spread[:, :, :], 1.0).then_inc(S["cut"], 1)
            v = spread[:, :, :].rearrange("k m p -> k (m p)")
            pool.wait_ge(S["cut"], 4 + 1)
            pool.affine_select(out=v, in_=v, compare_op=ALU.is_ge, fill=0.0, base=0, pattern=[[1, QUARTERS * P]],
                               channel_multiplier=-SIDE).then_inc(S["cut"], 1)
            pool.wait_ge(S["cut"], 4 + 2)
            pool.affine_select(out=v, in_=v, compare_op=ALU.is_ge, fill=0.0, base=SIDE - 1, pattern=[[-1, QUARTERS * P]],
                               channel_multiplier=SIDE).then_inc(S["spread"], 1)

        @block.tensor
        def _(pe):
            pe.wait_ge(S["rows"], 4 + 1)
            pe.matmul(p_r[:, 0:PAIRS], K.page_before[:, :], row[:, :], start=True, stop=True).then_inc(S["before"], 1)
            for i in range(PAIRS):
                pe.wait_ge(s_left[i % 2], 4 + i // 2 + 1)
                pe.wait_ge(s_right[i % 2], 4 + i // 2 + 1)
                for k in range(PAGE):
                    last = pe.matmul(p_box[:, i, 0:VALS * SIDE], left[i % 2][:, k, :, :].rearrange("p q a -> p (q a)"),
                                     right[i % 2][:, k, :, :].rearrange("p v b -> p (v b)"), start=(k == 0), stop=(k == PAGE - 1))
                last.then_inc(S["box"], 1)
            pe.wait_ge(S["boxes"], 4 + 1)
            pe.wait_ge(S["spread"], 4 + 1)
            for m in range(QUARTERS):
                last = pe.matmul(p_s[:, m, :], spread[:, m, :], boxes[:, :, :, :].rearrange("k v i b -> k (v i b)"), start=True, stop=True)
            last.then_inc(S["spreadmm"], 1)

        @block.vector
        def _(dve):
            step = Steps(dve, S["step"])
            wide = [P, PAIRS, PAGE]
            dve.tensor_reduce(row[:, :], K.taken[:, :, :], AX.X, ALU.add).then_inc(S["rows"], 1)
            for i in range(PAIRS):
                last = dve.tensor_tensor_scan(rank[:, i, :], K.taken[:, i, :], K.taken[:, i, :], 0.0, ALU.add, ALU.bypass)
            dve.tensor_reduce(own[:, :], K.ident[:, :].rearrange("p (a b) -> p b a", b=SIDE), AX.X, ALU.add)
            dve.wait_ge(S["iota"], 4 + 1)
            step.link(dve.scalar_tensor_tensor(out=page[:, :], in0=K.half[:, 1:2], scalar=-float(NPAGE), in1=page[:, :],
                                               op0=ALU.mult, op1=ALU.add))
            dve.wait_ge(S["pid"], 4 + 32)
            dve.tensor_scalar(part[:, 0, :], pid[:, :], 3, None, ALU.logical_shift_right)
            step.link(dve.tensor_scalar(part[:, 1, :], pid[:, :], 7, None, ALU.bitwise_and))
            dve.tensor_copy(val[:, :, 0], page[:, 0:1].broadcast_to([P, PAIRS]))
            step.link(dve.tensor_copy(val[:, :, 1:3], part[:, :, :].rearrange("p v i -> p i v")))
            dve.wait_ge(S["before"], 4 + 1)
            step.link(dve.tensor_scalar(offset[:, :], p_r[:, 0:PAIRS], -1.0, None, ALU.add))
            step.link(dve.tensor_tensor(ranki[:, :, :], rank[:, :, :], offset[:, :].unsqueeze(2).broadcast_to(wide), ALU.add))
            dve.tensor_scalar(ab[:, 0, :, :], ranki[:, :, :], 4, None, ALU.arith_shift_right)
            step.link(dve.tensor_scalar(ab[:, 1, :, :], ranki[:, :, :], 15, None, ALU.bitwise_and))
            step.link(dve.scalar_tensor_tensor(out=a[:, :, :], in0=ab[:, 0, :, :], scalar=1.0, in1=K.taken[:, :, :],
                                               op0=ALU.add, op1=ALU.mult))
            dve.tensor_copy(b_[:, :, :], ab[:, 1, :, :])
            step.link(dve.tensor_scalar(a[:, :, :], a[:, :, :], -1.0, None, ALU.add))
            sides = side[:, :].unsqueeze(1).broadcast_to([P, PAGE, SIDE])
            for i in range(PAIRS):
                if i >= 2:
                    dve.wait_ge(S["box"], 4 + i - 1)
                step.link(dve.tensor_tensor(hot[0][:, :, :], a[:, i, :].unsqueeze(2).broadcast_to([P, PAGE, SIDE]), sides, ALU.is_equal))
                for req in range(2):
                    last = dve.tensor_scalar(left[i % 2][:, :, req, :], hot[0][:, :, :], K.half[:, req:req + 1], None, ALU.mult)
                last.then_inc(s_left[i % 2], 1)
                step.link(dve.tensor_tensor(hot[1][:, :, :], b_[:, i, :].unsqueeze(2).broadcast_to([P, PAGE, SIDE]), sides, ALU.is_equal))
                dve.tensor_tensor(right[i % 2][:, :, 0, :], hot[1][:, :, :], nextkey[:, :].unsqueeze(2).broadcast_to([P, PAGE, SIDE]), ALU.mult)
                for v in range(1, VALS):
                    last = dve.tensor_scalar(right[i % 2][:, :, v, :], hot[1][:, :, :], val[:, i, v - 1:v], None, ALU.mult)
                last.then_inc(s_right[i % 2], 1)
            dve.wait_ge(S["box"], 4 + PAIRS)
            dve.tensor_copy(boxes[:, :, :, :], p_box[:, :, 0:VALS * SIDE].rearrange("k i (v b) -> k v i b", v=VALS))\
               .then_inc(S["boxes"], 1)
            dve.wait_ge(S["spreadmm"], 4 + 1)
            mine = own[:, :].unsqueeze(1).broadcast_to([P, VALS * PAIRS, SIDE])
            for m in range(QUARTERS):
                last = dve.tensor_tensor(picked[:, m, :, :], p_s[:, m, :].rearrange("p (n b) -> p n b", b=SIDE), mine, ALU.mult)
            step.link(last)
            step.link(dve.tensor_reduce(got[:, :, :, :].rearrange("p m v i -> p m (v i)"), picked[:, :, :, :], AX.X, ALU.add))
            key1, pg, hi, lo = (got[:, :, v, :] for v in range(VALS))
            step.link(dve.tensor_scalar(at[:, :, :], key1, -1.0, 0.0, ALU.add, ALU.max))
            step.link(dve.scalar_tensor_tensor(out=hi, in0=hi, scalar=8.0, in1=lo, op0=ALU.mult, op1=ALU.add))
            dve.scalar_tensor_tensor(out=K.row[:, :, :], in0=hi, scalar=float(PAGE), in1=at[:, :, :], op0=ALU.mult, op1=ALU.add)
            dve.tensor_scalar(K.empty[:, :, :], key1, 1.0, NEG, ALU.is_lt, ALU.mult)
            step.link(dve.scalar_tensor_tensor(out=at[:, :, :], in0=pg, scalar=float(PAGE), in1=at[:, :, :], op0=ALU.mult, op1=ALU.add))
            step.link(dve.tensor_scalar(K.dist[:, :, :], at[:, :, :], -1.0, float(PAST), ALU.mult, ALU.add))


def step_attend(nc, K, cache_k, cache_v, q_norm):
    NC = DEC * QH
    with phase(nc, "satt") as (c, stack):
        kg, vg = c.sb("kg", [P, QUARTERS, PAIRS, KVH * HD]), c.sb("vg", [P, QUARTERS, PAIRS, KVH * HD])
        kt = c.sb("kt", [P, QUARTERS * PAIRS, KVH, P])
        q, qsq, inv = (c.sb(n, [P, QH, DEC]) for n in "q qsq inv".split())
        gain, own_bias = c.sb("gain", [P, 1]), c.sb("own_bias", [P, QH])
        nprod, ln = c.sb("nprod", [P, 2, PAIRS, QH]), c.sb("ln", [P, 2, PAIRS, QH])
        nmask = c.sb("nmask", [P, 2, PAIRS])
        starts = c.sb("starts", [P, BUCKETS])
        diff = c.sb("diff", [P, BUCKETS, QH])
        ge, part = c.sb("ge", [P, QUARTERS * PAIRS, BUCKETS]), c.sb("part", [P, QUARTERS * PAIRS, BUCKETS])
        bias = c.sb("bias", [P, QUARTERS * PAIRS, QH])
        lg = c.sb("lg", [P, 2, 2, PAIRS, QH])
        top, mx, tot, share = (c.sb(n, [P, 2, PAIRS, QH]) for n in "top mx tot share".split())
        tall, dgm = c.sb("tall", [NC, 1]), c.sb("dgm", [NC, NC])
        vnew = c.sb("vnew", [P, KVH, DEC])
        out = c.sb("out", [P, QH, DEC])
        p_t = [c.ps(f"t{b}", [P, 4, P]) for b in range(2)]
        p_l, p_o, p_a, p_b, p_v = (c.ps(n, [P, 512]) for n in "l o a b v".split())
        S = {n: c.sem(n) for n in ("q sq ss gainq starts step newp newl turn copy used maxed mturn diag "
                                   "mxb sub exp pv sums tot out st").split()}
        s_k, s_v = c.own_sems("k", 1)[0], c.own_sems("v", 1)[0]
        block = open_block(nc, stack, c)
        ks = cache_k.rearrange("l n k g d -> (l n k) (g d)")
        vs = cache_v.rearrange("l n k g d -> (l n k) (g d)")
        flat = lambda t: t[:, :, :, :].rearrange("p q i h -> p (q i h)")
        by_req = lambda ap: ap.rearrange("p (i q) -> p q i", q=2)

        @block.sync
        def _(sp):
            credit(sp, c)
            sp.dma_start(q[:, :, :], K.d_q[:, :, SEQ:TOK].rearrange("m p r -> p m r")).then_inc(S["q"], 16)
            sp.dma_start(gain[:, :], q_norm.rearrange("(p o) -> p o", o=1)).then_inc(S["q"], 16)
            sp.wait_ge(S["out"], 4 + 1)
            sp.dma_start(K.d_mix[GH:, :, SEQ:TOK].rearrange("m p r -> p m r"), out[:, :, :]).then_inc(S["st"], 16)
            sp.wait_ge(S["st"], 4 + 16)

        @block.gpsimd
        def _(pool):
            for src, buf, sem in ((ks, kg, s_k), (vs, vg, s_v)):
                for m in range(QUARTERS):
                    for i in range(PAIRS):
                        pool.indirect_dma_start(buf[:, m, i, :], None, src,
                                                bass.IndirectOffsetOnAxis(ap=K.row[:, m, i:i + 1].bitcast(U32), axis=0)).then_inc(sem, 16)

        @block.tensor
        def _(pe):
            pe.wait_ge(S["sq"], 4 + 1)
            pe.matmul(p_a[:, 0:NC], K.ones[:, :], qsq[:, :, :].rearrange("p h r -> p (h r)"), start=True, stop=True)\
              .then_inc(S["ss"], 1)
            pe.wait_ge(S["newp"], 4 + 1)
            pe.matmul(p_a[:, 0:NC], K.ones[:, :], flat(nprod), start=True, stop=True)
            pe.matmul(p_a[:, NC:NC + DEC], K.ones[:, :], nmask[:, :, :].rearrange("p q i -> p (q i)"), start=True, stop=True)
            for g in range(KVH):
                last = pe.transpose(p_v[:, g * P:(g + 1) * P], K.v[:, NT, g * HD:(g + 1) * HD], K.ident[:, :])
            last.then_inc(S["newl"], 1)
            pe.wait_ge(s_k, 16 * QUARTERS * PAIRS)
            rows = kg[:, :, :, :].rearrange("p m i n -> p (m i) n")

            def turn(u):
                pe.wait_ge(S["copy"], 4 + u - 1)
                for k in range(2):
                    for g in range(KVH):
                        last = pe.transpose(p_t[u % 2][:, k * 2 + g, :], rows[:, u * 2 + k, g * HD:(g + 1) * HD], K.ident[:, :])
                last.then_inc(S["turn"], 1)
            UNITS = QUARTERS * PAIRS // 2
            turn(0)
            for u in range(UNITS):
                if u + 1 < UNITS:
                    turn(u + 1)
                pe.wait_ge(S["copy"], 4 + u + 1)
                for k in range(2):
                    m, i = divmod(u * 2 + k, PAIRS)
                    r = i * 2 + m // 2
                    for g in range(KVH):
                        col = (u * 2 + k) * QH + g * GROUP
                        last = pe.matmul(p_l[:, col:col + GROUP], kt[:, u * 2 + k, g, :], q[:, g * GROUP:(g + 1) * GROUP, r],
                                         start=True, stop=True)
            last.then_inc(S["used"], 1)
            pe.wait_ge(S["maxed"], 4 + 1)
            pe.transpose(p_b[0:NC, 0:P], flat(top), K.ident[:, :]).then_inc(S["mturn"], 1)
            pe.wait_ge(S["diag"], 4 + 1)
            pe.matmul(p_a[:, 0:NC], K.ones[0:NC, :], dgm[:, :], start=True, stop=True).then_inc(S["mxb"], 1)
            pe.wait_ge(S["exp"], 4 + 1)
            pe.wait_ge(s_v, 16 * QUARTERS * PAIRS)
            for req in range(2):
                for i in range(PAIRS):
                    for g in range(KVH):
                        col = (req * PAIRS + i) * QH + g * GROUP
                        for u in range(2):
                            last = pe.matmul(p_o[:, col:col + GROUP], vg[:, req * 2 + u, i, g * HD:(g + 1) * HD],
                                             lg[:, req, u, i, g * GROUP:(g + 1) * GROUP], start=(u == 0), stop=(u == 1))
            last.then_inc(S["pv"], 1)
            pe.wait_ge(S["sums"], 4 + 1)
            pe.matmul(p_a[:, 0:NC], K.ones[:, :], flat(tot), start=True, stop=True).then_inc(S["tot"], 1)

        @block.scalar
        def _(act):
            act.wait_ge(S["q"], 4 + 32)
            act.activation(qsq[:, :, :], q[:, :, :], ACT.Square).then_inc(S["sq"], 1)
            act.wait_ge(S["gainq"], 4 + 1)
            act.activation(inv[:, :, :], inv[:, :, :], ACT.Sqrt).then_inc(S["gainq"], 1)
            for u in range(QUARTERS * PAIRS // 2):
                act.wait_ge(S["turn"], 4 + u + 1)
                act.activation(kt[:, u * 2:u * 2 + 2, :, :].rearrange("p k g n -> p (k g) n"), p_t[u % 2][:, :, :], ACT.Copy)\
                   .then_inc(S["copy"], 1)
            act.wait_ge(S["sub"], 4 + 1)
            act.activation(ln[:, :, :, :], ln[:, :, :, :], ACT.Exp)
            act.activation(lg[:, :, :, :, :].rearrange("p q u i h -> p (q u i h)"), lg[:, :, :, :, :].rearrange("p q u i h -> p (q u i h)"),
                           ACT.Exp).then_inc(S["exp"], 1)

        @block.vector
        def _(dve):
            step = Steps(dve, S["step"])
            for b, start in enumerate(bucket_starts()):
                dve.memset(starts[:, b:b + 1], float(start) if b else -1.0)
            dve.tensor_tensor(diff[:, 1:, :], K.rb[:, 1:, :], K.rb[:, :-1, :], ALU.subtract)
            dve.tensor_tensor(diff[:, 0, :], K.rb[:, 0, :], K.rb[:, BUCKETS - 1, :], ALU.subtract)
            step.link(dve.tensor_tensor(own_bias[:, :], K.rb[:, 0, :], K.rb[:, BUCKETS - 1, :], ALU.subtract))
            dve.wait_ge(S["ss"], 4 + 1)
            iflat = inv[:, :, :].rearrange("p h r -> p (h r)")
            step.link(dve.tensor_scalar(iflat, p_a[:, 0:NC], 1.0 / HD, EPS, ALU.mult, ALU.add))
            dve.reciprocal(iflat, iflat).then_inc(S["gainq"], 1)
            dve.wait_ge(S["gainq"], 4 + 2)
            step.link(dve.scalar_tensor_tensor(out=q[:, :, :], in0=q[:, :, :], scalar=gain[:, 0:1], in1=inv[:, :, :],
                                               op0=ALU.mult, op1=ALU.mult))
            step.link(dve.tensor_scalar(q[:, :, :], q[:, :, :], SCALE, None, ALU.mult))
            for h in range(QH):
                dve.tensor_tensor(nprod[:, :, :, h], by_req(q[:, h, :]), by_req(K.kt[:, h // GROUP, SEQ:TOK]), ALU.mult)
            dve.tensor_tensor(nmask[:, :, :], K.new_taken[:, :].unsqueeze(1).broadcast_to([P, 2, PAIRS]),
                              K.ident[:, 0:P:NPAGE].unsqueeze(2).broadcast_to([P, 2, PAIRS]), ALU.mult).then_inc(S["newp"], 1)
            step.link(dve.tensor_tensor(ge[:, :, :], K.dist[:, :, :].rearrange("p m i -> p (m i)").unsqueeze(2)
                                        .broadcast_to([P, QUARTERS * PAIRS, BUCKETS]),
                                        starts[:, :].unsqueeze(1).broadcast_to([P, QUARTERS * PAIRS, BUCKETS]), ALU.is_ge))
            for h in range(QH):
                step.link(dve.tensor_tensor(part[:, :, :], ge[:, :, :], diff[:, :, h].unsqueeze(1).broadcast_to([P, QUARTERS * PAIRS, BUCKETS]),
                                            ALU.mult))
                step.link(dve.tensor_reduce(bias[:, :, h], part[:, :, :], AX.X, ALU.add))
            step.link(dve.tensor_tensor(bias[:, :, :], bias[:, :, :], K.empty[:, :, :].rearrange("p m i -> p (m i)").unsqueeze(2)
                                        .broadcast_to([P, QUARTERS * PAIRS, QH]), ALU.add))
            dve.wait_ge(S["newl"], 4 + 1)
            step.link(dve.tensor_scalar(nmask[:, :, :].rearrange("p q i -> p (q i)"), p_a[:, NC:NC + DEC], -1.0, -NEG, ALU.add, ALU.mult))
            step.link(dve.tensor_tensor(ln[:, :, :, :].rearrange("p q i h -> p (q i) h"), p_a[:, 0:NC].rearrange("p (n h) -> p n h", h=QH),
                                        own_bias[:, :].unsqueeze(1).broadcast_to([P, DEC, QH]), ALU.add))
            step.link(dve.tensor_tensor(ln[:, :, :, :].rearrange("p q i h -> p (q i) h"), ln[:, :, :, :].rearrange("p q i h -> p (q i) h"),
                                        nmask[:, :, :].rearrange("p q i -> p (q i)").unsqueeze(2).broadcast_to([P, DEC, QH]), ALU.add))
            step.link(dve.tensor_copy(vnew[:, :, :], p_v[:, 0:2 * P].rearrange("p (g n) -> p g n", g=KVH)[:, :, 0:DEC]))
            dve.wait_ge(S["used"], 4 + 1)
            step.link(dve.tensor_tensor(lg[:, :, :, :, :].rearrange("p q u i h -> p (q u i h)"), p_l[:, 0:2 * NC],
                                        bias[:, :, :].rearrange("p n h -> p (n h)"), ALU.add))
            half = [lg[:, :, u, :, :].rearrange("p q i h -> p q (i h)") for u in range(2)]
            pair = lambda t: t[:, :, :, :].rearrange("p q i h -> p q (i h)")
            step.link(dve.tensor_tensor(pair(top), half[0], half[1], ALU.max))
            dve.tensor_tensor(pair(top), pair(top), pair(ln), ALU.max).then_inc(S["maxed"], 1)
            dve.wait_ge(S["mturn"], 4 + 1)
            step.link(dve.tensor_reduce(tall[:, :], p_b[0:NC, 0:P], AX.X, ALU.max))
            dve.tensor_scalar(dgm[:, :], K.ident[0:NC, 0:NC], tall[:, 0:1], None, ALU.mult).then_inc(S["diag"], 1)
            dve.wait_ge(S["mxb"], 4 + 1)
            step.link(dve.tensor_copy(flat(mx), p_a[:, 0:NC]))
            for u in range(2):
                dve.tensor_tensor(half[u], half[u], pair(mx), ALU.subtract)
            dve.tensor_tensor(pair(ln), pair(ln), pair(mx), ALU.subtract).then_inc(S["sub"], 1)
            dve.wait_ge(S["exp"], 4 + 1)
            dve.tensor_tensor(pair(tot), half[0], half[1], ALU.add).then_inc(S["sums"], 1)
            for h in range(QH):
                last = dve.tensor_tensor(share[:, :, :, h], ln[:, :, :, h], by_req(vnew[:, h // GROUP, :]), ALU.mult)
            step.link(last)
            dve.wait_ge(S["pv"], 4 + 1)
            step.link(dve.tensor_tensor(flat(share), flat(share), p_o[:, 0:NC], ALU.add))
            dve.wait_ge(S["tot"], 4 + 1)
            step.link(dve.tensor_tensor(flat(tot), p_a[:, 0:NC], flat(ln), ALU.add))
            step.link(dve.reciprocal(flat(tot), flat(tot)))
            for h in range(QH):
                last = dve.tensor_tensor(by_req(out[:, h, :]), share[:, :, :, h], tot[:, :, :, h], ALU.mult)
            last.then_inc(S["out"], 1)


def mix(nc, K, x_prompt, x_sample, w_out, norm_ffn):
    with phase(nc, "mix") as (c, stack):
        two = lambda name, shape, dt=F32: [c.sb(f"{name}{b}", shape, dt) for b in range(2)]
        w = c.sb("w", [P, KD, D])
        m, x, xn = two("m", [P, KD, P]), two("x", [P, D]), two("xn", [P, D])
        junk, h = c.sb("junk", [P, D], BF16), c.sb("h", [P, KD, P])
        stat = two("stat", [P, 4])
        gain = c.sb("gain", [P, KD])
        p_y = [c.ps(f"y{b}", [P, 2, 512]) for b in range(2)]
        p_t = [c.ps(f"t{b}", [P, KD, P]) for b in range(2)]
        s_w = c.sem("w")
        s_m, s_x, s_mm, s_x2, s_sum, s_mean, s_root, s_inv, s_norm, s_turn, s_ht, s_st = (
            c.sems(n) for n in "m x mm x2 sum mean root inv norm turn ht st".split())
        s_high, s_low = c.sem("high"), c.sem("low")
        block = open_block(nc, stack, c)
        LAST = NT // 2

        @block.sync
        def _(sp):
            credit(sp, c)
            sp.dma_start(gain[:, :], norm_ffn.rearrange("(k p) -> p k", p=P), allow_slow_non_contiguous=True)\
              .then_inc(s_w, 16)

            def load(j, b, n=P):
                rows = ds(j * 256 + b * P, P) if n == P else slice(SEQ, TOK)
                sp.wait_ge(s_mm[b], 4 + j)
                sp.dma_start(m[b][:, :, 0:n], K.d_mix[:, :, rows].rearrange("k p n -> p k n")).then_inc(s_m[b], 16)
                sp.wait_ge(s_norm[b], 4 + j)
                sp.wait_ge(s_st[b], 4 + j * 16)
                sp.dma_start(x[b][0:n, :], x_prompt[rows, :] if n == P else x_sample).then_inc(s_x[b], 16)

            def store(j, b, n=P):
                rows = ds(j * 256 + b * P, P) if n == P else slice(SEQ, TOK)
                sp.wait_ge(s_x2[b], 4 + j + 1)
                sp.dma_start(K.d_x2[rows, :], x[b][0:n, :]).then_inc(s_st[b], 16)
            load(0, 0)
            load(0, 1)
            with sp.Fori(0, LAST - 1) as j:
                for b in range(2):
                    store(j, b)
                    load(j + 1, b)
            store(LAST - 1, 0)
            load(LAST, 0, DEC)
            store(LAST - 1, 1)
            store(LAST, 0, DEC)
            sp.wait_ge(s_st[0], 4 + (LAST + 1) * 16)
            sp.wait_ge(s_st[1], 4 + LAST * 16)

        @block.tensor
        def _(pe):
            def multiply(j, b):
                pe.wait_ge(s_m[b], 4 + j * 16 + 16)
                pe.wait_ge(s_x2[b], 4 + j)
                for k in range(KD):
                    for half in range(2):
                        last = pe.matmul(p_y[b][:, half, :], m[b][:, k, :], w[:, k, half * 512:(half + 1) * 512],
                                         start=(k == 0), stop=(k == KD - 1))
                last.then_inc(s_mm[b], 1)

            def turn(j, b):
                pe.wait_ge(s_norm[b], 4 + j + 1)
                pe.wait_ge(s_ht[b], 4 + j)
                for k in range(KD):
                    last = pe.transpose(p_t[b][:, k, :], xn[b][:, k * P:(k + 1) * P], K.ident[:, :])
                last.then_inc(s_turn[b], 1)
            pe.wait_ge(s_w, 4 + 32)
            multiply(0, 0)
            with pe.Fori(0, LAST) as j:
                multiply(j, 1)
                turn(j, 0)
                multiply(j + 1, 0)
                turn(j, 1)
            turn(LAST, 0)

        @block.scalar
        def _(act):
            act.dma_start(w[:, :, :], w_out.rearrange("(k p) n -> p k n", p=P)).then_inc(s_w, 16)

            def stats(j, b):
                act.wait_ge(s_x2[b], 4 + j + 1)
                act.activation(junk[:, :], x[b][:, :], ACT.Square, accum_out=stat[b][:, 0:1]).then_inc(s_sum[b], 1)
                act.wait_ge(s_mean[b], 4 + j + 1)
                act.activation(stat[b][:, 2:3], stat[b][:, 1:2], ACT.Sqrt).then_inc(s_root[b], 1)

            def high(j, b, n=P):
                act.wait_ge(s_ht[b], 4 + j + 1)
                act.activation(K.ht[:, :, ds(j * 256 + b * P, n)], h[:, :, 0:n], ACT.Copy).then_inc(s_high, 1)
            stats(0, 0)
            with act.Fori(0, LAST) as j:
                stats(j, 1)
                high(j, 0)
                stats(j + 1, 0)
                high(j, 1)
            high(LAST, 0, DEC)

        @block.gpsimd
        def _(pool):
            def low(j, b, n=P):
                cols = ds(j * 256 + b * P, n)
                pool.wait_ge(s_high, 4 + j * 2 + b + 1)
                pool.tensor_tensor(K.hl[:, :, cols], h[:, :, 0:n], K.ht[:, :, cols].bitcast(F32), ALU.subtract).then_inc(s_low, 1)
            with pool.Fori(0, LAST) as j:
                low(j, 0)
                low(j, 1)
            low(LAST, 0, DEC)

        @block.vector
        def _(dve):
            dve.wait_ge(s_w, 4 + 32)

            def norm(j, b):
                dve.wait_ge(s_x[b], 4 + j * 16 + 16)
                dve.wait_ge(s_mm[b], 4 + j + 1)
                dve.tensor_tensor(x[b][:, :], p_y[b][:, :, :].rearrange("p a n -> p (a n)"), x[b][:, :], ALU.add)\
                   .then_inc(s_x2[b], 1)
                dve.wait_ge(s_sum[b], 4 + j + 1)
                dve.tensor_scalar(stat[b][:, 1:2], stat[b][:, 0:1], 1.0 / D, EPS, ALU.mult, ALU.add).then_inc(s_mean[b], 1)
                dve.wait_ge(s_root[b], 4 + j + 1)
                dve.reciprocal(stat[b][:, 3:4], stat[b][:, 2:3]).then_inc(s_inv[b], 1)
                dve.wait_ge(s_inv[b], 4 + j + 1)
                dve.wait_ge(s_turn[b], 4 + j)
                dve.tensor_scalar(xn[b][:, :], x[b][:, :], stat[b][:, 3:4], None, ALU.mult).then_inc(s_norm[b], 1)

            def scale(j, b):
                dve.wait_ge(s_turn[b], 4 + j + 1)
                dve.wait_ge(s_low, 4 + j * 2 + b)
                dve.tensor_tensor(h[:, :, :], p_t[b][:, :, :],
                                  gain[:, :].unsqueeze(2).broadcast_to([P, KD, P]), ALU.mult).then_inc(s_ht[b], 1)
            norm(0, 0)
            with dve.Fori(0, LAST) as j:
                norm(j, 1)
                scale(j, 0)
                norm(j + 1, 0)
                scale(j, 1)
            scale(LAST, 0)


def ffn_up(nc, K, w_up, conv_w, conv_b, conv_state, outs):
    PAST = DEC * 2
    with phase(nc, "up") as (c, stack):
        two = lambda name, shape, dt=F32: [c.sb(f"{name}{b}", shape, dt) for b in range(2)]
        w = two("w", [P, KD, P])
        wh, wl = two("wh", [P, KD, P], F32R), two("wl", [P, KD, P], F32R)
        pre = [c.sb(f"pre{s}", [P, 2 + SEQ]) for s in range(2)]
        new = c.sb("new", [P, 2, 2 + DEC])
        acc = [c.sb(f"acc{s}", [P, TOK]) for s in range(2)]
        past = two("past", [P, 2, P])
        rows = c.sb("rows", [2 * (2 + DEC), FF])
        slab = c.sb("slab", [P, 4, P])
        taps = c.sb("taps", [P, 4, 2, NF])
        p_g = [c.ps(f"g{g}", [P, 512]) for g in range(4)]
        p_s = c.ps("s", [P, 2, DEC])
        p_past = c.ps("past", [P, 2, P])
        p_rows = c.ps("rows", [2 * (2 + DEC), P])
        p_taps = c.ps("taps", [P, 4, P])
        S = {n: c.sem(n) for n in ("slab zero tturn taps mm smm used free sfree new hist back rows conv step silu res state").split()}
        s_w, s_past, s_st = c.sems("w"), c.sems("past"), c.sem("st")
        s_wh, s_wl = c.sems("wh"), c.sems("wl")
        wv = w_up.rearrange("(k p) n -> p k n", p=P)
        block = open_block(nc, stack, c)

        @block.sync
        def _(sp):
            credit(sp, c)
            sp.wait_ge(S["zero"], 4 + 4)
            for i in range(3):
                sp.dma_start(slab[0:2 * NF, i, :], conv_w[i, :].rearrange("(m p) -> m p", p=P)).then_inc(S["slab"], 16)
            sp.dma_start(slab[0:2 * NF, 3, :], conv_b.rearrange("(m p) -> m p", p=P)).then_inc(S["slab"], 16)
            with sp.Fori(0, NF // 2) as j:
                for b in range(2):
                    for s in range(2):
                        cols = ds(j * 256 + b * P + s * FF, P)
                        sp.wait_ge(s_wl[s], 4 + j * 2 + b)
                        sp.dma_start(w[s][:, :, :], wv[:, :, cols]).then_inc(s_w[s], 16)
                        if s == 0:
                            sp.wait_ge(S["hist"], 4 + (j * 2 + b) - 1)
                        sp.dma_start(past[b][0:PAST, s, :], conv_state[:, cols]).then_inc(s_past[b], 16)
            sp.wait_ge(S["rows"], 4 + NF)
            for s in range(2):
                o, cols = s * (2 + DEC), slice(s * FF, (s + 1) * FF)
                sp.dma_start(outs["p_fconv"][:, cols], rows[o:o + 2, :]).then_inc(S["state"], 16)
                sp.dma_start(outs["s_fconv"][:, 1, cols], rows[o + 2:o + 2 + DEC, :]).then_inc(S["state"], 16)
            sp.dma_start(outs["s_fconv"][:, 0, :], conv_state.rearrange("(b j) n -> b j n", j=2)[:, 1, :])\
              .then_inc(S["state"], 16)
            sp.wait_ge(S["state"], 4 + 80)

        @block.tensor
        def _(pe):
            pe.wait_ge(S["slab"], 4 + 64)
            for i in range(4):
                last = pe.transpose(p_taps[:, i, :], slab[:, i, :], K.ident[:, :])
            last.then_inc(S["tturn"], 1)
            with pe.Fori(0, NF // 2) as j:
                for b in range(2):
                    n = j * 2 + b
                    for s in range(2):
                        pe.wait_ge(s_wl[s], 4 + n + 1)
                        parts = ((wh, K.ht), (wh, K.hl), (wl, K.ht))
                        for g in range(GROUPS):
                            pe.wait_ge(S["free"], 4 + n * 8 + s * 4 + g - 3)
                            for k in range(KD):
                                for m, (wp, hp) in enumerate(parts):
                                    last = pe.matmul(p_g[g][:, :], wp[s][:, k, :], hp[:, k, g * 512:(g + 1) * 512],
                                                     start=(k == 0 and m == 0), stop=(k == KD - 1 and m == 2))
                            last.then_inc(S["mm"], 1)
                        pe.wait_ge(S["sfree"], 4 + n)
                        for k in range(KD):
                            for m, (wp, hp) in enumerate(parts):
                                last = pe.matmul(p_s[:, s, :], wp[s][:, k, :], hp[:, k, SEQ:TOK],
                                                 start=(k == 0 and m == 0), stop=(k == KD - 1 and m == 2))
                        last.then_inc(S["used"], 1)
                    pe.wait_ge(s_past[b], 4 + j * 32 + 32)
                    pe.wait_ge(S["conv"], 4 + n)
                    for s in range(2):
                        last = pe.transpose(p_past[:, s, :], past[b][:, s, :], K.ident[:, :])
                    last.then_inc(S["hist"], 1)
                    pe.wait_ge(S["new"], 4 + n + 1)
                    pe.wait_ge(S["rows"], 4 + n)
                    pe.transpose(p_rows[:, :], new[:, :, :].rearrange("p s r -> p (s r)"), K.ident[:, :]).then_inc(S["back"], 1)

        @block.scalar
        def _(act):
            act.wait_ge(S["zero"], 4 + 4)

            def split(n, s):
                act.wait_ge(s_w[s], 4 + n * 16 + 16)
                act.wait_ge(S["used"], 4 + n * 2 + s - 1)
                act.activation(wh[s][:, :, :], w[s][:, :, :], ACT.Copy).then_inc(s_wh[s], 1)

            def copies(n, last):
                act.wait_ge(S["conv"], 4 + n)
                for s in range(2):
                    for g in range(GROUPS):
                        act.wait_ge(S["mm"], 4 + n * 8 + s * 4 + g + 1)
                        act.activation(pre[s][:, 2 + g * 512:2 + (g + 1) * 512], p_g[g][:, :], ACT.Copy).then_inc(S["free"], 1)
                    if not last:
                        split(n + 1, s)
                act.wait_ge(S["used"], 4 + n * 2 + 2)
                act.wait_ge(S["back"], 4 + n)
                act.activation(new[:, :, 2:], p_s[:, :, :], ACT.Copy).then_inc(S["sfree"], 1)
                act.wait_ge(S["free"], 4 + n * 8 + 8)
                act.activation(new[:, 0, 0:2], pre[0][:, SEQ:], ACT.Copy)
                act.activation(new[:, 1, 0:2], pre[1][:, SEQ:], ACT.Copy).then_inc(S["new"], 1)

            def finish(n):
                act.wait_ge(S["conv"], 4 + n + 1)
                act.activation(acc[0][:, :], acc[0][:, :], ACT.Silu).then_inc(S["silu"], 1)
                act.wait_ge(S["back"], 4 + n + 1)
                act.activation(rows[:, ds(n * P, P)], p_rows[:, :], ACT.Copy).then_inc(S["rows"], 1)
                act.wait_ge(S["res"], 4 + n + 1)
                act.dma_start(K.d_act[ds(n, 1), :, :].rearrange("o p n -> (o p) n"), acc[1][:, :]).then_inc(s_st, 16)
            split(0, 0)
            split(0, 1)
            with act.Fori(0, NF - 1) as n:
                copies(n, False)
                finish(n)
            copies(NF - 1, True)
            finish(NF - 1)
            act.wait_ge(s_st, 4 + NF * 16)

        @block.gpsimd
        def _(pool):
            with pool.Fori(0, NF) as n:
                for s in range(2):
                    pool.wait_ge(s_wh[s], 4 + n + 1)
                    pool.tensor_tensor(wl[s][:, :, :], w[s][:, :, :], wh[s][:, :, :].bitcast(F32), ALU.subtract).then_inc(s_wl[s], 1)

        @block.vector
        def _(dve):
            for s in range(2):
                dve.memset(pre[s][:, 0:2], 0.0)
            dve.memset(slab[:, :, :], 0.0).then_inc(S["zero"], 2)
            for b in range(2):
                dve.memset(past[b][:, :, :], 0.0).then_inc(S["zero"], 1)
            dve.wait_ge(S["tturn"], 4 + 1)
            dve.tensor_copy(taps[:, :, :, :].rearrange("p i s m -> p i (s m)"), p_taps[:, :, 0:2 * NF]).then_inc(S["taps"], 1)
            dve.wait_ge(S["taps"], 4 + 1)
            step = Steps(dve, S["step"])
            with dve.Fori(0, NF // 2) as j:
                step.enter(j, 4, NF // 2)
                for b in range(2):
                    n = j * 2 + b
                    tap = [[taps[:, i, s, ds(n, 1)] for i in range(4)] for s in range(2)]
                    a = [acc[s][:, 0:SEQ] for s in range(2)]
                    t = [acc[s][:, SEQ:] for s in range(2)]
                    dve.wait_ge(S["new"], 4 + n + 1)
                    dve.wait_ge(S["hist"], 4 + n + 1)
                    dve.wait_ge(S["res"], 4 + n)
                    dve.wait_ge(s_st, 4 + n * 16)
                    for s in range(2):
                        dve.tensor_scalar(a[s], pre[s][:, 0:SEQ], tap[s][0], tap[s][3], ALU.mult, ALU.add)
                        last = dve.tensor_scalar(t[s], p_past[:, s, 0:PAST:2], tap[s][0], tap[s][3], ALU.mult, ALU.add)
                    step.link(last)
                    for s in range(2):
                        dve.scalar_tensor_tensor(out=a[s], in0=pre[s][:, 1:SEQ + 1], scalar=tap[s][1], in1=a[s],
                                                 op0=ALU.mult, op1=ALU.add)
                        last = dve.scalar_tensor_tensor(out=t[s], in0=p_past[:, s, 1:PAST:2], scalar=tap[s][1], in1=t[s],
                                                        op0=ALU.mult, op1=ALU.add)
                    step.link(last)
                    for s in range(2):
                        dve.scalar_tensor_tensor(out=a[s], in0=pre[s][:, 2:], scalar=tap[s][2], in1=a[s],
                                                 op0=ALU.mult, op1=ALU.add)
                        last = dve.scalar_tensor_tensor(out=t[s], in0=new[:, s, 2:], scalar=tap[s][2], in1=t[s],
                                                        op0=ALU.mult, op1=ALU.add)
                    last.then_inc(S["conv"], 1)
                    dve.wait_ge(S["silu"], 4 + n + 1)
                    dve.tensor_tensor(acc[1][:, :], acc[0][:, :], acc[1][:, :], ALU.mult).then_inc(S["res"], 1)
                step.leave()


def ffn_down(nc, K, w_down, outs):
    with phase(nc, "down") as (c, stack):
        two = lambda name, shape, dt=F32: [c.sb(f"{name}{b}", shape, dt) for b in range(2)]
        H = D // 2
        w = two("w", [P, 2, H])
        wh, wl = c.sb("wh", [P, NF, H], F32R), c.sb("wl", [P, NF, H], F32R)
        a, ah, al = two("a", [P, NF, P]), two("ah", [P, NF, P], F32R), two("al", [P, NF, P], F32R)
        x = two("x", [P, H])
        p_y = [c.ps(f"y{b}", [P, H]) for b in range(2)]
        s_w = c.sems("w")
        s_wh, s_wl = c.sem("wh"), c.sem("wl")
        s_a, s_ah, s_al, s_x, s_mm, s_y, s_st = (c.sems(n) for n in "a ah al x mm y st".split())
        block = open_block(nc, stack, c)
        LAST = NT // 2
        CH = NF // 2
        done = lambda o, j, b: j + o * (LAST + 1 - b)

        def rows_of(j, b, n):
            return ds(j * 256 + b * P, P) if n == P else slice(SEQ, TOK)

        @block.sync
        def _(sp):
            credit(sp, c)
            for o in range(2):
                cols = slice(o * H, (o + 1) * H)

                def load(j, b, n=P):
                    t = done(o, j, b)
                    sp.wait_ge(s_al[b], 4 + t)
                    sp.dma_start(a[b][:, :, 0:n], K.d_act[:, :, rows_of(j, b, n)].rearrange("f p n -> p f n")).then_inc(s_a[b], 16)
                    sp.wait_ge(s_st[b], 4 + t * 16)
                    sp.dma_start(x[b][0:n, :], K.d_x2[rows_of(j, b, n), cols]).then_inc(s_x[b], 16)

                def store(j, b, n=P):
                    sp.wait_ge(s_y[b], 4 + done(o, j, b) + 1)
                    dst = outs["y_prompt"][ds(j * 256 + b * P, P), cols] if n == P else outs["y_sample"][:, cols]
                    sp.dma_start(dst, x[b][0:n, :]).then_inc(s_st[b], 16)
                load(0, 0)
                load(0, 1)
                with sp.Fori(0, LAST - 1) as j:
                    for b in range(2):
                        store(j, b)
                        load(j + 1, b)
                store(LAST - 1, 0)
                load(LAST, 0, DEC)
                store(LAST - 1, 1)
                store(LAST, 0, DEC)
            sp.wait_ge(s_st[0], 4 + 2 * (LAST + 1) * 16)
            sp.wait_ge(s_st[1], 4 + 2 * LAST * 16)

        @block.scalar
        def _(act):
            rows = w_down.rearrange("(f p) n -> p f n", p=P)

            def fetch(o, k):
                n = o * CH + k
                act.wait_ge(s_wl, 4 + n - 1)
                act.dma_start(w[n % 2][:, :, :], rows[:, 2 * k:2 * k + 2, o * H:(o + 1) * H]).then_inc(s_w[n % 2], 16)

            def high(o, j, b):
                t = done(o, j, b)
                act.wait_ge(s_a[b], 4 + t * 16 + 16)
                act.wait_ge(s_mm[b], 4 + t)
                act.activation(ah[b][:, :, :], a[b][:, :, :], ACT.Copy).then_inc(s_ah[b], 1)
            for o in range(2):
                fetch(o, 0)
                fetch(o, 1)
                high(o, 0, 0)
                if o:
                    act.wait_ge(s_mm[0], 4 + LAST + 1)
                for k in range(CH):
                    n = o * CH + k
                    act.wait_ge(s_w[n % 2], 4 + n // 2 * 16 + 16)
                    act.activation(wh[:, 2 * k:2 * k + 2, :], w[n % 2][:, :, :], ACT.Copy).then_inc(s_wh, 1)
                    if k + 2 < CH:
                        fetch(o, k + 2)
                with act.Fori(0, LAST) as j:
                    high(o, j, 1)
                    high(o, j + 1, 0)

        @block.gpsimd
        def _(pool):
            def low(o, j, b):
                pool.wait_ge(s_ah[b], 4 + done(o, j, b) + 1)
                pool.tensor_tensor(al[b][:, :, :], a[b][:, :, :], ah[b][:, :, :].bitcast(F32), ALU.subtract).then_inc(s_al[b], 1)
            for o in range(2):
                low(o, 0, 0)
                with pool.Fori(0, LAST) as j:
                    low(o, j, 1)
                    low(o, j + 1, 0)

        @block.tensor
        def _(pe):
            def multiply(o, j, b, m=P, first=False):
                t = done(o, j, b)
                pe.wait_ge(s_al[b], 4 + t + 1)
                pe.wait_ge(s_y[b], 4 + t)
                for f in range(NF):
                    if first and f % 2 == 0:
                        pe.wait_ge(s_wl, 4 + o * CH + f // 2 + 1)
                    for i, (ap, wp) in enumerate(((ah, wh), (ah, wl), (al, wh))):
                        last = pe.matmul(p_y[b][0:m, :], ap[b][:, f, 0:m], wp[:, f, :],
                                         start=(f == 0 and i == 0), stop=(f == NF - 1 and i == 2))
                last.then_inc(s_mm[b], 1)
            for o in range(2):
                multiply(o, 0, 0, first=True)
                with pe.Fori(0, LAST) as j:
                    multiply(o, j, 1)
                    multiply(o, j + 1, 0)

        @block.vector
        def _(dve):
            def add(o, j, b):
                t = done(o, j, b)
                dve.wait_ge(s_x[b], 4 + t * 16 + 16)
                dve.wait_ge(s_mm[b], 4 + t + 1)
                dve.tensor_tensor(x[b][:, :], p_y[b][:, :], x[b][:, :], ALU.add).then_inc(s_y[b], 1)
            for o in range(2):
                for k in range(CH):
                    n = o * CH + k
                    dve.wait_ge(s_wh, 4 + n + 1)
                    dve.tensor_tensor(wl[:, 2 * k:2 * k + 2, :], w[n % 2][:, :, :], wh[:, 2 * k:2 * k + 2, :].bitcast(F32),
                                      ALU.subtract).then_inc(s_wl, 1)
                with dve.Fori(0, LAST) as j:
                    add(o, j, 0)
                    add(o, j, 1)
                add(o, LAST, 0)


def build(nc, ins, outs):
    K = Held()

    def scratch(name, shape):
        return nc.dram_tensor(f"scratch_{name}", shape, F32, kind="Internal").ap()
    K.d_qkv = scratch("qkv", (CONVW, P, TOK))
    K.d_z = scratch("z", (GH, P, TOK))
    K.d_q = scratch("q", (QH, P, TOK))
    K.d_iq = scratch("iq", (IH // 2, P, TOK))
    K.d_mix = scratch("mix", (KD, P, TOK))
    K.d_x2 = scratch("x2", (TOK, D))
    K.d_act = scratch("act", (NF, P, TOK))
    with ExitStack() as held:
        def keep(name, shape, dt=F32, stack=held):
            return stack.enter_context(nc.sbuf_tensor(name, shape, dt))
        K.ident, K.ones = keep("ident", [P, P]), keep("ones", [P, P])
        with ExitStack() as mixer:
            K.upto, K.before, K.after = (keep(name, [P, P], F32, mixer) for name in ("upto", "before", "after"))
            K.below = keep("below", [P, 896], F32, mixer)
            K.rb = keep("rb", [P, BUCKETS, QH], F32, mixer)
            K.near = keep("near", [P, QH, 256], F32, mixer)
            constants(nc, K, ins["rel_bias"])
            K.knew = keep("knew", [P, KVH * HD], F32, mixer)
            K.v = keep("v", [P, TILES, KVH * HD], F32, mixer)
            K.small = keep("small", [P, TILES, SMALL], F32, mixer)
            K.kt = keep("kt", [P, KVH, COLS], F32, mixer)
            K.ikt = keep("ikt", [P, COLS], F32, mixer)
            with ExitStack() as hidden:
                K.ht = keep("ht", [P, KD, COLS], F32, hidden)
                K.k = keep("k", [P, TILES, KVH * HD], F32, hidden)
                w_in = ins["w_in"].rearrange("l k n -> (l k) n")
                project(nc, K, ins["x_prompt"].rearrange("b t d -> (b t) d"), ins["x_sample"].rearrange("b t d -> (b t) d"),
                        ins["norm_mix"].rearrange("l d -> (l d)"), w_in)
                keys(nc, K, ins["k_norm"].rearrange("l d -> (l d)"), outs)
                channels(nc, K, w_in, ins["gdn_conv_w"].rearrange("l j n -> (l j) n"),
                         ins["state_gdn_conv"].rearrange("l b j n -> (l b j) n"), None, outs)
            with ExitStack() as rule:
                per_token = lambda name: keep(name, [P, TILES, GH], F32, rule)
                K.g, K.beta, K.decay_sum = per_token("g"), per_token("beta"), per_token("gc")
                K.kdec, K.bexp, K.glast = per_token("kdec"), per_token("bexp"), per_token("glast")
                K.join, K.join_t = keep("join", [P, LEVELS, P], F32, rule), keep("join_t", [P, LEVELS, P], F32, rule)
                K.state = keep("state", [P, GH, HD], F32, rule)
                gates(nc, K, ins["gdn_a_log"], ins["gdn_dt_bias"])
                delta(nc, K, ins["gdn_out_norm"].rearrange("l d -> (l d)"), outs)
                delta_step(nc, K, ins["state_gdn"].rearrange("l b h k v -> (l b) h k v"),
                           ins["gdn_out_norm"].rearrange("l d -> (l d)"), dict(outs, s_gdn=outs["s_gdn"].rearrange("(b h) k v -> b h k v", h=GH)))
            with ExitStack() as step:
                K.taken, K.new_taken = keep("taken", [P, PAIRS, PAGE], F32, step), keep("new_taken", [P, PAIRS], F32, step)
                K.half, K.halves = keep("half", [P, 2], F32, step), keep("halves", [P, P], F32, step)
                K.page_before = keep("page_before", [P, P], F32, step)
                step_select(nc, K, ins["cache_idx_k"].rearrange("l n p d -> (l n) p d"), ins["page_table"])
                K.row, K.dist = keep("row", [P, QUARTERS, PAIRS], I32, step), keep("dist", [P, QUARTERS, PAIRS], F32, step)
                K.empty = keep("empty", [P, QUARTERS, PAIRS], F32, step)
                step_slots(nc, K, ins["page_table"])
                step_attend(nc, K, ins["cache_k"], ins["cache_v"], ins["q_norm"].rearrange("l d -> (l d)"))
            attend(nc, K, ins["q_norm"].rearrange("l d -> (l d)"), outs)
        with ExitStack() as hidden:
            K.ht, K.hl = keep("ht_high", [P, KD, TOK], F32R, hidden), keep("ht_low", [P, KD, TOK], F32R, hidden)
            mix(nc, K, ins["x_prompt"].rearrange("b t d -> (b t) d"), ins["x_sample"].rearrange("b t d -> (b t) d"),
                ins["w_out"].rearrange("l k n -> (l k) n"), ins["norm_ffn"].rearrange("l d -> (l d)"))
            ffn_up(nc, K, ins["w_up"].rearrange("l k n -> (l k) n"), ins["ffn_conv_w"].rearrange("l j n -> (l j) n"),
                   ins["ffn_conv_b"].rearrange("l n -> (l n)"), ins["state_ffn_conv"].rearrange("l b j n -> (l b j) n"), outs)
        ffn_down(nc, K, ins["w_down"].rearrange("l f n -> (l f) n"), outs)


class Held:
    pass


_OUTS = [("y_prompt", (1, SEQ, D)), ("y_sample", (DEC, 1, D)),
         ("p_k", (1, 1, SEQ, KVH, HD)), ("p_v", (1, 1, SEQ, KVH, HD)), ("p_idx", (1, 1, SEQ, ID)),
         ("p_gdn", (1, 1, GH, HD, HD)), ("p_gconv", (1, 1, 3, CONV_CH)), ("p_fconv", (1, 1, 2, 2 * FF)),
         ("s_k", (1, DEC, 1, KVH, HD)), ("s_v", (1, DEC, 1, KVH, HD)), ("s_idx", (1, DEC, 1, ID)),
         ("s_gdn", (1, DEC, GH, HD, HD)), ("s_gconv", (1, DEC, 3, CONV_CH)), ("s_fconv", (1, DEC, 2, 2 * FF))]
_FLAT = {"y_prompt": "a t d -> (a t) d", "y_sample": "b t d -> (b t) d",
         "p_k": "l b t g d -> (l b t) (g d)", "p_v": "l b t g d -> (l b t) (g d)", "p_idx": "l b t d -> (l b t) d",
         "p_gdn": "l b h k v -> (l b h) k v", "p_gconv": "l b j n -> (l b j) n", "p_fconv": "l b j n -> (l b j) n",
         "s_k": "l b t g d -> (l b t) (g d)", "s_v": "l b t g d -> (l b t) (g d)", "s_idx": "l b t d -> (l b t) d",
         "s_gdn": "l b h k v -> (l b h) k v", "s_gconv": "l b j n -> (l b) j n", "s_fconv": "l b j n -> (l b) j n"}
_INS = ["x_prompt", "x_sample", "cache_k", "cache_v", "cache_idx_k", "state_gdn", "state_gdn_conv",
        "state_ffn_conv", "page_table", "rel_bias", "norm_mix", "w_in", "gdn_conv_w", "gdn_a_log", "gdn_dt_bias",
        "gdn_out_norm", "q_norm", "k_norm", "w_out", "norm_ffn", "w_up", "ffn_conv_w", "ffn_conv_b", "w_down"]


def kernel(**inputs):
    import concourse.bacc as bacc
    from concourse.bass_utils import run_bass_kernel_spmd

    nc = bacc.Bacc("TRN2", target_bir_lowering=False, num_devices=1)
    arrays, ins, outs = {}, {}, {}
    for name in _INS:
        a = np.ascontiguousarray(inputs[name])
        arrays[f"in_{name}"] = a
        ins[name] = nc.dram_tensor(f"in_{name}", a.shape, mybir.dt.from_np(a.dtype), kind="ExternalInput").ap()
    for name, shape in _OUTS:
        outs[name] = nc.dram_tensor(f"out_{name}", shape, F32, kind="ExternalOutput").ap().rearrange(_FLAT[name])
    build(nc, ins, outs)
    r = run_bass_kernel_spmd(nc, [arrays], core_ids=[0])
    return tuple(r.results[0][f"out_{name}"] for name, _ in _OUTS)
```
